# Optimizing a Trainium2 kernel written in Bass

```python
import jax, jax.numpy as jnp
from jax import lax
import numpy as np

D_MODEL = 1024
BATCH = 1
SEQ = 256
DEPTH = 2

CHUNK = 64
Q_BLOCK = 128
N_BRANCHES = 3
BRANCH_WIDTH = 512
SB_HEADS = 8
SB_HEAD_DIM = BRANCH_WIDTH // SB_HEADS
CONV_CHANNELS = BRANCH_WIDTH
CONV_WIDTH = 31
GLA_HEADS = 4
GLA_KEY_DIM = BRANCH_WIDTH // 2
GLA_VALUE_DIM = BRANCH_WIDTH
GLA_HEAD_K = GLA_KEY_DIM // GLA_HEADS
GLA_HEAD_V = GLA_VALUE_DIM // GLA_HEADS
GLA_GATE_RANK = 16
GLA_GATE_TAU = 16.0
D_FF = 2816
NORM_EPS = 1e-6

IN_WIDTHS = (
    BRANCH_WIDTH, BRANCH_WIDTH, BRANCH_WIDTH,
    2 * CONV_CHANNELS,
    GLA_KEY_DIM, GLA_KEY_DIM, GLA_VALUE_DIM,
    GLA_VALUE_DIM,
    GLA_GATE_RANK,
    N_BRANCHES * D_MODEL,
)
IN_WIDTH = sum(IN_WIDTHS)


def rms_norm(x, g):
    xf = x.astype(jnp.float32)
    y = xf * lax.rsqrt(jnp.mean(xf * xf, axis=-1, keepdims=True) + NORM_EPS)
    return (y * g.astype(jnp.float32)).astype(x.dtype)

def swiglu_ffn(h, w_gate, w_up, w_down):
    return (jax.nn.silu(h @ w_gate) * (h @ w_up)) @ w_down

def stick_breaking_attention(q, k, v):
    b, nh, s, dh = q.shape
    nb = s // Q_BLOCK
    q_blocks = q.reshape(b, nh, nb, Q_BLOCK, dh).transpose(2, 0, 1, 3, 4)
    key_pos = jnp.arange(s)
    scale = dh ** -0.5

    def one_block(args):
        q_blk, blk = args
        z = jnp.einsum('bhqd,bhkd->bhqk', q_blk, k).astype(jnp.float32) * scale
        query_pos = blk * Q_BLOCK + jnp.arange(Q_BLOCK)
        earlier = key_pos[None, :] < query_pos[:, None]
        log_keep = jnp.where(earlier, jax.nn.log_sigmoid(-z), 0.0)
        log_stick = lax.cumsum(log_keep, axis=3, reverse=True) - log_keep
        w = jnp.where(earlier, jnp.exp(jax.nn.log_sigmoid(z) + log_stick), 0.0)
        return jnp.einsum('bhqk,bhkd->bhqd', w.astype(v.dtype), v)

    out = lax.map(one_block, (q_blocks, jnp.arange(nb)))
    return out.transpose(1, 2, 0, 3, 4).reshape(b, nh, s, dh)

def conformer_conv(u_glu, conv_w, conv_b, ln_g, ln_b):
    a, g = jnp.split(u_glu, 2, axis=-1)
    u = a * jax.nn.sigmoid(g)
    y = lax.conv_general_dilated(
        u, conv_w[:, None, :], window_strides=(1,),
        padding=[(CONV_WIDTH - 1, 0)],
        dimension_numbers=('NWC', 'WIO', 'NWC'),
        feature_group_count=CONV_CHANNELS) + conv_b
    yf = y.astype(jnp.float32)
    mu = jnp.mean(yf, axis=-1, keepdims=True)
    var = jnp.mean(jnp.square(yf - mu), axis=-1, keepdims=True)
    yn = (yf - mu) * lax.rsqrt(var + NORM_EPS) * ln_g.astype(jnp.float32) + ln_b.astype(jnp.float32)
    return jax.nn.silu(yn).astype(u.dtype)

def gla_chunked(q, k, v, log_alpha):
    b, s, nh, dk = q.shape
    dv = v.shape[-1]
    n = s // CHUNK

    def to_chunks(t):
        return t.reshape(b, n, CHUNK, nh, t.shape[-1]).transpose(1, 0, 2, 3, 4)

    la_c = to_chunks(log_alpha.astype(jnp.float32))
    decay_to_end = lax.cumsum(la_c, axis=2, reverse=True) - la_c
    chunk_decay = jnp.exp(jnp.sum(la_c, axis=2))
    k_dec = to_chunks(k).astype(jnp.float32) * jnp.exp(decay_to_end)
    q_c = to_chunks(q).astype(jnp.float32) * (dk ** -0.5)
    v_c = to_chunks(v).astype(jnp.float32)

    def step(state, xs):
        q_n, k_n, v_n, lam = xs
        state = lam[..., None] * state + jnp.einsum('bchk,bchv->bhkv', k_n, v_n)
        return state, jnp.einsum('bchk,bhkv->bchv', q_n, state)

    state0 = jnp.zeros((b, nh, dk, dv), jnp.float32)
    _, o = lax.scan(step, state0, (q_c, k_dec, v_c, chunk_decay))
    return o.transpose(1, 0, 2, 3, 4).reshape(b, s, nh, dv).astype(v.dtype)

def hybrid_mixer(h, w_in, conv_w, conv_b, conv_ln_g, conv_ln_b,
                 gla_w_alpha, gla_b_alpha, gla_norm_g, w_branch, w_out):
    b, s, _ = h.shape
    proj = h @ w_in
    offsets = [int(o) for o in np.cumsum(IN_WIDTHS)[:-1]]
    (sb_q, sb_k, sb_v, conv_in, gla_q, gla_k, gla_v, gla_r, gla_lr,
     gate_logits) = jnp.split(proj, offsets, axis=-1)

    def heads(t, nh):
        return t.reshape(b, s, nh, -1)

    sb_out = stick_breaking_attention(
        heads(sb_q, SB_HEADS).transpose(0, 2, 1, 3),
        heads(sb_k, SB_HEADS).transpose(0, 2, 1, 3),
        heads(sb_v, SB_HEADS).transpose(0, 2, 1, 3))
    sb_out = sb_out.transpose(0, 2, 1, 3).reshape(b, s, BRANCH_WIDTH)

    conv_out = conformer_conv(conv_in, conv_w, conv_b, conv_ln_g, conv_ln_b)

    log_alpha = jax.nn.log_sigmoid((gla_lr @ gla_w_alpha + gla_b_alpha).astype(jnp.float32)) / GLA_GATE_TAU
    gla_o = gla_chunked(heads(gla_q, GLA_HEADS), heads(gla_k, GLA_HEADS),
                        heads(gla_v, GLA_HEADS), heads(log_alpha, GLA_HEADS))
    gla_o = rms_norm(gla_o, gla_norm_g.reshape(GLA_HEADS, GLA_HEAD_V))
    gla_out = gla_o.reshape(b, s, GLA_VALUE_DIM) * jax.nn.silu(gla_r)

    branches = jnp.stack([sb_out, conv_out, gla_out], axis=2)
    branch_d = jnp.einsum('bsgw,gwd->bsgd', branches, w_branch)
    gates = jax.nn.sigmoid(gate_logits.reshape(b, s, N_BRANCHES, D_MODEL))
    merged = jnp.sum(gates * branch_d, axis=2)
    return merged @ w_out

def first_inputs(seed: int = 0) -> dict:
    key = jax.random.key(seed)
    ks = jax.random.split(key, 20)

    def nrm(k, shape, scale):
        return jax.random.normal(k, shape, jnp.float32) * scale

    L, D = DEPTH, D_MODEL
    return {
        "x": nrm(ks[0], (BATCH, SEQ, D), 1.0),
        "norm_pre": 1.0 + nrm(ks[1], (L, 3, D), 0.05),
        "norm_post": 1.0 + nrm(ks[2], (L, 3, D), 0.05),
        "ffn1_w_gate": nrm(ks[3], (L, D, D_FF), D ** -0.5),
        "ffn1_w_up": nrm(ks[4], (L, D, D_FF), D ** -0.5),
        "ffn1_w_down": nrm(ks[5], (L, D_FF, D), D_FF ** -0.5),
        "ffn2_w_gate": nrm(ks[6], (L, D, D_FF), D ** -0.5),
        "ffn2_w_up": nrm(ks[7], (L, D, D_FF), D ** -0.5),
        "ffn2_w_down": nrm(ks[8], (L, D_FF, D), D_FF ** -0.5),
        "w_in": nrm(ks[9], (L, D, IN_WIDTH), D ** -0.5),
        "conv_w": nrm(ks[10], (L, CONV_WIDTH, CONV_CHANNELS), CONV_WIDTH ** -0.5),
        "conv_b": nrm(ks[11], (L, CONV_CHANNELS), 0.02),
        "conv_ln_g": 1.0 + nrm(ks[12], (L, CONV_CHANNELS), 0.05),
        "conv_ln_b": nrm(ks[13], (L, CONV_CHANNELS), 0.02),
        "gla_w_alpha": nrm(ks[14], (L, GLA_GATE_RANK, GLA_KEY_DIM), GLA_GATE_RANK ** -0.5),
        "gla_b_alpha": nrm(ks[15], (L, GLA_KEY_DIM), 0.02),
        "gla_norm_g": 1.0 + nrm(ks[16], (L, GLA_VALUE_DIM), 0.05),
        "w_branch": nrm(ks[17], (L, N_BRANCHES, BRANCH_WIDTH, D), BRANCH_WIDTH ** -0.5),
        "w_out": nrm(ks[18], (L, D, D), D ** -0.5),
    }

def first_block(x, norm_pre, norm_post, ffn1_w_gate, ffn1_w_up, ffn1_w_down,
              ffn2_w_gate, ffn2_w_up, ffn2_w_down, w_in, conv_w, conv_b,
              conv_ln_g, conv_ln_b, gla_w_alpha, gla_b_alpha, gla_norm_g,
              w_branch, w_out):
    for l in range(DEPTH):
        h = rms_norm(x, norm_pre[l, 0])
        x = x + 0.5 * rms_norm(swiglu_ffn(h, ffn1_w_gate[l], ffn1_w_up[l], ffn1_w_down[l]), norm_post[l, 0])
        h = rms_norm(x, norm_pre[l, 1])
        m = hybrid_mixer(h, w_in[l], conv_w[l], conv_b[l], conv_ln_g[l], conv_ln_b[l],
                         gla_w_alpha[l], gla_b_alpha[l], gla_norm_g[l], w_branch[l], w_out[l])
        x = x + rms_norm(m, norm_post[l, 1])
        h = rms_norm(x, norm_pre[l, 2])
        x = x + 0.5 * rms_norm(swiglu_ffn(h, ffn2_w_gate[l], ffn2_w_up[l], ffn2_w_down[l]), norm_post[l, 2])
    return x


MEM_LEN = 256
HEAD_DIM = 64
LRU_WIDTH = 256
LRU_BLOCKS = 4
LRU_BLOCK = LRU_WIDTH // LRU_BLOCKS
CONV_WIDTH_2 = 4
LRU_C = 8.0
FOX_HEADS = 8
FOX_WIDTH = FOX_HEADS * HEAD_DIM
RET_HEADS = 4
RET_WIDTH = RET_HEADS * HEAD_DIM
MIX_WIDTH = LRU_WIDTH + FOX_WIDTH + RET_WIDTH
SPLIT_SIZES = (LRU_WIDTH, LRU_WIDTH, FOX_WIDTH, FOX_WIDTH, FOX_WIDTH, FOX_HEADS, RET_WIDTH, RET_WIDTH, RET_WIDTH, RET_WIDTH)
IN_WIDTH_2 = sum(SPLIT_SIZES)
CROSS_HEADS = 4
CROSS_HEAD_DIM = D_MODEL // CROSS_HEADS
D_FF_2 = ((8 * D_MODEL + 3 * 256 - 1) // (3 * 256)) * 256
RET_CHUNK = 128
ROPE_THETA = 10000.0
EPS = 1e-6


def rms_norm_2(x, g):
    xf = x.astype(jnp.float32)
    y = xf * lax.rsqrt(jnp.mean(xf * xf, axis=-1, keepdims=True) + EPS)
    return (y * g.astype(jnp.float32)).astype(x.dtype)

def causal_depthwise_conv(x, w, b):
    c = x.shape[-1]
    xp = jnp.pad(x, ((0, 0), (CONV_WIDTH_2 - 1, 0), (0, 0)))
    out = lax.conv_general_dilated(xp, w.astype(x.dtype)[:, None, :], window_strides=(1,), padding='VALID', dimension_numbers=('NWC', 'WIO', 'NWC'), feature_group_count=c)
    return out + b.astype(x.dtype)

def rg_lru(x, w_r, b_r, w_i, b_i, lam):
    bsz, s, _ = x.shape
    xb = x.reshape(bsz, s, LRU_BLOCKS, LRU_BLOCK)
    r = jax.nn.sigmoid((jnp.einsum('bsni,nij->bsnj', xb, w_r).reshape(bsz, s, LRU_WIDTH) + b_r).astype(jnp.float32))
    i = jax.nn.sigmoid((jnp.einsum('bsni,nij->bsnj', xb, w_i).reshape(bsz, s, LRU_WIDTH) + b_i).astype(jnp.float32))
    log_a = -LRU_C * r * jax.nn.softplus(-lam.astype(jnp.float32))
    a = jnp.exp(log_a)
    u = jnp.sqrt(-jnp.expm1(2.0 * log_a)) * (i * x.astype(jnp.float32))

    def combine(left, right):
        a1, b1 = left
        a2, b2 = right
        return a1 * a2, a2 * b1 + b2

    _, h = lax.associative_scan(combine, (a, u), axis=1)
    return h.astype(x.dtype)

def forgetting_attention(q, k, v, f_logit, b_f):
    bsz, s, _ = q.shape
    q = q.reshape(bsz, s, FOX_HEADS, HEAD_DIM).transpose(0, 2, 1, 3)
    k = k.reshape(bsz, s, FOX_HEADS, HEAD_DIM).transpose(0, 2, 1, 3)
    v = v.reshape(bsz, s, FOX_HEADS, HEAD_DIM).transpose(0, 2, 1, 3)
    log_f = jax.nn.log_sigmoid((f_logit + b_f).astype(jnp.float32))
    c = jnp.cumsum(log_f, axis=1).transpose(0, 2, 1)
    key_pos = jnp.arange(s)
    scale = HEAD_DIM ** -0.5

    def block(bi):
        start = bi * Q_BLOCK
        qb = lax.dynamic_slice_in_dim(q, start, Q_BLOCK, axis=2)
        cb = lax.dynamic_slice_in_dim(c, start, Q_BLOCK, axis=2)
        logits = jnp.einsum('bhqd,bhkd->bhqk', qb, k).astype(jnp.float32) * scale + cb[..., None] - c[:, :, None, :]
        q_pos = start + jnp.arange(Q_BLOCK)
        mask = key_pos[None, :] <= q_pos[:, None]
        p = jax.nn.softmax(jnp.where(mask, logits, -jnp.inf), axis=-1)
        return jnp.einsum('bhqk,bhkd->bhqd', p.astype(v.dtype), v)

    out = lax.map(block, jnp.arange(s // Q_BLOCK))
    return out.transpose(1, 0, 3, 2, 4).reshape(bsz, s, FOX_WIDTH)

def rotary(x, positions):
    half = x.shape[-1] // 2
    inv_freq = ROPE_THETA ** (-jnp.arange(half, dtype=jnp.float32) / half)
    ang = positions.astype(jnp.float32)[..., None] * inv_freq
    cos = jnp.cos(ang)[:, :, None, :]
    sin = jnp.sin(ang)[:, :, None, :]
    xf = x.astype(jnp.float32)
    x1, x2 = xf[..., :half], xf[..., half:]
    return jnp.concatenate([x1 * cos - x2 * sin, x1 * sin + x2 * cos], axis=-1)

def retention(q, k, v, g, positions):
    bsz, s, _ = q.shape
    n_chunks = s // RET_CHUNK
    shp = (bsz, n_chunks, RET_CHUNK, RET_HEADS, HEAD_DIM)
    qc = rotary(q.reshape(bsz, s, RET_HEADS, HEAD_DIM), positions).reshape(shp)
    kc = (rotary(k.reshape(bsz, s, RET_HEADS, HEAD_DIM), positions) * HEAD_DIM ** -0.5).reshape(shp)
    vc = v.astype(jnp.float32).reshape(shp)
    log_gamma = jnp.log1p(-jnp.exp2(-5.0 - jnp.arange(RET_HEADS, dtype=jnp.float32)))
    idx = jnp.arange(RET_CHUNK, dtype=jnp.float32)
    diff = idx[:, None] - idx[None, :]
    decay = jnp.where(diff >= 0, jnp.exp(log_gamma[:, None, None] * jnp.maximum(diff, 0.0)), 0.0)
    scores = jnp.einsum('bnihd,bnjhd->bnhij', qc, kc) * decay[None, None]
    y_inner = jnp.einsum('bnhij,bnjhd->bnihd', scores, vc)
    k_w = jnp.exp(log_gamma[None, :] * (RET_CHUNK - 1.0 - idx)[:, None])
    u = jnp.einsum('bnjhd,bnjhe,jh->bnhde', kc, vc, k_w)
    chunk_decay = jnp.exp(log_gamma * RET_CHUNK)[None, :, None, None]

    def step(state, u_n):
        return chunk_decay * state + u_n, state

    init = jnp.zeros((bsz, RET_HEADS, HEAD_DIM, HEAD_DIM), jnp.float32)
    _, prev_states = lax.scan(step, init, u.transpose(1, 0, 2, 3, 4))
    q_w = jnp.exp(log_gamma[None, :] * (idx + 1.0)[:, None])
    y_cross = jnp.einsum('bnihd,nbhde,ih->bnihe', qc, prev_states, q_w)
    y = (y_inner + y_cross).reshape(bsz, s, RET_HEADS, HEAD_DIM)
    mu = jnp.mean(y, axis=-1, keepdims=True)
    var = jnp.mean(jnp.square(y - mu), axis=-1, keepdims=True)
    y = ((y - mu) * lax.rsqrt(var + EPS)).reshape(bsz, s, RET_WIDTH)
    return (jax.nn.silu(g.astype(jnp.float32)) * y).astype(g.dtype)

def parallel_mixer(h, positions, w_in, conv_w, conv_b, w_rg, b_rg, w_ig, b_ig, lru_lambda, fox_b_f, w_out):
    proj = h @ w_in
    lx, ly, fq, fk, fv, ff, rq, rk, rv, rg = jnp.split(proj, np.cumsum(SPLIT_SIZES)[:-1].tolist(), axis=-1)
    lru_out = rg_lru(causal_depthwise_conv(lx, conv_w, conv_b), w_rg, b_rg, w_ig, b_ig, lru_lambda) * jax.nn.gelu(ly)
    fox_out = forgetting_attention(fq, fk, fv, ff, fox_b_f)
    ret_out = retention(rq, rk, rv, rg, positions)
    return jnp.concatenate([lru_out, fox_out.astype(h.dtype), ret_out], axis=-1) @ w_out

def memory_cross_attention(h, mem_n, w_q, w_k, w_v, w_o):
    bsz, s, _ = h.shape
    m = mem_n.shape[1]
    q = (h @ w_q).reshape(bsz, s, CROSS_HEADS, CROSS_HEAD_DIM)
    k = (mem_n @ w_k).reshape(bsz, m, CROSS_HEADS, CROSS_HEAD_DIM)
    v = (mem_n @ w_v).reshape(bsz, m, CROSS_HEADS, CROSS_HEAD_DIM)
    logits = jnp.einsum('bshd,bmhd->bhsm', q, k).astype(jnp.float32) * CROSS_HEAD_DIM ** -0.5
    p = jax.nn.softmax(logits, axis=-1)
    o = jnp.einsum('bhsm,bmhd->bshd', p.astype(v.dtype), v).reshape(bsz, s, D_MODEL)
    return o @ w_o

def swiglu(h, w_gate, w_up, w_down):
    return (jax.nn.silu(h @ w_gate) * (h @ w_up)) @ w_down

def second_inputs(seed: int = 0) -> dict:
    key = jax.random.key(seed)
    ks = jax.random.split(key, 32)

    def nrm(k, shape, scale):
        return scale * jax.random.normal(k, shape, jnp.float32)

    def gain(k, shape):
        return 1.0 + 0.02 * jax.random.normal(k, shape, jnp.float32)

    u = jax.random.uniform(ks[12], (DEPTH, LRU_WIDTH), jnp.float32, 0.9, 0.999)
    a_base = u ** (1.0 / LRU_C)
    lru_lambda = jnp.log(a_base) - jnp.log1p(-a_base)
    return {
        'x': nrm(ks[0], (BATCH, SEQ, D_MODEL), 1.0),
        'mem': nrm(ks[1], (BATCH, MEM_LEN, D_MODEL), 1.0),
        'positions': jnp.tile(jnp.arange(SEQ, dtype=jnp.int32)[None, :], (BATCH, 1)),
        'pre_mix_g': gain(ks[2], (DEPTH, D_MODEL)),
        'post_mix_g': gain(ks[3], (DEPTH, D_MODEL)),
        'w_in': nrm(ks[4], (DEPTH, D_MODEL, IN_WIDTH_2), D_MODEL ** -0.5),
        'conv_w': nrm(ks[5], (DEPTH, CONV_WIDTH_2, LRU_WIDTH), CONV_WIDTH_2 ** -0.5),
        'conv_b': nrm(ks[6], (DEPTH, LRU_WIDTH), 0.01),
        'w_rg': nrm(ks[7], (DEPTH, LRU_BLOCKS, LRU_BLOCK, LRU_BLOCK), LRU_BLOCK ** -0.5),
        'b_rg': nrm(ks[8], (DEPTH, LRU_WIDTH), 0.01),
        'w_ig': nrm(ks[9], (DEPTH, LRU_BLOCKS, LRU_BLOCK, LRU_BLOCK), LRU_BLOCK ** -0.5),
        'b_ig': nrm(ks[10], (DEPTH, LRU_WIDTH), 0.01),
        'lru_lambda': lru_lambda,
        'fox_b_f': 2.0 + nrm(ks[11], (DEPTH, FOX_HEADS), 0.5),
        'w_out': nrm(ks[13], (DEPTH, MIX_WIDTH, D_MODEL), MIX_WIDTH ** -0.5),
        'pre_cross_g': gain(ks[14], (DEPTH, D_MODEL)),
        'post_cross_g': gain(ks[15], (DEPTH, D_MODEL)),
        'mem_norm_g': gain(ks[16], (D_MODEL,)),
        'w_cq': nrm(ks[17], (DEPTH, D_MODEL, D_MODEL), D_MODEL ** -0.5),
        'w_ck': nrm(ks[18], (DEPTH, D_MODEL, D_MODEL), D_MODEL ** -0.5),
        'w_cv': nrm(ks[19], (DEPTH, D_MODEL, D_MODEL), D_MODEL ** -0.5),
        'w_co': nrm(ks[20], (DEPTH, D_MODEL, D_MODEL), D_MODEL ** -0.5),
        'pre_ffn_g': gain(ks[21], (DEPTH, D_MODEL)),
        'post_ffn_g': gain(ks[22], (DEPTH, D_MODEL)),
        'w_gate': nrm(ks[23], (DEPTH, D_MODEL, D_FF_2), D_MODEL ** -0.5),
        'w_up': nrm(ks[24], (DEPTH, D_MODEL, D_FF_2), D_MODEL ** -0.5),
        'w_down': nrm(ks[25], (DEPTH, D_FF_2, D_MODEL), D_FF_2 ** -0.5),
    }

def second_block(x, mem, positions, pre_mix_g, post_mix_g, w_in, conv_w, conv_b, w_rg, b_rg, w_ig, b_ig, lru_lambda, fox_b_f, w_out, pre_cross_g, post_cross_g, mem_norm_g, w_cq, w_ck, w_cv, w_co, pre_ffn_g, post_ffn_g, w_gate, w_up, w_down):
    mem_n = rms_norm_2(mem, mem_norm_g)
    for l in range(DEPTH):
        h = rms_norm_2(x, pre_mix_g[l])
        mix = parallel_mixer(h, positions, w_in[l], conv_w[l], conv_b[l], w_rg[l], b_rg[l], w_ig[l], b_ig[l], lru_lambda[l], fox_b_f[l], w_out[l])
        x = x + rms_norm_2(mix, post_mix_g[l])
        h = rms_norm_2(x, pre_cross_g[l])
        x = x + rms_norm_2(memory_cross_attention(h, mem_n, w_cq[l], w_ck[l], w_cv[l], w_co[l]), post_cross_g[l])
        h = rms_norm_2(x, pre_ffn_g[l])
        x = x + rms_norm_2(swiglu(h, w_gate[l], w_up[l], w_down[l]), post_ffn_g[l])
    return x


def setup_inputs(seed=0):
    out = dict(first_inputs(seed))
    for name, value in second_inputs(seed + 1).items():
        if name != "x":
            out[name + "_2"] = value
    return out


def reference(
    x, norm_pre, norm_post, ffn1_w_gate, ffn1_w_up, ffn1_w_down, ffn2_w_gate, ffn2_w_up,
    ffn2_w_down, w_in, conv_w, conv_b, conv_ln_g, conv_ln_b, gla_w_alpha, gla_b_alpha,
    gla_norm_g, w_branch, w_out, mem_2, positions_2, pre_mix_g_2, post_mix_g_2, w_in_2,
    conv_w_2, conv_b_2, w_rg_2, b_rg_2, w_ig_2, b_ig_2, lru_lambda_2, fox_b_f_2, w_out_2,
    pre_cross_g_2, post_cross_g_2, mem_norm_g_2, w_cq_2, w_ck_2, w_cv_2, w_co_2, pre_ffn_g_2,
    post_ffn_g_2, w_gate_2, w_up_2, w_down_2,
):
    x = first_block(
        x, norm_pre, norm_post, ffn1_w_gate, ffn1_w_up, ffn1_w_down, ffn2_w_gate, ffn2_w_up,
        ffn2_w_down, w_in, conv_w, conv_b, conv_ln_g, conv_ln_b, gla_w_alpha, gla_b_alpha,
        gla_norm_g, w_branch, w_out,
    )
    return second_block(
        x, mem_2, positions_2, pre_mix_g_2, post_mix_g_2, w_in_2, conv_w_2, conv_b_2, w_rg_2,
        b_rg_2, w_ig_2, b_ig_2, lru_lambda_2, fox_b_f_2, w_out_2, pre_cross_g_2, post_cross_g_2,
        mem_norm_g_2, w_cq_2, w_ck_2, w_cv_2, w_co_2, pre_ffn_g_2, post_ffn_g_2, w_gate_2,
        w_up_2, w_down_2,
    )


_drawn_inputs = setup_inputs


def setup_inputs(seed=0):
    import zlib

    import numpy as np

    out = dict(_drawn_inputs(seed))
    spreads = {}
    factors = {'conv_ln_b': 2.773,
     'gla_b_alpha': 7.75,
     'post_mix_g_2': 4.241,
     'conv_b_2': 3.51,
     'b_rg_2': 8.0,
     'b_ig_2': 8.0,
     'pre_cross_g_2': 4.788,
     'post_cross_g_2': 4.456,
     'mem_norm_g_2': 2.884,
     'pre_ffn_g_2': 3.739,
     'post_ffn_g_2': 5.347}
    for name, (base, spread) in spreads.items():
        noise = np.random.default_rng([zlib.crc32(name.encode()), seed]).standard_normal(out[name].shape)
        drawn = base * np.exp(spread * noise) if base else spread * noise
        out[name] = __import__('jax').numpy.asarray(drawn.astype(out[name].dtype))
    for name, factor in factors.items():
        out[name] = (out[name] * factor).astype(out[name].dtype)
    return out
```

```python
from contextlib import ExitStack

import numpy as np

import concourse.bass as bass
from concourse import mybir

F32 = mybir.dt.float32
F32R = mybir.dt.float32r
I32 = mybir.dt.int32
ALU = mybir.AluOpType
ACT = mybir.ActivationFunctionType
AX = mybir.AxisListType

P = 128
DEPTH = 2
T = 256
TT = T // P
D = 1024
KD = D // P
F = 2816
FC = 256
NCHUNK = F // FC
RING = 3
AHEAD = 2
EPS = 1e-6
BW = 512
CW = 31
CPAD = CW - 1
GLA_CHUNK = 64
TAU = 16.0
CW2 = 4
PAD2 = CW2 - 1
LRU_C = 8.0
RANK = 16
NEG = -1e30

U_FFN = 3 * NCHUNK
U_MIX_A = 1 + 2 * 8 + 2 * 6 + 6 + 4
U_LAYER_A = 2 * U_FFN + U_MIX_A
U_MIX_B = 1 + 2 * 6 + 8 + 4 + 8
U_LAYER_B = U_MIX_B + U_FFN
assert U_MIX_A % RING == 0 and U_MIX_B % RING == 0 and U_FFN % RING == 0
UNITS = DEPTH * (U_LAYER_A + U_LAYER_B)

A_LR = 4096
A_CHUNKS = {"gla_qk": 2560, "gla_v": 3072, "gla_r": 3584, "conv_a": 1536, "conv_g": 2048,
            "sb_q": 0, "sb_k": 512, "sb_v": 1024}
A_GATES = 4112
A_SECTIONS = (2, 0, 1)
B_FF = 2048
B_CHUNKS = {"fox_q": 512, "fox_k": 1024, "lru_xy": 0, "fox_v": 1536, "ret_qk": 2056, "ret_vg": 2568}

CONST = {}


def _constants():
    i = np.arange(P)
    parts = {
        "ident": np.eye(P),
        "ones": np.ones((P, P)),
        "tri_ge": (i[:, None] >= i[None, :]) * 1.0,
        "tri_le": (i[:, None] <= i[None, :]) * 1.0,
        "sb_keep": (i[:, None] < i[None, :]) * 1.0,
        "sb_neg": np.where(i[:, None] < i[None, :], 0.0, NEG),
        "gla_suffix": ((i[:, None] > i[None, :]) & (i[:, None] // GLA_CHUNK == i[None, :] // GLA_CHUNK)) * 1.0,
        "gla_chunk": (i[:, None] // GLA_CHUNK == np.arange(2)[None, :]) * 1.0,
        "fox_neg": np.where(i[None, :] <= i[:, None], 0.0, NEG),
    }
    log_gamma = np.log1p(-np.exp2(-5.0 - np.arange(4)))
    diff = np.arange(T)[None, :] - i[:, None]
    decay = np.where(diff[:, None, :] >= 0, np.exp(log_gamma[None, :, None] * np.maximum(diff, 0)[:, None, :]), 0.0)
    parts["ret_decay"] = (decay * 64 ** -0.5).reshape(P, 4 * T)
    freq = (np.float32(10000.0) ** (-np.arange(32, dtype=np.float32) / np.float32(32))).astype(np.float32)
    parts["inv_freq"] = np.tile(freq, (P, 1))
    sel = np.zeros((P, 8, P))
    for h in range(8):
        sel[h, h, :] = -1.0
        sel[64 + h, h, :] = -1.0
    parts["fox_pick"] = sel.reshape(P, 8 * P)
    at = 0
    for name, a in parts.items():
        CONST[name] = (at, a.shape[1])
        at += a.shape[1]
    return np.concatenate([a.astype(np.float32) for a in parts.values()], axis=1)


CONST_ARRAY = _constants()

PACK_A = {"conv_w": (0, 4 * CW), "conv_b": (124, 4), "ln_g": (128, 4), "ln_b": (132, 4), "gla_g": (136, 4),
          "w_alpha": (140, 256)}
PACK_A_W = 396
PACK_B = {"conv_w": (0, 8), "conv_b": (8, 2), "b_r": (10, 2), "b_i": (12, 2), "lam": (14, 2), "fox_b": (16, 8),
          "w_r": (24, 256), "w_i": (280, 256)}
PACK_B_W = 536


class Signals:

    def __init__(self, make, counted):
        self.make, self.counted = make, counted
        self.sems, self.seen = {}, {}

    def _sem(self, stage):
        if stage not in self.sems:
            self.sems[stage] = self.make(stage)
        return self.sems[stage]

    def done(self, stage, step):
        steps = self.seen.setdefault(stage, [])
        assert step not in steps, (stage, step)
        steps.append(step)
        return self._sem(stage), 1

    def after(self, stage, step, layer):
        steps = self.counted.get(stage) if self.counted else None
        if steps is None:
            assert not self.counted, stage
            return self._sem(stage), layer + 1
        return self._sem(stage), layer * len(steps) + steps.index(step) + 1


def build(nc, d, out, counted):
    with ExitStack() as ctx:
        return _program(ctx, nc, d, out, counted)


def _program(ctx, nc, d, out, counted):
    def sb(name, shape, dt=F32):
        return ctx.enter_context(nc.sbuf_tensor(name, shape, dt))

    def sem(name):
        return ctx.enter_context(nc.semaphore(name))

    S = Signals(sem, counted)
    done, after = S.done, S.after

    ps = ctx.enter_context(nc.psum_tensor("ps", [P, 8, 512], F32))
    x = sb("x", [P, TT, D])
    raw = sb("raw", [P, RING, 2048])
    w_hi = sb("w_hi", [P, RING, 2048], F32R)
    w_lo = sb("w_lo", [P, RING, 2048], F32R)
    hT_hi = sb("hT_hi", [P, KD, T], F32R)
    hT_lo = sb("hT_lo", [P, KD, T], F32R)
    bT_hi = sb("bT_hi", [P, KD + 2, T], F32R)
    bT_lo = sb("bT_lo", [P, KD + 2, T], F32R)
    pre_g = sb("pre_g", [P, D])
    post_g = sb("post_g", [P, D])
    const = sb("const", [P, CONST_ARRAY.shape[1]])
    pack = sb("pack", [P, max(PACK_A_W, PACK_B_W)])
    stat = sb("stat", [P, 128])
    SCRATCH = 17200
    scratch = sb("scratch", [P, SCRATCH])

    def konst(name):
        at, w = CONST[name]
        return const[:, at:at + w]

    ident = konst("ident")

    def packed(table, name):
        at, w = table[name]
        return pack[:, at:at + w]

    stat_at = [0]

    def column(n):
        stat_at[0] += n
        return stat[:, stat_at[0] - n:stat_at[0]]

    ss_in, std_in, rstd_in = column(TT), column(TT), column(TT)
    ss_out, std_out, rstd_out = column(TT), column(TT), column(TT)

    class Carve:

        def __init__(self, at):
            self.at = at

        def __call__(self, n):
            self.at += n
            assert self.at <= SCRATCH, self.at
            return scratch[:, self.at - n:self.at]

    shared = Carve(0)
    wide = shared(2048)
    xn = wide.rearrange("p (t n) -> p t n", t=TT)
    pairbuf = shared(1024)
    sil = pairbuf[:, 0:512].rearrange("p (t n) -> p t n", t=TT)
    hid = pairbuf[:, 512:1024].rearrange("p (t n) -> p t n", t=TT)

    a_mem = Carve(shared.at)
    gqk_f, gv_f, gr_f, gqT_f = a_mem(1024), a_mem(1024), a_mem(1024), a_mem(512)
    gqk = gqk_f.rearrange("p (t n) -> p t n", t=TT)
    gv = gv_f.rearrange("p (t n) -> p t n", t=TT)
    gr = gr_f.rearrange("p (t n) -> p t n", t=TT)
    gqT = gqT_f.rearrange("p (c t) -> p c t", c=2)
    sbqT = gqk_f.rearrange("p (c t) -> p c t", c=4)
    sbkT = gv_f.rearrange("p (c t) -> p c t", c=4)
    sbv = gr
    uT = a_mem(4 * (T + CPAD)).rearrange("p (c t) -> p c t", c=4)
    conv_y_f = a_mem(1024)
    conv_y = conv_y_f.rearrange("p (c t) -> p c t", c=4)
    sb_sp = a_mem(768)
    sg = a_mem(2048).rearrange("p (h t n) -> p h t n", h=2, t=TT)
    merged_f = a_mem(2048)
    merged = merged_f.rearrange("p (t n) -> p t n", t=TT)
    lr_rows = a_mem(32).rearrange("p (t r) -> p t r", t=TT)
    lrT = a_mem(256)
    lam = a_mem(8).rearrange("p (c n) -> p c n", c=2)
    nla, gdec = pairbuf[:, 0:512], pairbuf[:, 512:1024]
    gstate = sg[:, 0, :, :].rearrange("p t n -> p (t n)").rearrange("p (c n v) -> p c n v", c=2, n=4)
    go_f, gsq_f = merged_f[:, 0:1024], merged_f[:, 1024:2048]
    conv_u = wide[:, 0:1024].rearrange("p (t n) -> p t n", t=TT)
    conv_s = wide[:, 1024:2048].rearrange("p (t n) -> p t n", t=TT)
    sb_q, sb_k = conv_u, conv_s
    sb_z, sb_e = wide[:, 0:768], wide[:, 768:1536]
    conv_n = pairbuf.rearrange("p (t n) -> p t n", t=TT)
    ssg, stdg, rstdg = column(8), column(8), column(8)
    cmu, css, cstd, crstd = column(TT), column(TT), column(TT), column(TT)

    b_mem = Carve(shared.at)
    fqk_f = b_mem(2048)
    fq = fqk_f[:, 0:1024].rearrange("p (t n) -> p t n", t=TT)
    fk = fqk_f[:, 1024:2048].rearrange("p (t n) -> p t n", t=TT)
    rqk = fq
    rope = fk
    ret_s = fqk_f.rearrange("p (h n) -> p h n", h=4)
    fqkT_f = b_mem(2048)
    fqT = fqkT_f[:, 0:1024].rearrange("p (c t) -> p c t", c=4)
    fkT = fqkT_f[:, 1024:2048].rearrange("p (c t) -> p c t", c=4)
    kmT = fqkT_f.rearrange("p (c m) -> p c m", c=KD)
    fvrT_f = b_mem(2048)
    fv_f, rT_f = fvrT_f[:, 0:1024], fvrT_f[:, 1024:2048]
    fv = fv_f.rearrange("p (t n) -> p t n", t=TT)
    rT = rT_f.rearrange("p (c t) -> p c t", c=4)
    rv_f, rg_f = b_mem(512), b_mem(512)
    rv = rv_f.rearrange("p (t n) -> p t n", t=TT)
    rg = rg_f.rearrange("p (t n) -> p t n", t=TT)
    fl_f = b_mem(1024)
    fl = fl_f.rearrange("p (h s) -> p h s", h=4)
    fpT_f = b_mem(1024)
    fpT = fpT_f.rearrange("p (b t) -> p b t", b=8)
    vm = b_mem(2048).rearrange("p (m n) -> p m n", m=TT)
    lxT = b_mem(2 * (T + PAD2)).rearrange("p (c t) -> p c t", c=2)
    lyT = b_mem(512)
    flog, fcum = b_mem(16).rearrange("p (t h) -> p t h", t=TT), b_mem(16).rearrange("p (t h) -> p t h", t=TT)
    ftmp = b_mem(16)
    fcT = b_mem(256)
    cos, sin = b_mem(64), b_mem(64)
    lru_c, lru_t, lsp = column(2), column(2), column(2)
    fmax, fden, frd = column(4), column(4), column(4)
    rstat, rstat2, rstat3 = column(8), column(8), column(8)
    lxy = pairbuf.rearrange("p (t n) -> p t n", t=TT)
    ry_f, rsq_f = pairbuf[:, 0:512], pairbuf[:, 512:1024]
    lru = [wide[:, 512 * n:512 * n + 512] for n in range(4)]
    km = xn
    cq = xn
    cqT = fqk_f.rearrange("p (c t) -> p c t", c=KD)
    cp = [fl_f.rearrange("p (h m) -> p h m", h=4), fpT_f.rearrange("p (h m) -> p h m", h=4)]
    cpT = fvrT_f.rearrange("p (b t) -> p b t", b=8)
    cmax, cden, crd = column(8), column(8), column(8)
    positions = ctx.enter_context(nc.sbuf_tensor("positions", [P, TT], I32))[:, :]

    raw_landed = [sem(f"raw_landed{i}") for i in range(RING)]
    high_ready, low_ready, unit_done = sem("high_ready"), sem("low_ready"), sem("unit_done")
    pre_loaded, post_loaded, pack_loaded = sem("pre_gain_loaded"), sem("post_gain_loaded"), sem("pack_loaded")
    start_loaded = sem("start_loaded")
    x_ready, sq_in, std_ready, rstd_ready = sem("x_ready"), sem("sq_in"), sem("std_ready"), sem("rstd_ready")
    h_ready, h_turned, hT_hi_ready, hT_ready = sem("h_ready"), sem("h_turned"), sem("hT_hi_ready"), sem("hT_ready")
    sq_out, std_out_ready, rstd_out_ready = sem("sq_out"), sem("std_out_ready"), sem("rstd_out_ready")
    scaled = sem("out_scaled")
    silu_ready, hid_ready, hid_turned = sem("silu_ready"), sem("hid_ready"), sem("hid_turned")
    gT_hi_ready, gT_ready = sem("gT_hi_ready"), sem("gT_ready")
    stored, memory_loaded = sem("stored"), sem("memory_loaded")
    raw_free, gla_free = sem("raw_free"), sem("gla_free")

    CREDIT = RING

    class Layer:

        def __init__(self, block, l):
            self.l = l
            self.b = block == "B"
            self.unit0 = l * U_LAYER_B + DEPTH * U_LAYER_A if self.b else l * U_LAYER_A
            self.turn0 = l * (U_LAYER_B // RING) + DEPTH * U_LAYER_A // RING if self.b else l * (U_LAYER_A // RING)
            self.sub0 = l * 3 + 3 * DEPTH if self.b else l * 3

        def done_units(self, k):
            return self.unit0 + (k + 1 + CREDIT)

        def turn(self, k):
            return self.turn0 + (k // RING + 1)

        def ffn(self, n):
            return self.l + 2 * DEPTH if self.b else self.l * 2 + n

    class Chunk(Layer):

        def __init__(self, L, c):
            self.l, self.b, self.sub0 = L.l, L.b, L.sub0
            self.unit0 = L.unit0 + (c - 2) * RING
            self.turn0 = L.turn0 + (c - 2)

    block = ctx.enter_context(nc.Block())

    @block.sync
    def _(sp):
        def unit(L, k, halves):
            sp.wait_ge(low_ready, L.unit0 + (k + 1))
            sp.sem_inc(raw_free, 1)
            for dst, src in halves:
                sp.dma_start(dst, src).then_inc(raw_landed[k % RING], 16)

        def rows(w, l, k0, n, c0, width):
            return w[bass.ds(l, 1), k0:k0 + n * P, c0:c0 + width].rearrange("o (k p) n -> p (o k) n", p=P)

        def square(L, k, w, k0, c0):
            dst = raw[:, k % RING, :].rearrange("p (k n) -> p k n", k=4)
            unit(L, k, [(dst[:, 2 * i:2 * i + 2, :], rows(w, L.l, k0 + 2 * P * i, 2, c0, 512)) for i in range(2)])

        def narrow(L, k, w, c0, width):
            dst = raw[:, k % RING, 0:KD * width].rearrange("p (k n) -> p k n", k=KD)
            unit(L, k, [(dst[:, 4 * i:4 * i + 4, :], rows(w, L.l, 512 * i, 4, c0, width)) for i in range(2)])

        def gate_up(L, k, kh, wg, wu, c):
            dst = raw[:, k % RING, :].rearrange("p (k g n) -> p k g n", k=4, g=2)
            halves = []
            for g, w in enumerate((wg, wu)):
                src = w[bass.ds(L.l, 1), 512 * kh:512 * kh + 512, bass.ds(c * FC, FC)]
                halves.append((dst[:, :, g, :], src.rearrange("o (k p) n -> p (o k) n", p=P)))
            unit(L, k, halves)

        def down(L, k, wd, c):
            dst = raw[:, k % RING, :].rearrange("p (k n) -> p k n", k=2)
            src = wd[bass.ds(L.l, 1), bass.ds(c * FC, FC), :].rearrange("o (k p) n -> p (o k) n", p=P)
            unit(L, k, [(dst[:, i:i + 1, :], src[:, i:i + 1, :]) for i in range(2)])

        def ffn(L, k0, wg, wu, wd):
            for kh in range(2):
                gate_up(L, k0 + kh, kh, wg, wu, 0)

            def chunk(c, k, L=L):
                gate_up(L, k, 0, wg, wu, c)
                gate_up(L, k + 1, 1, wg, wu, c)
                down(L, k + 2, wd, c - 1)

            chunk(1, k0 + 2)
            with sp.Fori(2, NCHUNK) as c:
                chunk(c, k0 + 5, Chunk(L, c))
            down(L, k0 + U_FFN - 1, wd, NCHUNK - 1)

        for t in range(TT):
            sp.dma_start(x[:, t, :], d["x"][0, t * P:(t + 1) * P, :]).then_inc(start_loaded, 16)
        sp.dma_start(const[:, :], d["const"]).then_inc(start_loaded, 16)
        with sp.Fori(0, DEPTH) as l:
            L = Layer("A", l)
            ffn(L, 0, d["ffn1_w_gate"], d["ffn1_w_up"], d["ffn1_w_down"])
            k = U_FFN
            narrow(L, k, d["w_in"], A_LR, RANK)
            k += 1
            for c0 in A_CHUNKS.values():
                for kh in range(2):
                    square(L, k, d["w_in"], 512 * kh, c0)
                    k += 1
            for b in A_SECTIONS:
                for half in range(2):
                    for kh in range(2):
                        square(L, k, d["w_in"], 512 * kh, A_GATES + b * D + 512 * half)
                        k += 1
                for half in range(2):
                    square(L, k, d["w_branch"], b * BW, 512 * half)
                    k += 1
            for kh in range(2):
                for half in range(2):
                    square(L, k, d["w_out"], 512 * kh, 512 * half)
                    k += 1
            assert k == U_FFN + U_MIX_A
            ffn(L, k, d["ffn2_w_gate"], d["ffn2_w_up"], d["ffn2_w_down"])
        with sp.Fori(0, DEPTH) as l:
            L = Layer("B", l)
            narrow(L, 0, d["w_in_2"], B_FF, 8)
            k = 1
            for c0 in B_CHUNKS.values():
                for kh in range(2):
                    square(L, k, d["w_in_2"], 512 * kh, c0)
                    k += 1
            for name in ("w_cv_2", "w_ck_2"):
                for half in range(2):
                    for kh in range(2):
                        square(L, k, d[name], 512 * kh, 512 * half)
                        k += 1
            for name in ("w_out_2", "w_cq_2", "w_co_2"):
                for kh in range(2):
                    for half in range(2):
                        square(L, k, d[name], 512 * kh, 512 * half)
                        k += 1
            assert k == U_MIX_B
            ffn(L, k, d["w_gate_2"], d["w_up_2"], d["w_down_2"])
        last = Layer("B", DEPTH)
        for k in range(AHEAD):
            dst = raw[:, k, :].rearrange("p (k n) -> p k n", k=4)
            src = d["w_co_2"][DEPTH - 1, 0:512, 512 * k:512 * k + 512].rearrange("(k p) n -> p k n", p=P)
            unit(last, k, [(dst[:, 2 * i:2 * i + 2, :], src[:, 2 * i:2 * i + 2, :]) for i in range(2)])
        for t in range(TT):
            sp.wait_ge(x_ready, 2 * 6 * DEPTH + t + 1)
            sp.dma_start(out[0, t * P:(t + 1) * P, :], x[:, t, :]).then_inc(stored, 16)
        sp.wait_ge(stored, 16 * TT)

    @block.gpsimd
    def _(pool):
        nc.gpsimd.sem_inc(low_ready, CREDIT)
        total = UNITS + AHEAD

        def low(slot, u):
            pool.wait_ge(high_ready, u + 1)
            nc.gpsimd.tensor_tensor(w_lo[:, slot, :], raw[:, slot, :], w_hi[:, slot, :].bitcast(F32),
                                    ALU.subtract).then_inc(low_ready, 1)

        with pool.Fori(0, total // RING) as r:
            for slot in range(RING):
                low(slot, r * RING + slot)
        for slot in range(total % RING):
            low(slot, total - total % RING + slot)

    @block.tensor
    def _(pe):
        def products(left, tiles, slot, view, bank, start, stop, before=None, halves=1):
            hi, lo = left
            parts = [view(w[:, slot, :]) for w in (w_hi, w_lo)]
            passes = ((hi, 0), (hi, 1), (lo, 0))
            for t in range(TT):
                if before:
                    before(t)
                for half in range(halves):
                    for i, k in enumerate(tiles):
                        for n, (act, part) in enumerate(passes):
                            w = parts[part][:, i, :]
                            if halves > 1:
                                w = w[:, 512 * half:512 * half + 512]
                            mm = nc.tensor.matmul(bank(t, half), act[:, k, t * P:(t + 1) * P], w,
                                                  start=start and i == 0 and n == 0,
                                                  stop=stop and i == len(tiles) - 1 and n == 2)
            return mm

        def weights(L, k):
            pe.wait_ge(low_ready, L.done_units(k))

        by4 = lambda w: w.rearrange("p (k n) -> p k n", k=4)
        by2 = lambda w: w.rearrange("p (k n) -> p k n", k=2)
        hT, bT = (hT_hi, hT_lo), (bT_hi, bT_lo)

        def left_ready(L, j, kh):
            return lambda t: pe.wait_ge(hT_ready, L.sub0 * 4 + (4 * j + 2 * t + kh + 1))

        def square(L, k, left, first, bank, start, stop, before=None):
            weights(L, k)
            products(left, range(first, first + 4), k % RING, by4, bank, start, stop, before).then_inc(unit_done, 1)

        def norm_turn(L, j):
            for t in range(TT):
                pe.wait_ge(h_ready, L.sub0 * 2 + (2 * j + t + 1))
                for kh in range(2):
                    for c in range(4):
                        mm = nc.tensor.transpose(ps[:, 2 * t + kh, c * P:(c + 1) * P],
                                                 xn[:, t, (4 * kh + c) * P:(4 * kh + c + 1) * P], ident)
                    mm.then_inc(h_turned, 1)

        def turn(src, banks, blocks=4):
            for c in range(blocks):
                for t in range(TT):
                    at = (c % 2) * T + t * P
                    mm = nc.tensor.transpose(ps[:, banks + c // 2, at:at + P], src[:, t, c * P:(c + 1) * P], ident)
            return mm

        def ffn(L, n, j, k0):
            f = L.ffn(n)
            mid = lambda t, half: ps[:, 4 + t, :]
            acc = lambda t, half: ps[:, 2 * t + half, :]

            def gate_up(M, k, before):
                for kh in range(2):
                    square(M, k + kh, hT, 4 * kh, mid, kh == 0, kh == 1, before(kh) if before else None)

            def hidden(c):
                pe.wait_ge(hid_ready, f * NCHUNK + (c + 1))
                for i in range(2):
                    for t in range(TT):
                        mm = nc.tensor.transpose(ps[:, 6, i * T + t * P:i * T + (t + 1) * P],
                                                 hid[:, t, i * P:(i + 1) * P], ident)
                mm.then_inc(hid_turned, 1)

            def down(M, k, c, start, stop):
                weights(M, k)
                pe.wait_ge(gT_ready, f * NCHUNK + (c + 1))
                products(bT, (KD, KD + 1), k % RING, by2, acc, start, stop, None, 2).then_inc(unit_done, 1)

            gate_up(L, k0, lambda kh: left_ready(L, j, kh))
            hidden(0)
            gate_up(L, k0 + 2, None)
            down(L, k0 + 4, 0, True, False)
            with pe.Fori(2, NCHUNK) as c:
                M = Chunk(L, c)
                hidden(c - 1)
                gate_up(M, k0 + 5, None)
                down(M, k0 + 7, c - 1, False, False)
            hidden(NCHUNK - 1)
            down(L, k0 + U_FFN - 1, NCHUNK - 1, False, True)

        def pair(n):
            return lambda t, half: ps[:, 2 * (n % 2) + t, :]

        def narrow(L, k, width, j):
            weights(L, k)
            view = lambda w: w[:, 0:KD * width].rearrange("p (k n) -> p k n", k=KD)

            def before(t):
                left_ready(L, j, 0)(t)
                left_ready(L, j, 1)(t)
            products(hT, range(KD), k % RING, view, lambda t, half: ps[:, 6, t * width:(t + 1) * width], True, True,
                     before).then_inc(unit_done, 1)

        def gla_rank(l):
            pe.wait_ge(*after("gla_rank", "rows", l))
            for t in range(TT):
                mm = nc.tensor.transpose(ps[0:RANK, 6, P + t * P:P + (t + 1) * P], lr_rows[:, t, :], ident)
            mm.then_inc(*done("gla_rank_turned", "turned"))

        def gla_alpha(l):
            pe.wait_ge(*after("gla_rank", "turned", l))
            pe.wait_ge(pack_loaded, l * 16 + 16)
            for t in range(TT):
                mm = nc.tensor.matmul(ps[:, 7, t * T:(t + 1) * T], lrT[0:RANK + 1, t * P:(t + 1) * P],
                                      packed(PACK_A, "w_alpha")[0:RANK + 1, :], start=True, stop=True)
            mm.then_inc(*done("gla_alpha", "logits"))

        def gla_decays(l):
            pe.wait_ge(*after("gla_in", "qk", l))
            for c in range(2):
                for t in range(TT):
                    mm = nc.tensor.transpose(ps[:, 6, c * T + t * P:c * T + (t + 1) * P], gqk[:, t, c * P:(c + 1) * P],
                                             ident)
            mm.then_inc(*done("gla_turned", "q"))
            pe.wait_ge(*after("gla_keep", "softplus", l))
            for t in range(TT):
                nc.tensor.matmul(ps[:, 4, t * T:(t + 1) * T], konst("gla_suffix"), nla[:, t * T:(t + 1) * T],
                                 start=True, stop=True)
            for c in range(2):
                for t in range(TT):
                    mm = nc.tensor.matmul(ps[:, 5, 4 * c + 2 * t:4 * c + 2 * t + 2],
                                          nla[:, t * T + c * P:t * T + (c + 1) * P], konst("gla_chunk"),
                                          start=True, stop=True)
            mm.then_inc(*done("gla_sums", "sums"))

        def gla_updates(l):
            pe.wait_ge(*after("gla_decay", "keys", l))
            pe.wait_ge(*after("gla_in", "v", l))
            pe.wait_ge(*after("gla_decay", "q", l))
            pe.sem_inc(gla_free, 1)
            for half in range(2):
                rows = slice(64 * half, 64 * half + 64)
                for t in range(TT):
                    for c in range(2):
                        for e in range(2):
                            h = 2 * c + e
                            mm = nc.tensor.matmul(
                                ps[64 * e:64 * e + 64, 6 + half, (2 * c + t) * P:(2 * c + t + 1) * P],
                                gdec[rows, t * T + h * 64:t * T + h * 64 + 64], gv[rows, t, h * P:(h + 1) * P],
                                start=True, stop=True)
            mm.then_inc(*done("gla_updates", "updates"))

        def gla_reads(l):
            pe.wait_ge(*after("gla_state", "last", l))
            pe.sem_inc(gla_free, 1)
            for e in range(2):
                rows = slice(64 * e, 64 * e + 64)
                for n in range(4):
                    t, half = n // 2, n % 2
                    for c in range(2):
                        mm = nc.tensor.matmul(
                            ps[64 * half:64 * half + 64, 4 + e, (2 * t + c) * P:(2 * t + c + 1) * P],
                            gqT[rows, c, n * 64:n * 64 + 64], gstate[rows, c, n, :], start=True, stop=True)
            mm.then_inc(*done("gla_reads", "reads"))

        def conv_turn(l):
            pe.wait_ge(*after("conv_glu", "glu", l))
            turn(conv_u, 6).then_inc(*done("conv_turned", "u"))

        def sb_turn_q(l):
            pe.wait_ge(*after("sb_in", "q", l))
            pe.wait_ge(*after("gla_out", "rows", l))
            turn(sb_q, 4).then_inc(*done("sb_turned", "q"))

        def gla_turn(l):
            pe.wait_ge(*after("gla_out", "gated", l))
            pe.wait_ge(*after("conv_glu", "u", l))
            turn(go_f.rearrange("p (t n) -> p t n", t=TT), 6).then_inc(*done("gla_out_turned", "turned"))

        def sb_turn_k(l):
            pe.wait_ge(*after("sb_in", "k", l))
            pe.wait_ge(*after("sb_in", "qT", l))
            turn(sb_k, 4).then_inc(*done("sb_turned", "k"))

        def sb_logits(l, c):
            pe.wait_ge(*after("sb_in", "kT", l))
            if c:
                pe.wait_ge(*after("sb_weights", f"copied{c - 1}", l))
                pe.wait_ge(*after("sb_out_low", f"out{c - 1}", l))
            for e in range(2):
                r = slice(64 * e, 64 * e + 64)
                nc.tensor.matmul(ps[:, 4 + e, 0:256], sbkT[r, c, 0:P], sbqT[r, c, :], start=True, stop=True)
                mm = nc.tensor.matmul(ps[:, 4 + e, 256:384], sbkT[r, c, P:T], sbqT[r, c, P:T], start=True, stop=True)
            mm.then_inc(*done("sb_logits", f"logits{c}"))

        def sb_sums(l, c):
            pe.wait_ge(*after("sb_keep", f"masked{c}", l))
            if c:
                pe.wait_ge(*after("sb_keep", f"exponent{c - 1}", l))
            else:
                pe.wait_ge(*after("gla_out_low", "out", l))
            for e in range(2):
                s = sb_sp[:, e * 384:(e + 1) * 384]
                nc.tensor.matmul(ps[:, 6 + e, 256:384], konst("tri_ge"), s[:, 256:384], start=True, stop=True)
                nc.tensor.matmul(ps[:, 6 + e, 0:256], konst("tri_ge"), s[:, 0:256], start=True, stop=False)
                mm = nc.tensor.matmul(ps[:, 6 + e, P:256], konst("ones"), s[:, 256:384], start=False, stop=True)
            mm.then_inc(*done("sb_sums", f"sums{c}"))

        def sb_out(l, c):
            pe.wait_ge(*after("sb_weights", f"weights{c}", l))
            for e in range(2):
                w = sb_e[:, e * 384:(e + 1) * 384]
                r, h = slice(64 * e, 64 * e + 64), 2 * c + e
                v = sbv[:, :, h * 64:h * 64 + 64]
                nc.tensor.matmul(ps[r, 4, 384:512], v[:, 0, :], w[:, 0:P], start=True, stop=True)
                nc.tensor.matmul(ps[r, 5, 384:512], v[:, 0, :], w[:, P:256], start=True, stop=False)
                mm = nc.tensor.matmul(ps[r, 5, 384:512], v[:, 1, :], w[:, 256:384], start=False, stop=True)
            mm.then_inc(*done("sb_out", f"out{c}"))

        def conv_rows(l):
            pe.wait_ge(*after("conv_taps", f"tap{CW - 1}_3", l))
            pe.wait_ge(*after("sb_keep", "exponent3", l))
            for t in range(TT):
                for c in range(4):
                    mm = nc.tensor.transpose(ps[:, 6 + t, c * P:(c + 1) * P], conv_y[:, c, t * P:(t + 1) * P], ident)
            mm.then_inc(*done("conv_rows", "rows"))

        def conv_normed(l):
            pe.wait_ge(*after("conv_norm", "normed1", l))
            pe.wait_ge(*after("sb_out_low", "out3", l))
            turn(conv_n, 4).then_inc(*done("conv_normed", "turned"))

        def merged_turn(l):
            pe.wait_ge(*after("conv_out", "act3", l))
            for kh in range(2):
                pe.wait_ge(*after("merge", f"branch2_{kh}", l))
                for t in range(TT):
                    for c in range(4):
                        mm = nc.tensor.transpose(ps[:, 4 + 2 * kh + t, c * P:(c + 1) * P],
                                                 merged[:, t, (4 * kh + c) * P:(4 * kh + c + 1) * P], ident)
                    mm.then_inc(*done("merged_turned", f"k{kh}t{t}"))

        def mixer_a(L):
            l, k = L.l, U_FFN
            norm_turn(L, 1)
            narrow(L, k, RANK, 1)
            k += 1
            evicted = list(A_CHUNKS)
            steps = {("gla_qk", 1): [gla_rank], ("gla_v", 1): [gla_alpha], ("gla_r", 1): [gla_decays],
                     ("conv_a", 1): [gla_updates], ("conv_g", 1): [gla_reads], ("sb_q", 0): [conv_turn],
                     ("sb_k", 0): [sb_turn_q], ("sb_k", 1): [gla_turn], ("sb_v", 0): [sb_turn_k]}
            for n, name in enumerate(evicted):
                if n >= 2:
                    prev = evicted[n - 2]
                    pe.wait_ge(*after(f"{prev.split('_')[0]}_in", prev.split("_")[1], l))
                for kh in range(2):
                    square(L, k, hT, 4 * kh, pair(n), kh == 0, kh == 1)
                    k += 1
                    for step in steps.get((name, kh), ()):
                        step(l)
            first_of_branch = {2: 0, 0: 4, 1: 0}
            for i, b in enumerate(A_SECTIONS):
                for half in range(2):
                    if i or half:
                        pe.wait_ge(*after("gates", f"gate{i if half else i - 1}_{1 - half}", l))
                    else:
                        pe.wait_ge(*after("sb_in", "k", l))
                    for kh in range(2):
                        square(L, k, hT, 4 * kh, pair(0), kh == 0, kh == 1)
                        k += 1
                        n = 6 * i + 2 * half + kh
                        if n % 2 == 0 and 2 <= n <= 8:
                            sb_out(l, n // 2 - 1)
                        if n % 2 == 0 and n < 8:
                            sb_logits(l, n // 2)
                        if n % 2 == 1 and n < 8:
                            sb_sums(l, n // 2)
                        if n == 14:
                            conv_normed(l)
                pe.wait_ge(*after(("gla_out_low", "sb_out_low", "conv_out_low")[i], ("out", "out3", "out")[i], l))
                for half in range(2):
                    if i or half:
                        pe.wait_ge(*after("merge", f"branch{i if half else i - 1}_{1 - half}", l))
                    else:
                        pe.wait_ge(*after("sb_in", "v", l))
                    square(L, k, bT, first_of_branch[b], pair(1), True, True)
                    k += 1
                    n = 6 * i + 4 + half
                    if n in (4,):
                        sb_out(l, 1)
                        sb_logits(l, 2)
                    if n == 5:
                        sb_sums(l, 2)
                    if n == 11:
                        conv_rows(l)
            merged_turn(l)
            for kh in range(2):
                for half in range(2):
                    before = lambda t, kh=kh: pe.wait_ge(*after("merged_low", f"k{kh}t{t}", l))
                    square(L, k, hT, 4 * kh, lambda t, _, half=half: ps[:, 2 * t + half, :], kh == 0, kh == 1, before)
                    k += 1

        def memory_turn():
            for t in range(TT):
                pe.wait_ge(*after("memory_rows", f"normed{t}", 0))
                for kh in range(2):
                    for c in range(4):
                        mm = nc.tensor.transpose(ps[:, 2 * t + kh, c * P:(c + 1) * P],
                                                 xn[:, t, (4 * kh + c) * P:(4 * kh + c + 1) * P], ident)
                    mm.then_inc(*done("memory_turned", f"t{t}k{kh}"))

        def fox_decay(l):
            pe.wait_ge(*after("fox_gate", "log", l))
            nc.tensor.matmul(ps[:, 7, 0:8], konst("tri_le"), flog[:, 0, :], start=True, stop=True)
            nc.tensor.matmul(ps[:, 7, 8:16], konst("ones"), flog[:, 0, :], start=True, stop=False)
            nc.tensor.matmul(ps[:, 7, 8:16], konst("tri_le"), flog[:, 1, :], start=False, stop=True)
            for r in (0, 64):
                nc.tensor.matmul(ps[r:r + 8, 7, 128:256], flog[:, 0, :], konst("tri_le"), start=True, stop=True)
                nc.tensor.matmul(ps[r:r + 8, 7, 256:384], flog[:, 0, :], konst("ones"), start=True, stop=False)
                mm = nc.tensor.matmul(ps[r:r + 8, 7, 256:384], flog[:, 1, :], konst("tri_le"), start=False, stop=True)
            mm.then_inc(*done("fox_decay", "sums"))

        def fox_turn(l, which):
            pe.wait_ge(*after("fox_in", which, l))
            if which == "k":
                pe.wait_ge(*after("fox_gate", "rows", l))
            turn(fq if which == "q" else fk, 4 if which == "q" else 6).then_inc(*done("fox_turned", which))

        def lru_turn(l):
            pe.wait_ge(*after("lru_in", "xy", l))
            pe.wait_ge(*after("fox_in", "qT", l))
            turn(lxy, 4).then_inc(*done("lru_turned", "xy"))

        def fox_logits(l, g):
            t, n = g // 2, P * (g // 2 + 1)
            if g == 0:
                pe.wait_ge(*after("fox_in", "kT", l))
                pe.wait_ge(*after("fox_gate", "rows", l))
            elif g == 1:
                pe.wait_ge(*after("fox_rows", "rows0", l))
            elif g == 2:
                pe.wait_ge(*after("ret_scores", "scores1", l))
            else:
                pe.wait_ge(*after("fox_rows", "rows2", l))
            for i in range(2):
                c = 2 * (g % 2) + i
                for e in range(2):
                    r, h = 64 * e, 2 * c + e
                    bank = ps[:, 6 + e, i * T:i * T + n]
                    pick = konst("fox_pick").rearrange("p (h q) -> p h q", h=8)
                    nc.tensor.matmul(bank, pick[r:r + 8, h, :], fcT[r:r + 8, 0:n], start=True, stop=False)
                    mm = nc.tensor.matmul(bank, fqT[r:r + 64, c, t * P:(t + 1) * P], fkT[r:r + 64, c, 0:n],
                                          start=False, stop=True)
            mm.then_inc(*done("fox_logits", f"logits{g}"))

        def lru_gates(l):
            pe.wait_ge(*after("lru_conv", f"tap{CW2 - 1}_1", l))
            for g, name in enumerate(("w_r", "w_i")):
                w = packed(PACK_B, name).rearrange("p (c n) -> p c n", c=2)
                for c in range(2):
                    mm = nc.tensor.matmul(ps[:, 4 + g, c * T:(c + 1) * T], w[:, c, :], lru[0][:, c * T:(c + 1) * T],
                                          start=True, stop=True)
            mm.then_inc(*done("lru_gates", "logits"))

        def fox_turn_p(l, g):
            pe.wait_ge(*after("fox_rows", f"weights{g}", l))
            if g == 0:
                pe.wait_ge(*after("lru_act", "i1", l))
            else:
                pe.wait_ge(*after("fox_out_low", f"out{g - 1}", l))
            for s in range(g // 2 + 1):
                for b in range(4):
                    mm = nc.tensor.transpose(ps[:, 4 + s, b * P:(b + 1) * P], fl[:, b, s * P:(s + 1) * P], ident)
            mm.then_inc(*done("fox_p_turned", f"turned{g}"))

        def fox_out(l, g):
            pe.wait_ge(*after("fox_p", f"copied{g}", l))
            pe.wait_ge(*after("fox_in", "v", l))
            for i in range(2):
                for e in range(2):
                    h = 2 * (2 * (g % 2) + i) + e
                    for s in range(g // 2 + 1):
                        mm = nc.tensor.matmul(ps[64 * e:64 * e + 64, 4, i * P:(i + 1) * P], fv[:, s, h * 64:h * 64 + 64],
                                              fpT[:, 4 * s + 2 * i + e, :], start=s == 0, stop=s == g // 2)
            mm.then_inc(*done("fox_out", f"out{g}"))

        def ret_turn(l):
            pe.wait_ge(*after("ret_rope", "rotated", l))
            pe.wait_ge(*after("fox_rows", "rows1", l))
            turn(rope, 6).then_inc(*done("ret_turned", "qk"))

        def ret_scores(l, c):
            if c == 0:
                pe.wait_ge(*after("ret_rope", "qkT", l))
            else:
                pe.wait_ge(*after("ret_scores", "scores0", l))
            for e in range(2):
                r = slice(64 * e, 64 * e + 64)
                q, kk = rT[r, c, :], rT[r, 2 + c, :]
                nc.tensor.matmul(ps[:, 6 + e, 0:256], kk[:, 0:P], q, start=True, stop=True)
                mm = nc.tensor.matmul(ps[:, 6 + e, 256:384], kk[:, P:T], q[:, P:T], start=True, stop=True)
            mm.then_inc(*done("ret_dots", f"dots{c}"))

        def ret_rows(l):
            pe.wait_ge(*after("ret_scores", "scores1", l))
            pe.wait_ge(*after("ret_in", "v", l))
            pe.wait_ge(*after("fox_rows", "rows3", l))
            for t in range(TT):
                for h in range(4):
                    o = ps[:, 6, t * 256 + h * 64:t * 256 + h * 64 + 64]
                    if t == 0:
                        mm = nc.tensor.matmul(o, ret_s[:, h, 0:P], rv[:, 0, h * 64:h * 64 + 64], start=True, stop=True)
                    else:
                        nc.tensor.matmul(o, ret_s[:, h, P:T], rv[:, 0, h * 64:h * 64 + 64], start=True, stop=False)
                        mm = nc.tensor.matmul(o, ret_s[:, h, T:384], rv[:, 1, h * 64:h * 64 + 64], start=False, stop=True)
            mm.then_inc(*done("ret_rows", "rows"))

        def ret_back(l):
            pe.wait_ge(*after("ret_norm", "gated", l))
            turn(ry_f.rearrange("p (t n) -> p t n", t=TT), 6, 2).then_inc(*done("ret_back", "turned"))

        def keys_turn(l, half):
            pe.wait_ge(*after("memory_in", f"k{half}", l))
            if half == 0:
                pe.wait_ge(*after("fox_out_low", "out3", l))
            else:
                pe.wait_ge(*after("ret_out_low", "out", l))
            turn(km[:, :, half * 512:half * 512 + 512], 4 + 2 * half).then_inc(*done("keys_turned", f"k{half}"))

        def mixer_b(L):
            l = L.l
            norm_turn(L, 0)
            narrow(L, 0, 8, 0)
            k = 1
            chunks = [("fox_q", 512), ("fox_k", 0), ("lru_xy", 0), ("fox_v", 0), ("ret_qk", 0), ("ret_vg", 0)]
            read = [("fox_in", "q"), ("fox_in", "k"), ("lru_in", "xy"), ("fox_in", "v"), ("ret_in", "qk"),
                    ("ret_in", "g"), ("memory_in", "v0"), ("memory_in", "v1"), ("memory_in", "k0"), ("memory_in", "k1")]
            steps = {0: [fox_decay], 1: [lambda l: fox_turn(l, "q")], 2: [lambda l: fox_turn(l, "k")],
                     3: [lru_turn, lambda l: fox_logits(l, 0)], 4: [lru_gates, lambda l: fox_logits(l, 1)],
                     5: [lambda l: fox_turn_p(l, 0), ret_turn]}
            for n in range(len(chunks)):
                if n >= 2:
                    pe.wait_ge(*after(*read[n - 2], l))
                for kh in range(2):
                    square(L, k, hT, 4 * kh, pair(n), kh == 0, kh == 1)
                    k += 1
                for step in steps[n]:
                    step(l)
            memory_steps = [[lambda: fox_out(l, 0), lambda: ret_scores(l, 0)], [lambda: fox_turn_p(l, 1), lambda: ret_scores(l, 1)],
                            [lambda: fox_out(l, 1), lambda: fox_logits(l, 2)], [lambda: fox_turn_p(l, 2), lambda: fox_logits(l, 3)],
                            [lambda: fox_out(l, 2), lambda: ret_rows(l)], [lambda: fox_turn_p(l, 3)],
                            [lambda: fox_out(l, 3), lambda: ret_back(l)], [lambda: keys_turn(l, 0)]]
            for n in range(4):
                pe.wait_ge(*after(*read[4 + n], l))
                for kh in range(2):
                    square(L, k, bT, 4 * kh, pair(n), kh == 0, kh == 1)
                    k += 1
                    for step in memory_steps[2 * n + kh]:
                        step()
            acc = lambda half: (lambda t, _: ps[:, 2 * t + half, :])
            pe.wait_ge(*after("lru_low", "out", l))
            pe.wait_ge(*after("memory_in", "k1", l))
            for kh in range(2):
                if kh:
                    pe.wait_ge(*after("ret_out_low", "out", l))
                else:
                    pe.wait_ge(*after("fox_out_low", "out3", l))
                for half in range(2):
                    square(L, k, hT, 4 * kh, acc(half), kh == 0, kh == 1)
                    k += 1
            keys_turn(l, 1)
            assert k == 25

        def cross(L):
            l, k = L.l, 25
            acc = lambda half: (lambda t, _: ps[:, 2 * t + half, :])
            norm_turn(L, 1)
            pe.wait_ge(hT_ready, L.sub0 * 4 + 8)
            for kh in range(2):
                for half in range(2):
                    square(L, k, hT, 4 * kh, acc(half), kh == 0, kh == 1)
                    k += 1
            for half in range(2):
                for t in range(TT):
                    pe.wait_ge(*after("cross_in", f"q{t}", l))
                pe.wait_ge(*after("memory_keys", "k1", l))
                turn(cq[:, :, half * 512:half * 512 + 512], 4 + 2 * half).then_inc(*done("cross_turned", f"q{half}"))
            for t in range(TT):
                pe.wait_ge(*after("cross_in", "qT1", l))
                for h in range(4):
                    for i in range(2):
                        c = 2 * h + i
                        mm = nc.tensor.matmul(ps[:, 2 * t + h // 2, (h % 2) * T:(h % 2 + 1) * T],
                                              cqT[:, c, t * P:(t + 1) * P], kmT[:, c, :], start=i == 0, stop=i == 1)
                mm.then_inc(*done("cross_logits", f"logits{t}"))
            for t in range(TT):
                pe.wait_ge(*after("cross_rows", f"weights{t}", l))
                for m in range(2):
                    for h in range(4):
                        mm = nc.tensor.transpose(ps[:, 4 + 2 * t + m, h * P:(h + 1) * P], cp[t][:, h, m * P:(m + 1) * P],
                                                 ident)
                mm.then_inc(*done("cross_p_turned", f"turned{t}"))
            for t in range(TT):
                pe.wait_ge(*after("cross_p", f"copied{t}", l))
            for c in range(KD):
                for m in range(2):
                    mm = nc.tensor.matmul(ps[:, c // 2, (c % 2) * T:(c % 2 + 1) * T], vm[:, m, c * P:(c + 1) * P],
                                          cpT[:, 4 * m + c // 2, :], start=m == 0, stop=m == 1)
                if c % 2:
                    mm.then_inc(*done("cross_out", f"out{c // 2}"))
            for kh in range(2):
                pe.wait_ge(*after("cross_out_low", "out3" if kh == 0 else "out3", l))
                for half in range(2):
                    square(L, k, hT, 4 * kh, acc(half), kh == 0, kh == 1)
                    k += 1
            assert k == U_MIX_B

        nc.tensor.sem_inc(unit_done, CREDIT)
        pe.wait_ge(start_loaded, 16 * 3)
        with pe.Fori(0, DEPTH) as l:
            L = Layer("A", l)
            norm_turn(L, 0)
            ffn(L, 0, 0, 0)
            mixer_a(L)
            norm_turn(L, 2)
            ffn(L, 1, 2, U_FFN + U_MIX_A)
        memory_turn()
        with pe.Fori(0, DEPTH) as l:
            L = Layer("B", l)
            mixer_b(L)
            cross(L)
            norm_turn(L, 2)
            ffn(L, 0, 2, U_MIX_B)

    @block.scalar
    def _(act):
        def high(L, k):
            slot = k % RING
            act.wait_ge(raw_landed[slot], L.turn(k) * 32)
            act.wait_ge(unit_done, L.unit0 + (k + 1))
            nc.scalar.activation(w_hi[:, slot, :], raw[:, slot, :], ACT.Copy).then_inc(high_ready, 1)

        def multiplied(L, k):
            act.wait_ge(unit_done, L.done_units(k))

        def norm_in(L, j):
            s2 = L.sub0 * 2 + 2 * j
            for t in range(TT):
                act.wait_ge(x_ready, s2 + (t + 1))
                nc.scalar.activation(xn[:, t, :], x[:, t, :], ACT.Square,
                                     accum_out=ss_in[:, t:t + 1]).then_inc(sq_in, 1)
            for t in range(TT):
                act.wait_ge(sq_in, s2 + (t + 1))
                nc.scalar.activation(std_in[:, t:t + 1], ss_in[:, t:t + 1], ACT.Sqrt, bias=EPS,
                                     scale=1.0 / D).then_inc(std_ready, 1)
            for t in range(TT):
                for kh in range(2):
                    act.wait_ge(h_turned, s2 * 2 + (2 * t + kh + 1))
                    nc.scalar.activation(hT_hi[:, 4 * kh:4 * kh + 4, t * P:(t + 1) * P],
                                         ps[:, 2 * t + kh, :].rearrange("p (c n) -> p c n", c=4),
                                         ACT.Copy).then_inc(hT_hi_ready, 1)
            gain(post_g, L.sub0 + j, 1, post_loaded)
            act.wait_ge(h_ready, s2 + 2)
            gain(pre_g, L.sub0 + (j + 1), 0, pre_loaded)

        def gain(dst, s, side, loaded):
            act.dma_start(dst[:, :], d["gains"][bass.ds(s, 1), side, :].partition_broadcast(P)).then_inc(loaded, 16)

        def norm_out(L, j, k, half):
            s2 = L.sub0 * 2 + 2 * j
            m = 4.0 if half else 1.0
            multiplied(L, k)
            for t in range(TT):
                nc.scalar.activation(xn[:, t, :].rearrange("p (h n) -> p h n", h=2), ps[:, 2 * t:2 * t + 2, :], ACT.Square,
                                     accum_out=ss_out[:, t:t + 1]).then_inc(sq_out, 1)
            for t in range(TT):
                act.wait_ge(sq_out, s2 + (t + 1))
                nc.scalar.activation(std_out[:, t:t + 1], ss_out[:, t:t + 1], ACT.Sqrt, bias=m * EPS,
                                     scale=m / D).then_inc(std_out_ready, 1)

        def ffn(L, n, j, k0):
            f = L.ffn(n)

            def silu(M, k, c):
                multiplied(M, k)
                nc.scalar.activation(sil, ps[:, 4:6, 0:FC], ACT.Silu).then_inc(silu_ready, 1)

            def hidden(c):
                act.wait_ge(hid_turned, f * NCHUNK + (c + 1))
                nc.scalar.activation(bT_hi[:, KD:KD + 2, :], ps[:, 6, :].rearrange("p (i t) -> p i t", i=2),
                                     ACT.Copy).then_inc(gT_hi_ready, 1)

            def chunk(M, k, c):
                hidden(c - 1)
                high(M, k + AHEAD)
                high(M, k + 1 + AHEAD)
                silu(M, k + 1, c)
                high(M, k + 2 + AHEAD)

            high(L, k0 + AHEAD)
            high(L, k0 + 1 + AHEAD)
            silu(L, k0 + 1, 0)
            chunk(L, k0 + 2, 1)
            with act.Fori(2, NCHUNK) as c:
                chunk(Chunk(L, c), k0 + 5, c)
            hidden(NCHUNK - 1)
            high(L, k0 + U_FFN - 1 + AHEAD)
            norm_out(L, j, k0 + U_FFN - 1, not L.b)

        def copy(dst, src, stage, step, scale=1.0, func=ACT.Copy):
            nc.scalar.activation(dst, src, func, scale=scale).then_inc(*done(stage, step))

        def chunk_rows(n):
            return ps[:, 2 * (n % 2):2 * (n % 2) + 2, :]

        def two(bank):
            return ps[:, bank:bank + 2, :].rearrange("p b (c t) -> p (b c) t", c=2)

        def gla_alpha(l):
            act.wait_ge(*after("gla_alpha", "logits", l))
            nc.scalar.activation(gdec, ps[:, 7, :], ACT.Abs).then_inc(*done("gla_soft", "abs"))
            act.wait_ge(*after("gla_soft", "abs", l))
            nc.scalar.activation(gdec, gdec, ACT.Exp, scale=-1.0).then_inc(*done("gla_soft", "exp"))
            act.wait_ge(*after("gla_soft", "exp", l))
            nc.scalar.activation(gdec, gdec, ACT.Ln, bias=1.0).then_inc(*done("gla_soft", "ln"))

        def gla_decays(l):
            act.wait_ge(*after("gla_sums", "sums", l))
            nc.scalar.activation(gdec, ps[:, 4, :], ACT.Exp, scale=-1.0 / TAU).then_inc(*done("gla_exp", "to_end"))
            nc.scalar.activation(lam.rearrange("p c n -> p (c n)"), ps[:, 5, 0:8], ACT.Exp,
                                 scale=-1.0 / TAU).then_inc(*done("gla_exp", "chunk"))

        def gla_std(l):
            act.wait_ge(*after("gla_out", "sums", l))
            nc.scalar.activation(stdg, ssg, ACT.Sqrt, bias=EPS, scale=1.0 / P).then_inc(*done("gla_std", "std"))

        def gla_out(l):
            act.wait_ge(*after("gla_out_turned", "turned", l))
            for c in range(4):
                nc.scalar.activation(bT_hi[:, c, :], two(6)[:, c, :], ACT.Copy,
                                     scale=packed(PACK_A, "gla_g")[:, c:c + 1]).then_inc(*done("gla_out_high", f"out{c}"))

        def sb_weights(l, c):
            act.wait_ge(*after("sb_logits", f"logits{c}", l))
            nc.scalar.activation(sb_z.rearrange("p (e n) -> p e n", e=2), ps[:, 4:6, 0:384],
                                 ACT.Copy).then_inc(*done("sb_weights", f"copied{c}"))
            nc.scalar.activation(sb_e.rearrange("p (e n) -> p e n", e=2), ps[:, 4:6, 0:384],
                                 ACT.Abs).then_inc(*done("sb_weights", f"abs{c}"))
            act.wait_ge(*after("sb_weights", f"abs{c}", l))
            nc.scalar.activation(sb_e, sb_e, ACT.Exp, scale=-1.0).then_inc(*done("sb_weights", f"exp{c}"))
            act.wait_ge(*after("sb_weights", f"exp{c}", l))
            nc.scalar.activation(sb_e, sb_e, ACT.Ln, bias=1.0).then_inc(*done("sb_weights", f"ln{c}"))

        def sb_exp(l, c):
            act.wait_ge(*after("sb_keep", f"exponent{c}", l))
            nc.scalar.activation(sb_e, sb_z, ACT.Exp).then_inc(*done("sb_weights", f"weights{c}"))

        def sb_out(l, c):
            act.wait_ge(*after("sb_out", f"out{c}", l))
            nc.scalar.activation(bT_hi[:, 4 + c, :].rearrange("p (t n) -> p t n", t=TT), ps[:, 4:6, 384:512],
                                 ACT.Copy).then_inc(*done("sb_out_high", f"out{c}"))

        def conv_std(l):
            for t in range(TT):
                act.wait_ge(*after("conv_norm", f"centred{t}", l))
                nc.scalar.activation(conv_y_f[:, t * 512:(t + 1) * 512], conv_n[:, t, :], ACT.Square,
                                     accum_out=css[:, t:t + 1]).then_inc(*done("conv_std", f"sum{t}"))
            for t in range(TT):
                act.wait_ge(*after("conv_std", f"sum{t}", l))
                nc.scalar.activation(cstd[:, t:t + 1], css[:, t:t + 1], ACT.Sqrt, bias=EPS,
                                     scale=1.0 / BW).then_inc(*done("conv_std", f"std{t}"))

        def conv_out(l):
            act.wait_ge(*after("conv_normed", "turned", l))
            for c in range(4):
                nc.scalar.activation(conv_y[:, c, :], two(4)[:, c, :], ACT.Silu, bias=packed(PACK_A, "ln_b")[:, c:c + 1],
                                     scale=packed(PACK_A, "ln_g")[:, c:c + 1]).then_inc(*done("conv_out", f"act{c}"))
            act.wait_ge(*after("conv_out", "act3", l))
            multiplied_gla = U_FFN + 17 + 5
            act.wait_ge(unit_done, Layer("A", l).done_units(multiplied_gla))
            nc.scalar.activation(bT_hi[:, 0:4, :], conv_y, ACT.Copy).then_inc(*done("conv_out", "high"))

        def merged_high(l):
            for kh in range(2):
                for t in range(TT):
                    act.wait_ge(*after("merged_turned", f"k{kh}t{t}", l))
                    nc.scalar.activation(hT_hi[:, 4 * kh:4 * kh + 4, t * P:(t + 1) * P],
                                         ps[:, 4 + 2 * kh + t, :].rearrange("p (c n) -> p c n", c=4),
                                         ACT.Copy).then_inc(*done("merged_high", f"k{kh}t{t}"))

        def mixer_a(L):
            l, k = L.l, U_FFN
            act.wait_ge(x_ready, L.sub0 * 2 + 4)
            act.dma_start(pack[:, 0:PACK_A_W], d["pack_a"][bass.ds(l, 1), :, :].rearrange("o p n -> p (o n)")).then_inc(
                pack_loaded, 16)
            norm_in(L, 1)
            high(L, k + AHEAD)
            k += 1
            plan = {"gla_qk": (gqk, "gla_in", "qk", 1.0, ACT.Copy), "gla_v": (gv, "gla_in", "v", 1.0, ACT.Copy),
                    "gla_r": (gr, "gla_in", "r", 1.0, ACT.Silu), "conv_a": (conv_u, "conv_in", "a", 1.0, ACT.Copy),
                    "conv_g": (conv_s, "conv_in", "g", 1.0, ACT.Sigmoid),
                    "sb_q": (sb_q, "sb_in", "q", 0.125, ACT.Copy), "sb_k": (sb_k, "sb_in", "k", 1.0, ACT.Copy),
                    "sb_v": (sbv, "sb_in", "v", 1.0, ACT.Copy)}
            for n, name in enumerate(A_CHUNKS):
                high(L, k + AHEAD)
                if name == "gla_r":
                    gla_alpha(l)
                if name == "conv_a":
                    gla_decays(l)
                if name == "sb_k":
                    act.wait_ge(*after("sb_turned", "q", l))
                    copy(sbqT, two(4), "sb_in", "qT")
                if name == "sb_v":
                    gla_out(l)
                    act.wait_ge(*after("sb_turned", "k", l))
                    copy(sbkT, two(4), "sb_in", "kT")
                if name == "sb_q":
                    gla_std(l)
                high(L, k + 1 + AHEAD)
                multiplied(L, k + 1)
                dst, stage, step, scale, func = plan[name]
                if name == "sb_q":
                    act.wait_ge(*after("conv_turned", "u", l))
                if name == "sb_v":
                    act.wait_ge(*after("gla_out", "gated", l))
                copy(dst, chunk_rows(n), stage, step, scale, func)
                k += 2
            for i, b in enumerate(A_SECTIONS):
                for half in range(2):
                    for kh in range(2):
                        high(L, k + AHEAD)
                        n = 6 * i + 2 * half + kh
                        if kh:
                            multiplied(L, k)
                            if i:
                                act.wait_ge(*after("merge", f"branch{i - 1}_{half}", l))
                            nc.scalar.activation(sg[:, half, :, :], chunk_rows(0), ACT.Sigmoid).then_inc(
                                *done("gates", f"gate{i}_{half}"))
                        if n < 12:
                            section_step(l, n)
                        if n == 12:
                            conv_std(l)
                        if n == 15:
                            conv_out(l)
                        k += 1
                for half in range(2):
                    high(L, k + AHEAD)
                    section_step(l, 6 * i + 4 + half)
                    k += 1
            merged_high(l)
            for _ in range(4):
                high(L, k + AHEAD)
                k += 1
            norm_out(L, 1, k - 1, False)

        def section_step(l, n):
            if n % 2 == 0 and 2 <= n <= 8:
                sb_out(l, n // 2 - 1)
            if n % 2 == 0 and n < 8:
                sb_weights(l, n // 2)
            if n % 2 == 1 and n < 8:
                sb_exp(l, n // 2)

        def memory_rows():
            act.wait_ge(x_ready, 2 * 3 * DEPTH + TT)
            act.dma_start(xn[:, :, :], d["mem"][0, :, :].rearrange("(t p) n -> p t n", p=P)).then_inc(memory_loaded, 16)
            act.dma_start(pairbuf, d["mem_g"][0:1, :].partition_broadcast(P)).then_inc(memory_loaded, 16)
            act.dma_start(positions, d["positions"][:, :]).then_inc(memory_loaded, 16)
            act.wait_ge(memory_loaded, 16 * 3)
            for t in range(TT):
                nc.scalar.activation(fvrT_f[:, 0:D], xn[:, t, :], ACT.Square,
                                     accum_out=ss_in[:, t:t + 1]).then_inc(*done("memory_std", f"sum{t}"))
                act.wait_ge(*after("memory_std", f"sum{t}", 0))
                nc.scalar.activation(std_in[:, t:t + 1], ss_in[:, t:t + 1], ACT.Sqrt, bias=EPS,
                                     scale=1.0 / D).then_inc(*done("memory_std", f"std{t}"))
            for t in range(TT):
                for kh in range(2):
                    act.wait_ge(*after("memory_turned", f"t{t}k{kh}", 0))
                    nc.scalar.activation(bT_hi[:, 4 * kh:4 * kh + 4, t * P:(t + 1) * P],
                                         ps[:, 2 * t + kh, :].rearrange("p (c n) -> p c n", c=4),
                                         ACT.Copy).then_inc(*done("memory_high", f"t{t}k{kh}"))
            for name, table in (("sin", sin), ("cos", cos)):
                act.wait_ge(*after("rope_angles", name, 0))
                nc.scalar.activation(table, table, ACT.Sin).then_inc(*done("rope_tables", name))

        def fox_soft(l):
            act.wait_ge(*after("fox_gate", "logits", l))
            z = flog.rearrange("p t h -> p (t h)")
            nc.scalar.activation(ftmp, z, ACT.Abs).then_inc(*done("fox_soft", "abs"))
            act.wait_ge(*after("fox_soft", "abs", l))
            nc.scalar.activation(ftmp, ftmp, ACT.Exp, scale=-1.0).then_inc(*done("fox_soft", "exp"))
            act.wait_ge(*after("fox_soft", "exp", l))
            nc.scalar.activation(ftmp, ftmp, ACT.Ln, bias=1.0).then_inc(*done("fox_soft", "ln"))

        def lru_lambda(l):
            act.wait_ge(pack_loaded, l * 16 + (16 * DEPTH + 16))
            nc.scalar.activation(lru_t, packed(PACK_B, "lam"), ACT.Abs).then_inc(*done("lru_act", "abs"))
            act.wait_ge(*after("lru_act", "abs", l))
            nc.scalar.activation(lru_t, lru_t, ACT.Exp, scale=-1.0).then_inc(*done("lru_act", "lambda"))

        def lru_gates(l):
            act.wait_ge(*after("lru_gates", "logits", l))
            for g, (dst, bias) in enumerate(((lru[1], "b_r"), (lru[2], "b_i"))):
                for c in range(2):
                    nc.scalar.activation(dst[:, c * T:(c + 1) * T], ps[:, 4 + g, c * T:(c + 1) * T], ACT.Sigmoid,
                                         bias=packed(PACK_B, bias)[:, c:c + 1]).then_inc(*done("lru_act", f"{'ri'[g]}{c}"))

        def lru_decay(l):
            act.wait_ge(*after("lru_math", "log1", l))
            nc.scalar.activation(lru[3], lru[1], ACT.Tanh).then_inc(*done("lru_act", "tanh"))
            act.wait_ge(*after("lru_act", "tanh", l))
            nc.scalar.activation(lru[1], lru[1], ACT.Exp).then_inc(*done("lru_act", "decay"))
            act.wait_ge(*after("lru_turn", "y", l))
            nc.scalar.activation(lyT, lyT, ACT.Gelu_apprx_tanh).then_inc(*done("lru_act", "gelu"))

        def lru_root(l):
            act.wait_ge(*after("lru_math", "square", l))
            nc.scalar.activation(lru[3], lru[3], ACT.Sqrt).then_inc(*done("lru_act", "root"))

        def lru_high(l):
            act.wait_ge(*after("lru_math", "out", l))
            nc.scalar.activation(hT_hi[:, 0:2, :], lru[0].rearrange("p (c t) -> p c t", c=2),
                                 ACT.Copy).then_inc(*done("lru_act", "high"))

        def fox_exp(l, g):
            n = P * (g // 2 + 1)
            act.wait_ge(*after("fox_rows", f"max{g}", l))
            for b in range(4):
                nc.scalar.activation(fl[:, b, 0:n], fl[:, b, 0:n], ACT.Exp, bias=fmax[:, b:b + 1],
                                     accum_out=fden[:, b:b + 1]).then_inc(*done("fox_exp", f"g{g}h{b}"))

        def fox_p(l, g):
            act.wait_ge(*after("fox_p_turned", f"turned{g}", l))
            n = g // 2 + 1
            nc.scalar.activation(fpT[:, 0:4 * n, :], ps[:, 4:4 + n, :].rearrange("p s (b t) -> p (s b) t", b=4),
                                 ACT.Copy).then_inc(*done("fox_p", f"copied{g}"))

        def fox_tiles(w, g):
            c, t = 2 + 2 * (g % 2), g // 2
            return w[:, c:c + 2, t * P:(t + 1) * P]

        def fox_out(l, g):
            act.wait_ge(*after("fox_out", f"out{g}", l))
            nc.scalar.activation(fox_tiles(hT_hi, g), ps[:, 4, 0:256].rearrange("p (c t) -> p c t", c=2),
                                 ACT.Copy).then_inc(*done("fox_out_high", f"out{g}"))

        def ret_std(l):
            act.wait_ge(*after("ret_norm", "sums", l))
            nc.scalar.activation(rstat2, rstat, ACT.Sqrt, bias=EPS, scale=1.0 / 64).then_inc(*done("ret_std", "std"))

        def ret_out(l):
            act.wait_ge(*after("ret_back", "turned", l))
            nc.scalar.activation(hT_hi[:, 6:8, :], ps[:, 6, :].rearrange("p (c t) -> p c t", c=2),
                                 ACT.Copy).then_inc(*done("ret_out_high", "out"))

        def keys(l, half):
            act.wait_ge(*after("keys_turned", f"k{half}", l))
            copy(kmT[:, 4 * half:4 * half + 4, :], two(4 + 2 * half), "memory_keys", f"k{half}")

        def mixer_b(L):
            l = L.l
            act.wait_ge(x_ready, L.sub0 * 2 + 2)
            act.dma_start(pack[:, 0:PACK_B_W], d["pack_b"][bass.ds(l, 1), :, :].rearrange("o p n -> p (o n)")).then_inc(
                pack_loaded, 16)
            norm_in(L, 0)
            high(L, AHEAD)
            k = 1
            between = {0: lambda: (fox_soft(l), lru_lambda(l)),
                       2: lambda: (act.wait_ge(*after("fox_turned", "q", l)), copy(fqT, two(4), "fox_in", "qT")),
                       3: lambda: (act.wait_ge(*after("fox_turned", "k", l)), copy(fkT, two(6), "fox_in", "kT")),
                       4: lambda: fox_exp(l, 0),
                       5: lambda: lru_gates(l)}
            rows = {0: [(fq, "fox_in", "q", 0.125)], 1: [(fk, "fox_in", "k", 1.0)], 2: [(lxy, "lru_in", "xy", 1.0)],
                    3: [(fv, "fox_in", "v", 1.0)], 4: [(rqk, "ret_in", "qk", 1.0)], 5: [(rv, "ret_in", "v", 1.0)]}
            for n in range(6):
                high(L, k + AHEAD)
                if n in between:
                    between[n]()
                high(L, k + 1 + AHEAD)
                multiplied(L, k + 1)
                for dst, stage, step, scale in rows[n]:
                    src = chunk_rows(n) if n < 5 else chunk_rows(n)[:, :, 0:256]
                    copy(dst, src, stage, step, scale)
                if n == 5:
                    copy(rg, chunk_rows(n)[:, :, 256:512], "ret_in", "g", 1.0, ACT.Silu)
                k += 2
            steps = [lambda: (fox_p(l, 0), fox_exp(l, 1)),
                     lambda: (lru_decay(l), fox_out(l, 0)),
                     lambda: (fox_p(l, 1), lru_root(l)),
                     lambda: (fox_out(l, 1), fox_exp(l, 2)),
                     lambda: (lru_high(l), fox_p(l, 2), fox_exp(l, 3)),
                     lambda: (fox_out(l, 2), ret_std(l)),
                     lambda: fox_p(l, 3),
                     lambda: (ret_out(l), fox_out(l, 3))]
            for n in range(4):
                name = ("v0", "v1", "k0", "k1")[n]
                dst = (vm, km)[n // 2][:, :, (n % 2) * 512:(n % 2) * 512 + 512]
                for kh in range(2):
                    high(L, k + kh + AHEAD)
                    steps[2 * n + kh]()
                multiplied(L, k + 1)
                if name == "k0":
                    act.wait_ge(*after("lru_low", "out", l))
                copy(dst, chunk_rows(n), "memory_in", name)
                k += 2
            keys(l, 0)
            for _ in range(4):
                high(L, k + AHEAD)
                k += 1
            keys(l, 1)
            norm_out(L, 0, k - 1, False)

        def cross(L):
            l, k = L.l, 25
            norm_in(L, 1)
            for _ in range(4):
                high(L, k + AHEAD)
                k += 1
            multiplied(L, k - 1)
            for t in range(TT):
                copy(cq[:, t, :].rearrange("p (h n) -> p h n", h=2), ps[:, 2 * t:2 * t + 2, :], "cross_in", f"q{t}", 1.0 / 16)
            for half in range(2):
                act.wait_ge(*after("cross_turned", f"q{half}", l))
                copy(cqT[:, 4 * half:4 * half + 4, :], two(4 + 2 * half), "cross_in", f"qT{half}")
            for t in range(TT):
                act.wait_ge(*after("cross_max", f"max{t}", l))
                for h in range(4):
                    nc.scalar.activation(cp[t][:, h, :], ps[:, 2 * t + h // 2, (h % 2) * T:(h % 2 + 1) * T], ACT.Exp,
                                         bias=cmax[:, 4 * t + h:4 * t + h + 1],
                                         accum_out=cden[:, 4 * t + h:4 * t + h + 1]).then_inc(*done("cross_exp", f"t{t}h{h}"))
            for t in range(TT):
                act.wait_ge(*after("cross_p_turned", f"turned{t}", l))
                copy(cpT[:, :, t * P:(t + 1) * P],
                     ps[:, 4 + 2 * t:6 + 2 * t, :].rearrange("p m (h n) -> p (m h) n", h=4), "cross_p", f"copied{t}")
            for c in range(4):
                act.wait_ge(*after("cross_out", f"out{c}", l))
                copy(hT_hi[:, 2 * c:2 * c + 2, :], ps[:, c, :].rearrange("p (c t) -> p c t", c=2), "cross_out_high", f"out{c}")
            for _ in range(4):
                high(L, k + AHEAD)
                k += 1
            norm_out(L, 1, k - 1, False)

        gain(pre_g, 0, 0, pre_loaded)
        act.wait_ge(start_loaded, 16 * 3)
        for k in range(AHEAD):
            act.wait_ge(raw_landed[k], 32)
            nc.scalar.activation(w_hi[:, k, :], raw[:, k, :], ACT.Copy).then_inc(high_ready, 1)
        with act.Fori(0, DEPTH) as l:
            L = Layer("A", l)
            norm_in(L, 0)
            ffn(L, 0, 0, 0)
            mixer_a(L)
            norm_in(L, 2)
            ffn(L, 1, 2, U_FFN + U_MIX_A)
        memory_rows()
        with act.Fori(0, DEPTH) as l:
            L = Layer("B", l)
            mixer_b(L)
            cross(L)
            norm_in(L, 2)
            ffn(L, 0, 2, U_MIX_B)
        act.wait_ge(pre_loaded, 16 * (6 * DEPTH + 1))

    @block.vector
    def _(dve):
        V = nc.vector

        def flat(w):
            return w.bitcast(F32)

        def multiplied(L, k):
            dve.wait_ge(unit_done, L.done_units(k))

        def norm_in(L, j):
            s2 = L.sub0 * 2 + 2 * j
            for t in range(TT):
                dve.wait_ge(std_ready, s2 + (t + 1))
                V.reciprocal(rstd_in[:, t:t + 1], std_in[:, t:t + 1]).then_inc(rstd_ready, 1)
                dve.wait_ge(rstd_ready, s2 + (t + 1))
                if t == 0:
                    dve.wait_ge(pre_loaded, L.sub0 * 16 + (16 * j + 16))
                V.scalar_tensor_tensor(xn[:, t, :], x[:, t, :], rstd_in[:, t:t + 1], pre_g[:, :], ALU.mult,
                                       ALU.mult).then_inc(h_ready, 1)
            for t in range(TT):
                for kh in range(2):
                    dve.wait_ge(hT_hi_ready, s2 * 2 + (2 * t + kh + 1))
                    tiles = (slice(None), slice(4 * kh, 4 * kh + 4), slice(t * P, (t + 1) * P))
                    V.tensor_tensor(hT_lo[tiles], ps[:, 2 * t + kh, :].rearrange("p (c n) -> p c n", c=4),
                                    flat(hT_hi[tiles]), ALU.subtract).then_inc(hT_ready, 1)

        def norm_out(L, j):
            s2 = L.sub0 * 2 + 2 * j
            for t in range(TT):
                dve.wait_ge(std_out_ready, s2 + (t + 1))
                V.reciprocal(rstd_out[:, t:t + 1], std_out[:, t:t + 1]).then_inc(rstd_out_ready, 1)
                dve.wait_ge(rstd_out_ready, s2 + (t + 1))
                if t == 0:
                    dve.wait_ge(post_loaded, L.sub0 * 16 + (16 * j + 16))
                V.scalar_tensor_tensor(xn[:, t, :], ps[:, 2 * t:2 * t + 2, :].rearrange("p b n -> p (b n)"),
                                       rstd_out[:, t:t + 1], post_g[:, :], ALU.mult, ALU.mult).then_inc(scaled, 1)
                dve.wait_ge(scaled, s2 + (t + 1))
                V.tensor_tensor(x[:, t, :], x[:, t, :], xn[:, t, :], ALU.add).then_inc(x_ready, 1)

        def ffn(L, n, j, k0):
            f = L.ffn(n)

            def hidden(c):
                dve.wait_ge(silu_ready, f * NCHUNK + (c + 1))
                V.tensor_tensor(hid, sil, ps[:, 4:6, FC:2 * FC], ALU.mult).then_inc(hid_ready, 1)

            def low(c):
                dve.wait_ge(gT_hi_ready, f * NCHUNK + (c + 1))
                V.tensor_tensor(bT_lo[:, KD:KD + 2, :], ps[:, 6, :].rearrange("p (i t) -> p i t", i=2),
                                flat(bT_hi[:, KD:KD + 2, :]), ALU.subtract).then_inc(gT_ready, 1)

            hidden(0)
            low(0)
            hidden(1)
            with dve.Fori(2, NCHUNK) as c:
                low(c - 1)
                hidden(c)
            low(NCHUNK - 1)
            norm_out(L, j)

        def two(bank):
            return ps[:, bank:bank + 2, :].rearrange("p b (c t) -> p (b c) t", c=2)

        def gla_rank_rows(L, k):
            l = L.l
            multiplied(L, k)
            V.tensor_copy(lr_rows, ps[:, 6, 0:2 * RANK].rearrange("p (t r) -> p t r", t=TT)).then_inc(*done("gla_rank", "rows"))

        def gla_rank_turned(l):
            dve.wait_ge(*after("gla_rank_turned", "turned", l))
            V.tensor_copy(lrT[0:RANK, :], ps[0:RANK, 6, P:P + T]).then_inc(*done("gla_rank", "turned"))

        def gla_keep(l):
            dve.wait_ge(*after("gla_soft", "abs", l))
            V.tensor_scalar(nla, ps[:, 7, :], -1.0, 0.0, ALU.mult, ALU.max).then_inc(*done("gla_keep", "max"))
            dve.wait_ge(*after("gla_keep", "max", l))
            dve.wait_ge(*after("gla_soft", "ln", l))
            V.tensor_tensor(nla, nla, gdec, ALU.add).then_inc(*done("gla_keep", "softplus"))

        def gla_keys(l):
            dve.wait_ge(*after("gla_turned", "q", l))
            V.tensor_copy(gqT, ps[:, 6, :].rearrange("p (c t) -> p c t", c=2)).then_inc(*done("gla_decay", "q"))
            dve.wait_ge(*after("gla_exp", "to_end", l))
            dve.wait_ge(*after("gla_in", "qk", l))
            g = gdec.rearrange("p (t n) -> p t n", t=TT)
            V.tensor_tensor(g, g, gqk[:, :, 256:512], ALU.mult).then_inc(*done("gla_decay", "keys"))

        def gla_states(l):
            dve.wait_ge(*after("gla_updates", "updates", l))
            dve.wait_ge(*after("gla_exp", "chunk", l))
            for n in range(4):
                for c in range(2):
                    t, half = n // 2, n % 2
                    update = ps[:, 6 + half, (2 * c + t) * P:(2 * c + t + 1) * P]
                    step = "last" if (n, c) == (3, 1) else f"n{n}c{c}"
                    if n == 0:
                        V.tensor_copy(gstate[:, c, n, :], update).then_inc(*done("gla_state", step))
                    else:
                        dve.wait_ge(*after("gla_state", f"n{n - 1}c{c}", l))
                        V.scalar_tensor_tensor(gstate[:, c, n, :], gstate[:, c, n - 1, :], lam[:, c, n:n + 1], update,
                                               ALU.mult, ALU.add).then_inc(*done("gla_state", step))

        def gla_rows(l):
            dve.wait_ge(*after("gla_reads", "reads", l))
            o = go_f.rearrange("p (t c e v) -> p t c e v", t=TT, c=2, e=2)
            for e in range(2):
                V.tensor_scalar(o[:, :, :, e, :], ps[:, 4 + e, :].rearrange("p (t c v) -> p t c v", t=TT, c=2), 0.125, None,
                                ALU.mult).then_inc(*done("gla_out", "rows" if e else "rows_even"))
            dve.wait_ge(*after("gla_out", "rows", l))
            V.tensor_tensor(gsq_f, go_f, go_f, ALU.mult).then_inc(*done("gla_out", "squares"))
            dve.wait_ge(*after("gla_out", "squares", l))
            V.tensor_reduce(ssg, gsq_f.rearrange("p (h v) -> p h v", h=8), AX.X, ALU.add).then_inc(*done("gla_out", "sums"))

        def gla_gated(l):
            dve.wait_ge(*after("gla_std", "std", l))
            V.reciprocal(rstdg, stdg).then_inc(*done("gla_out", "rstd"))
            dve.wait_ge(*after("gla_in", "r", l))
            V.tensor_tensor(go_f, go_f, gr_f, ALU.mult).then_inc(*done("gla_out", "with_r"))
            dve.wait_ge(*after("gla_out", "with_r", l))
            o = go_f.rearrange("p (h v) -> p h v", h=8)
            V.tensor_tensor(o, o, rstdg.unsqueeze(2).broadcast_to([P, 8, P]), ALU.mult).then_inc(*done("gla_out", "gated"))

        def gla_low(l):
            for c in range(4):
                dve.wait_ge(*after("gla_out_high", f"out{c | 1}", l))
                V.scalar_tensor_tensor(bT_lo[:, c, :], two(6)[:, c, :], packed(PACK_A, "gla_g")[:, c:c + 1],
                                       flat(bT_hi[:, c, :]), ALU.mult, ALU.subtract).then_inc(
                    *done("gla_out_low", "out" if c == 3 else f"out{c}"))

        def conv_glu(l):
            dve.wait_ge(*after("conv_in", "g", l))
            V.tensor_tensor(conv_u, conv_u, conv_s, ALU.mult).then_inc(*done("conv_glu", "glu"))

        def conv_in(l):
            dve.wait_ge(*after("conv_turned", "u", l))
            V.tensor_copy(uT[:, :, CPAD:CPAD + T], two(6)).then_inc(*done("conv_glu", "u"))
            dve.wait_ge(*after("conv_glu", "u", l))

        def conv_taps(l, first, last):
            w = packed(PACK_A, "conv_w").rearrange("p (c w) -> p c w", c=4)
            for i in range(first, min(last, CW - 1) + 1):
                for c in range(4):
                    src = uT[:, c, i:i + T]
                    if i == 0:
                        V.tensor_scalar(conv_y[:, c, :], src, w[:, c, 0:1], packed(PACK_A, "conv_b")[:, c:c + 1], ALU.mult,
                                        ALU.add).then_inc(*done("conv_taps", f"tap0_{c}"))
                    else:
                        dve.wait_ge(*after("conv_taps", f"tap{i - 1}_{c}", l))
                        V.scalar_tensor_tensor(conv_y[:, c, :], src, w[:, c, i:i + 1], conv_y[:, c, :], ALU.mult,
                                               ALU.add).then_inc(*done("conv_taps", f"tap{i}_{c}"))

        def conv_centre(l):
            dve.wait_ge(*after("conv_rows", "rows", l))
            V.tensor_reduce(cmu, ps[:, 6:8, :], AX.X, ALU.add).then_inc(*done("conv_norm", "sums"))
            dve.wait_ge(*after("conv_norm", "sums", l))
            V.tensor_scalar(cmu, cmu, 1.0 / BW, None, ALU.mult).then_inc(*done("conv_norm", "means"))
            dve.wait_ge(*after("conv_norm", "means", l))
            for t in range(TT):
                V.tensor_scalar(conv_n[:, t, :], ps[:, 6 + t, :], cmu[:, t:t + 1], None,
                                ALU.subtract).then_inc(*done("conv_norm", f"centred{t}"))

        def conv_normed(l):
            for t in range(TT):
                dve.wait_ge(*after("conv_std", f"std{t}", l))
                V.reciprocal(crstd[:, t:t + 1], cstd[:, t:t + 1]).then_inc(*done("conv_norm", f"rstd{t}"))
                dve.wait_ge(*after("conv_norm", f"rstd{t}", l))
                V.tensor_scalar(conv_n[:, t, :], conv_n[:, t, :], crstd[:, t:t + 1], None,
                                ALU.mult).then_inc(*done("conv_norm", f"normed{t}"))

        def conv_low(l):
            dve.wait_ge(*after("conv_out", "high", l))
            V.tensor_tensor(bT_lo[:, 0:4, :], conv_y, flat(bT_hi[:, 0:4, :]), ALU.subtract).then_inc(*done("conv_out_low", "out"))

        def diagonal(w):
            return w.rearrange("p (e b n) -> p e b n", e=2, b=3)[:, :, 0::2, :]

        def mask(name):
            return konst(name).unsqueeze(1).unsqueeze(1).broadcast_to([P, 2, 2, P])

        def sb_keep(l, c):
            dve.wait_ge(*after("sb_weights", f"ln{c}", l))
            V.scalar_tensor_tensor(sb_sp, sb_z, 0.0, sb_e, ALU.max, ALU.add).then_inc(*done("sb_keep", f"softplus{c}"))
            dve.wait_ge(*after("sb_keep", f"softplus{c}", l))
            V.tensor_tensor(diagonal(sb_sp), diagonal(sb_sp), mask("sb_keep"), ALU.mult).then_inc(*done("sb_keep", f"masked{c}"))
            V.tensor_tensor(diagonal(sb_z), diagonal(sb_z), mask("sb_neg"), ALU.add).then_inc(*done("sb_keep", f"barred{c}"))

        def sb_exponent(l, c):
            dve.wait_ge(*after("sb_sums", f"sums{c}", l))
            dve.wait_ge(*after("sb_keep", f"barred{c}", l))
            z = sb_z.rearrange("p (e n) -> p e n", e=2)
            V.tensor_tensor(z, z, ps[:, 6:8, 0:384], ALU.subtract).then_inc(*done("sb_keep", f"exponent{c}"))

        def sb_low(l, c):
            dve.wait_ge(*after("sb_out_high", f"out{c}", l))
            tiles = lambda w: w[:, 4 + c, :].rearrange("p (t n) -> p t n", t=TT)
            V.tensor_tensor(tiles(bT_lo), ps[:, 4:6, 384:512], flat(tiles(bT_hi)),
                            ALU.subtract).then_inc(*done("sb_out_low", f"out{c}"))

        def merge(L, k, i, half):
            l = L.l
            multiplied(L, k)
            dve.wait_ge(*after("gates", f"gate{i}_{half}", l))
            out_, rows = merged[:, :, half * 512:half * 512 + 512], sg[:, half, :, :]
            if i == 0:
                V.tensor_tensor(out_, rows, ps[:, 2:4, :], ALU.mult).then_inc(*done("merge", f"branch{i}_{half}"))
                return
            V.tensor_tensor(rows, rows, ps[:, 2:4, :], ALU.mult).then_inc(*done("merge", f"gated{i}_{half}"))
            dve.wait_ge(*after("merge", f"gated{i}_{half}", l))
            V.tensor_tensor(out_, out_, rows, ALU.add).then_inc(*done("merge", f"branch{i}_{half}"))

        def merged_low(l):
            for kh in range(2):
                for t in range(TT):
                    dve.wait_ge(*after("merged_high", f"k{kh}t{t}", l))
                    tiles = (slice(None), slice(4 * kh, 4 * kh + 4), slice(t * P, (t + 1) * P))
                    V.tensor_tensor(hT_lo[tiles], ps[:, 4 + 2 * kh + t, :].rearrange("p (c n) -> p c n", c=4),
                                    flat(hT_hi[tiles]), ALU.subtract).then_inc(*done("merged_low", f"k{kh}t{t}"))

        def mixer_a(L):
            l, k = L.l, U_FFN
            norm_in(L, 1)
            gla_rank_rows(L, k)
            gla_rank_turned(l)
            gla_keep(l)
            gla_keys(l)
            gla_states(l)
            conv_glu(l)
            gla_rows(l)
            gla_gated(l)
            conv_in(l)
            taps = [0]

            def some_taps():
                conv_taps(l, taps[0], taps[0] + 1)
                taps[0] += 2

            for _ in range(2):
                some_taps()
            gla_low(l)
            for _ in range(3):
                some_taps()
            k += 17
            for n in range(18):
                i, m = n // 6, n % 6
                if n % 2 == 0 and 2 <= n <= 8:
                    sb_low(l, n // 2 - 1)
                if n % 2 == 0 and n < 8:
                    sb_keep(l, n // 2)
                if n % 2 == 1 and n < 8:
                    sb_exponent(l, n // 2)
                if n < 11:
                    some_taps()
                if n == 12:
                    conv_centre(l)
                    conv_normed(l)
                if n == 16:
                    conv_low(l)
                if m >= 4:
                    merge(L, k + n, i, m - 4)
            assert taps[0] >= CW
            merged_low(l)
            norm_out(L, 1)

        def memory_rows():
            dve.wait_ge(memory_loaded, 16 * 3)
            for t in range(TT):
                dve.wait_ge(*after("memory_std", f"std{t}", 0))
                V.reciprocal(rstd_in[:, t:t + 1], std_in[:, t:t + 1]).then_inc(*done("memory_rows", f"rstd{t}"))
                dve.wait_ge(*after("memory_rows", f"rstd{t}", 0))
                V.scalar_tensor_tensor(xn[:, t, :], xn[:, t, :], rstd_in[:, t:t + 1], pairbuf, ALU.mult,
                                       ALU.mult).then_inc(*done("memory_rows", f"normed{t}"))
            V.memset(lxT[:, :, 0:PAD2], 0.0).then_inc(*done("memory_rows", "pad"))
            for t in range(TT):
                for kh in range(2):
                    dve.wait_ge(*after("memory_high", f"t{t}k{kh}", 0))
                    tiles = (slice(None), slice(4 * kh, 4 * kh + 4), slice(t * P, (t + 1) * P))
                    V.tensor_tensor(bT_lo[tiles], ps[:, 2 * t + kh, :].rearrange("p (c n) -> p c n", c=4),
                                    flat(bT_hi[tiles]), ALU.subtract).then_inc(*done("memory_low", f"t{t}k{kh}"))

        def rope_angles():
            ANGLE, WHOLE, POS = lru[0][:, 0:64], lru[1][:, 0:64], lru[2][:, 0:2]
            V.tensor_copy(POS, positions).then_inc(*done("rope_angles", "positions"))
            dve.wait_ge(*after("rope_angles", "positions", 0))
            for t in range(TT):
                V.tensor_scalar(ANGLE[:, 32 * t:32 * t + 32], konst("inv_freq"), POS[:, t:t + 1], None,
                                ALU.mult).then_inc(*done("rope_angles", f"angles{t}"))
            dve.wait_ge(*after("rope_angles", f"angles{TT - 1}", 0))
            for name, table, quarter in (("sin", sin, 0.0), ("cos", cos, 0.25)):
                ROUND = 1.5 * 2 ** 23
                steps = [
                    lambda: V.tensor_scalar(WHOLE, ANGLE, 1.0 / (2 * np.pi), quarter, ALU.mult, ALU.add),
                    lambda: V.tensor_scalar(WHOLE, WHOLE, ROUND, None, ALU.add),
                    lambda: V.tensor_scalar(WHOLE, WHOLE, ROUND, None, ALU.subtract),
                    lambda: V.scalar_tensor_tensor(table, WHOLE, -TURN[0], ANGLE, ALU.mult, ALU.add),
                    lambda: V.scalar_tensor_tensor(table, WHOLE, -TURN[1], table, ALU.mult, ALU.add),
                    lambda: V.scalar_tensor_tensor(table, WHOLE, -TURN[2], table, ALU.mult, ALU.add),
                    lambda: V.tensor_scalar(table, table, quarter * 2 * np.pi, PI_BELOW, ALU.add, ALU.min),
                    lambda: V.tensor_scalar(table, table, -PI_BELOW, None, ALU.max)]
                for n, step in enumerate(steps):
                    label = name if n == len(steps) - 1 else f"{name}{n}"
                    step().then_inc(*done("rope_angles", label))
                    dve.wait_ge(*after("rope_angles", label, 0))

        def fox_gate(L):
            l = L.l
            multiplied(L, 0)
            dve.wait_ge(pack_loaded, l * 16 + (16 * DEPTH + 16))
            V.tensor_tensor(flog, ps[:, 6, 0:16].rearrange("p (t h) -> p t h", t=TT),
                            packed(PACK_B, "fox_b").unsqueeze(1).broadcast_to([P, TT, 8]), ALU.add).then_inc(
                *done("fox_gate", "logits"))
            dve.wait_ge(*after("fox_soft", "ln", l))
            z = flog.rearrange("p t h -> p (t h)")
            V.scalar_tensor_tensor(z, z, 0.0, ftmp, ALU.min, ALU.subtract).then_inc(*done("fox_gate", "log"))

        def fox_sums(l):
            dve.wait_ge(*after("fox_decay", "sums", l))
            V.tensor_copy(fcum.rearrange("p t h -> p (t h)"), ps[:, 7, 0:16]).then_inc(*done("fox_gate", "sums"))
            V.tensor_copy(fcT[0:8, :], ps[0:8, 7, 128:384]).then_inc(*done("fox_gate", "rows0"))
            V.tensor_copy(fcT[64:72, :], ps[64:72, 7, 128:384]).then_inc(*done("fox_gate", "rows"))

        def lru_lambda(l):
            e, s, s2, acc = lru_t, lru_c, stat[:, 100:102], stat[:, 102:104]

            def then(ins, step):
                ins.then_inc(*done("lru_lambda", step))
                dve.wait_ge(*after("lru_lambda", step, l))

            then(V.tensor_scalar(lsp, packed(PACK_B, "lam"), -1.0, 0.0, ALU.mult, ALU.max), "max")
            dve.wait_ge(*after("lru_act", "lambda", l))
            then(V.tensor_scalar(s, e, 2.0, None, ALU.add), "two")
            then(V.reciprocal(s, s), "over")
            then(V.tensor_tensor(s, s, e, ALU.mult), "s")
            then(V.tensor_tensor(s2, s, s, ALU.mult), "s2")
            then(V.tensor_scalar(acc, s2, 1.0 / 17, 1.0 / 15, ALU.mult, ALU.add), "term15")
            for n in range(13, 0, -2):
                then(V.tensor_tensor(acc, acc, s2, ALU.mult), f"times{n}")
                then(V.tensor_scalar(acc, acc, 1.0 / n, None, ALU.add), f"term{n}")
            then(V.tensor_tensor(acc, acc, s, ALU.mult), "half")
            then(V.scalar_tensor_tensor(lsp, acc, 2.0, lsp, ALU.mult, ALU.add), "softplus")
            then(V.tensor_scalar(lsp, lsp, -LRU_C, None, ALU.mult), "scaled")

        def lru_conv(l):
            dve.wait_ge(*after("lru_turned", "xy", l))
            V.tensor_copy(lxT[:, :, PAD2:PAD2 + T], two(4)[:, 0:2, :]).then_inc(*done("lru_turn", "x"))
            V.tensor_copy(lyT.rearrange("p (c t) -> p c t", c=2), two(4)[:, 2:4, :]).then_inc(*done("lru_turn", "y"))
            dve.wait_ge(*after("lru_turn", "x", l))
            w = packed(PACK_B, "conv_w").rearrange("p (c w) -> p c w", c=2)
            for i in range(CW2):
                for c in range(2):
                    src, dst = lxT[:, c, i:i + T], lru[0][:, c * T:(c + 1) * T]
                    if i == 0:
                        V.tensor_scalar(dst, src, w[:, c, 0:1], packed(PACK_B, "conv_b")[:, c:c + 1], ALU.mult,
                                        ALU.add).then_inc(*done("lru_conv", f"tap0_{c}"))
                    else:
                        dve.wait_ge(*after("lru_conv", f"tap{i - 1}_{c}", l))
                        V.scalar_tensor_tensor(dst, src, w[:, c, i:i + 1], dst, ALU.mult,
                                               ALU.add).then_inc(*done("lru_conv", f"tap{i}_{c}"))

        def lru_log(l):
            dve.wait_ge(*after("lru_act", "i1", l))
            for c in range(2):
                r = lru[1][:, c * T:(c + 1) * T]
                V.tensor_scalar(r, r, lsp[:, c:c + 1], None, ALU.mult).then_inc(*done("lru_math", f"log{c}"))
            V.tensor_tensor(lru[2], lru[2], lru[0], ALU.mult).then_inc(*done("lru_math", "ix"))

        def lru_square(l):
            dve.wait_ge(*after("lru_act", "tanh", l))
            dve.wait_ge(*after("lru_math", "ix", l))
            V.tensor_scalar(lru[0], lru[3], -1.0, 1.0, ALU.mult, ALU.add).then_inc(*done("lru_math", "less"))
            dve.wait_ge(*after("lru_math", "less", l))
            V.reciprocal(lru[0], lru[0]).then_inc(*done("lru_math", "over"))
            dve.wait_ge(*after("lru_math", "over", l))
            V.scalar_tensor_tensor(lru[3], lru[3], -2.0, lru[0], ALU.mult, ALU.mult).then_inc(*done("lru_math", "square"))

        def lru_scan(l):
            dve.wait_ge(*after("lru_act", "root", l))
            V.tensor_tensor(lru[2], lru[2], lru[3], ALU.mult).then_inc(*done("lru_math", "u"))
            dve.wait_ge(*after("lru_math", "u", l))
            for c in range(2):
                s = slice(c * T, (c + 1) * T)
                V.tensor_tensor_scan(lru[3][:, s], lru[1][:, s], lru[2][:, s], 0.0, ALU.mult,
                                     ALU.add).then_inc(*done("lru_math", f"scan{c}"))
            dve.wait_ge(*after("lru_math", "scan1", l))
            dve.wait_ge(*after("lru_act", "gelu", l))
            V.tensor_tensor(lru[0], lru[3], lyT, ALU.mult).then_inc(*done("lru_math", "out"))

        def lru_low(l):
            dve.wait_ge(*after("lru_act", "high", l))
            V.tensor_tensor(hT_lo[:, 0:2, :], lru[0].rearrange("p (c t) -> p c t", c=2), flat(hT_hi[:, 0:2, :]),
                            ALU.subtract).then_inc(*done("lru_low", "out"))

        def fox_rows(l, g):
            t, n = g // 2, P * (g // 2 + 1)
            dve.wait_ge(*after("fox_logits", f"logits{g}", l))
            if g:
                dve.wait_ge(*after("fox_p_turned", f"turned{g - 1}", l))
            for i in range(2):
                for e in range(2):
                    b, h = 2 * i + e, 2 * (2 * (g % 2) + i) + e
                    src, decay = ps[:, 6 + e, i * T:i * T + n], fcum[:, t, h:h + 1]
                    label = f"rows{g}" if b == 3 else f"rows{g}_{b}"
                    if t:
                        V.tensor_scalar(fl[:, b, 0:P], src[:, 0:P], decay, None, ALU.add).then_inc(
                            *done("fox_rows", f"early{g}_{b}"))
                    V.scalar_tensor_tensor(fl[:, b, t * P:n], src[:, t * P:n], decay, konst("fox_neg"), ALU.add,
                                           ALU.add).then_inc(*done("fox_rows", label))
            dve.wait_ge(*after("fox_rows", f"rows{g}", l))
            V.tensor_reduce(fmax, fl[:, :, 0:n], AX.X, ALU.max).then_inc(*done("fox_rows", f"top{g}"))
            dve.wait_ge(*after("fox_rows", f"top{g}", l))
            V.tensor_scalar(fmax, fmax, -1.0, None, ALU.mult).then_inc(*done("fox_rows", f"max{g}"))

        def fox_weights(l, g):
            n = P * (g // 2 + 1)
            dve.wait_ge(*after("fox_exp", f"g{g}h3", l))
            V.reciprocal(frd, fden).then_inc(*done("fox_rows", f"over{g}"))
            dve.wait_ge(*after("fox_rows", f"over{g}", l))
            for b in range(4):
                V.tensor_scalar(fl[:, b, 0:n], fl[:, b, 0:n], frd[:, b:b + 1], None, ALU.mult).then_inc(
                    *done("fox_rows", f"weights{g}" if b == 3 else f"weights{g}_{b}"))

        def fox_low(l, g):
            dve.wait_ge(*after("fox_out_high", f"out{g}", l))
            c, t = 2 + 2 * (g % 2), g // 2
            tiles = (slice(None), slice(c, c + 2), slice(t * P, (t + 1) * P))
            V.tensor_tensor(hT_lo[tiles], ps[:, 4, 0:256].rearrange("p (c t) -> p c t", c=2), flat(hT_hi[tiles]),
                            ALU.subtract).then_inc(*done("fox_out_low", f"out{g}"))

        def ret_rope(l):
            dve.wait_ge(*after("ret_in", "qk", l))
            src = rqk.rearrange("p t (h u f) -> p t h u f", h=8, u=2)
            dst = rope.rearrange("p t (h u f) -> p t h u f", h=8, u=2)
            tmp = rsq_f.rearrange("p (t h f) -> p t h f", t=TT, h=8)
            for t in range(TT):
                wave = {"c": cos[:, 32 * t:32 * t + 32].unsqueeze(1).broadcast_to([P, 8, 32]),
                        "s": sin[:, 32 * t:32 * t + 32].unsqueeze(1).broadcast_to([P, 8, 32])}
                for u, (same, other, op) in enumerate((("c", "s", ALU.subtract), ("c", "s", ALU.add))):
                    V.tensor_tensor(dst[:, t, :, u, :], src[:, t, :, u, :], wave[same], ALU.mult).then_inc(
                        *done("ret_rope", f"same{t}{u}"))
                    if u:
                        dve.wait_ge(*after("ret_rope", f"sum{t}0", l))
                    V.tensor_tensor(tmp[:, t, :, :], src[:, t, :, 1 - u, :], wave[other], ALU.mult).then_inc(
                        *done("ret_rope", f"other{t}{u}"))
                    dve.wait_ge(*after("ret_rope", f"other{t}{u}", l))
                    V.tensor_tensor(dst[:, t, :, u, :], dst[:, t, :, u, :], tmp[:, t, :, :], op).then_inc(
                        *done("ret_rope", "rotated" if t and u else f"sum{t}{u}"))

        def ret_turned(l):
            dve.wait_ge(*after("ret_turned", "qk", l))
            V.tensor_copy(rT, two(6)).then_inc(*done("ret_rope", "qkT"))

        def ret_scores(l, c):
            dve.wait_ge(*after("ret_dots", f"dots{c}", l))
            decay = konst("ret_decay").rearrange("p (h n) -> p h n", h=4)[:, 2 * c:2 * c + 2, :]
            s = ret_s[:, 2 * c:2 * c + 2, :]
            V.tensor_tensor(s[:, :, 0:256], ps[:, 6:8, 0:256], decay, ALU.mult).then_inc(*done("ret_scores", f"first{c}"))
            V.tensor_tensor(s[:, :, 256:384], ps[:, 6:8, 256:384], decay[:, :, 0:P], ALU.mult).then_inc(
                *done("ret_scores", f"scores{c}"))

        def ret_norm(l):
            dve.wait_ge(*after("ret_rows", "rows", l))
            y = ry_f.rearrange("p (h v) -> p h v", h=8)
            V.tensor_reduce(rstat3, ps[:, 6, :].rearrange("p (h v) -> p h v", h=8), AX.X, ALU.add).then_inc(
                *done("ret_norm", "totals"))
            dve.wait_ge(*after("ret_norm", "totals", l))
            V.tensor_scalar(rstat3, rstat3, 1.0 / 64, None, ALU.mult).then_inc(*done("ret_norm", "means"))
            dve.wait_ge(*after("ret_norm", "means", l))
            V.tensor_tensor(y, ps[:, 6, :].rearrange("p (h v) -> p h v", h=8),
                            rstat3.unsqueeze(2).broadcast_to([P, 8, 64]), ALU.subtract).then_inc(*done("ret_norm", "centred"))
            dve.wait_ge(*after("ret_norm", "centred", l))
            V.tensor_tensor(rsq_f, ry_f, ry_f, ALU.mult).then_inc(*done("ret_norm", "squares"))
            dve.wait_ge(*after("ret_norm", "squares", l))
            V.tensor_reduce(rstat, rsq_f.rearrange("p (h v) -> p h v", h=8), AX.X, ALU.add).then_inc(*done("ret_norm", "sums"))

        def ret_gated(l):
            dve.wait_ge(*after("ret_std", "std", l))
            V.reciprocal(rstat3, rstat2).then_inc(*done("ret_norm", "over"))
            dve.wait_ge(*after("ret_in", "g", l))
            V.tensor_tensor(ry_f, ry_f, rg_f, ALU.mult).then_inc(*done("ret_norm", "with_g"))
            dve.wait_ge(*after("ret_norm", "with_g", l))
            y = ry_f.rearrange("p (h v) -> p h v", h=8)
            V.tensor_tensor(y, y, rstat3.unsqueeze(2).broadcast_to([P, 8, 64]), ALU.mult).then_inc(*done("ret_norm", "gated"))

        def ret_low(l):
            dve.wait_ge(*after("ret_out_high", "out", l))
            V.tensor_tensor(hT_lo[:, 6:8, :], ps[:, 6, :].rearrange("p (c t) -> p c t", c=2), flat(hT_hi[:, 6:8, :]),
                            ALU.subtract).then_inc(*done("ret_out_low", "out"))

        def mixer_b(L):
            l = L.l
            norm_in(L, 0)
            fox_gate(L)
            fox_sums(l)
            lru_lambda(l)
            lru_conv(l)
            fox_rows(l, 0)
            fox_weights(l, 0)
            ret_rope(l)
            fox_rows(l, 1)
            lru_log(l)
            ret_turned(l)
            fox_weights(l, 1)
            lru_square(l)
            fox_low(l, 0)
            ret_scores(l, 0)
            ret_scores(l, 1)
            lru_scan(l)
            fox_low(l, 1)
            fox_rows(l, 2)
            fox_weights(l, 2)
            lru_low(l)
            fox_rows(l, 3)
            fox_weights(l, 3)
            fox_low(l, 2)
            ret_norm(l)
            ret_gated(l)
            ret_low(l)
            fox_low(l, 3)
            norm_out(L, 0)

        def cross(L):
            l = L.l
            norm_in(L, 1)
            for t in range(TT):
                dve.wait_ge(*after("cross_logits", f"logits{t}", l))
                m = cmax[:, 4 * t:4 * t + 4]
                V.tensor_reduce(m, ps[:, 2 * t:2 * t + 2, :].rearrange("p b (h n) -> p (b h) n", h=2), AX.X,
                                ALU.max).then_inc(*done("cross_max", f"top{t}"))
                dve.wait_ge(*after("cross_max", f"top{t}", l))
                V.tensor_scalar(m, m, -1.0, None, ALU.mult).then_inc(*done("cross_max", f"max{t}"))
            for t in range(TT):
                dve.wait_ge(*after("cross_exp", f"t{t}h3", l))
                V.reciprocal(crd[:, 4 * t:4 * t + 4], cden[:, 4 * t:4 * t + 4]).then_inc(*done("cross_rows", f"over{t}"))
                dve.wait_ge(*after("cross_rows", f"over{t}", l))
                for h in range(4):
                    V.tensor_scalar(cp[t][:, h, :], cp[t][:, h, :], crd[:, 4 * t + h:4 * t + h + 1], None,
                                    ALU.mult).then_inc(*done("cross_rows", f"weights{t}" if h == 3 else f"weights{t}_{h}"))
            for c in range(4):
                dve.wait_ge(*after("cross_out_high", f"out{c}", l))
                V.tensor_tensor(hT_lo[:, 2 * c:2 * c + 2, :], ps[:, c, :].rearrange("p (c t) -> p c t", c=2),
                                flat(hT_hi[:, 2 * c:2 * c + 2, :]), ALU.subtract).then_inc(*done("cross_out_low", f"out{c}"))
            norm_out(L, 1)

        V.memset(uT[:, :, 0:CPAD], 0.0).then_inc(*done("start", "pad"))
        V.memset(lrT[:, :], 1.0).then_inc(*done("start", "ones"))
        dve.wait_ge(*after("start", "ones", 0))
        dve.wait_ge(start_loaded, 16 * 3)
        V.sem_inc(x_ready, TT)
        with dve.Fori(0, DEPTH) as l:
            L = Layer("A", l)
            norm_in(L, 0)
            ffn(L, 0, 0, 0)
            mixer_a(L)
            norm_in(L, 2)
            ffn(L, 1, 2, U_FFN + U_MIX_A)
        memory_rows()
        rope_angles()
        with dve.Fori(0, DEPTH) as l:
            L = Layer("B", l)
            mixer_b(L)
            cross(L)
            norm_in(L, 2)
            ffn(L, 0, 2, U_MIX_B)

    return S.seen


TURN = (6.28125, 0.0019350051879882812, 2 * np.pi - 6.28125 - 0.0019350051879882812)
PI_BELOW = 3.1415925


_WHOLE = ["x", "ffn1_w_gate", "ffn1_w_up", "ffn1_w_down", "ffn2_w_gate", "ffn2_w_up", "ffn2_w_down", "w_in", "w_branch",
          "w_out", "w_in_2", "w_cq_2", "w_ck_2", "w_cv_2", "w_co_2", "w_out_2", "w_gate_2", "w_up_2", "w_down_2"]


def _layout(inputs):
    get = lambda name: np.ascontiguousarray(np.asarray(inputs[name]))
    arrays = {name: get(name) for name in _WHOLE}
    arrays["w_branch"] = arrays["w_branch"].reshape(DEPTH, 3 * BW, D)
    gains = np.zeros((6 * DEPTH + 1, 2, D), np.float32)
    for l in range(DEPTH):
        for j in range(3):
            gains[3 * l + j, 0], gains[3 * l + j, 1] = get("norm_pre")[l, j], get("norm_post")[l, j]
        for j, name in enumerate(("mix", "cross", "ffn")):
            gains[3 * DEPTH + 3 * l + j, 0] = get(f"pre_{name}_g_2")[l]
            gains[3 * DEPTH + 3 * l + j, 1] = get(f"post_{name}_g_2")[l]
    arrays["gains"] = gains
    arrays["mem"], arrays["mem_g"] = get("mem_2"), get("mem_norm_g_2")[None, :]
    arrays["positions"] = np.ascontiguousarray(get("positions_2").reshape(TT, P).T)
    arrays["const"] = CONST_ARRAY

    def tiles(v):
        v = v.reshape(v.shape[:-1] + (-1, P))
        return np.moveaxis(np.moveaxis(v, -1, 0), -1, 1)

    a = np.zeros((DEPTH, P, PACK_A_W), np.float32)
    b = np.zeros((DEPTH, P, PACK_B_W), np.float32)

    def put(array, table, l, name, value):
        at, w = table[name]
        array[l, :value.shape[0], at:at + w] = value.reshape(value.shape[0], w)

    for l in range(DEPTH):
        put(a, PACK_A, l, "conv_w", tiles(get("conv_w")[l]))
        for name, source in (("conv_b", "conv_b"), ("ln_g", "conv_ln_g"), ("ln_b", "conv_ln_b"), ("gla_g", "gla_norm_g")):
            put(a, PACK_A, l, name, tiles(get(source)[l]))
        put(a, PACK_A, l, "w_alpha", np.concatenate([get("gla_w_alpha")[l], get("gla_b_alpha")[l][None, :]]))
        put(b, PACK_B, l, "conv_w", tiles(get("conv_w_2")[l]))
        for name, source in (("conv_b", "conv_b_2"), ("b_r", "b_rg_2"), ("b_i", "b_ig_2"), ("lam", "lru_lambda_2")):
            put(b, PACK_B, l, name, tiles(get(source)[l]))
        put(b, PACK_B, l, "fox_b", np.repeat(get("fox_b_f_2")[l][None, :], P, axis=0))
        for name, source in (("w_r", "w_rg_2"), ("w_i", "w_ig_2")):
            at, _ = PACK_B[name]
            for n in range(4):
                c, e = n // 2, n % 2
                b[l, 64 * e:64 * e + 64, at + c * P + 64 * e:at + c * P + 64 * e + 64] = get(source)[l, n]
    arrays["pack_a"], arrays["pack_b"] = a, b
    return arrays


def kernel(**inputs):
    import concourse.bacc as _bacc
    from concourse.bass_utils import run_bass_kernel_spmd

    arrays = _layout(inputs)
    counted = None
    for _ in range(2):
        nc = _bacc.Bacc("TRN2", target_bir_lowering=False, num_devices=1)
        d = {name: nc.dram_tensor(f"in_{name}", v.shape, I32 if name == "positions" else F32, kind="ExternalInput").ap()
             for name, v in arrays.items()}
        out = nc.dram_tensor("out", (1, T, D), F32, kind="ExternalOutput").ap()
        counted = build(nc, d, out, counted)
    result = run_bass_kernel_spmd(nc, [{f"in_{name}": v for name, v in arrays.items()}], core_ids=[0])
    return np.asarray(result.results[0]["out"])
```

```python
from contextlib import ExitStack

import numpy as np

import concourse.bass as bass
from concourse import mybir

F32 = mybir.dt.float32
F32R = mybir.dt.float32r
I32 = mybir.dt.int32
ALU = mybir.AluOpType
ACT = mybir.ActivationFunctionType
AX = mybir.AxisListType

P = 128
DEPTH = 2
T = 256
TT = T // P
D = 1024
KD = D // P
F = 2816
FC = 256
NCHUNK = F // FC
RING = 3
AHEAD = 2
EPS = 1e-6
BW = 512
CW = 31
CPAD = CW - 1
GLA_CHUNK = 64
TAU = 16.0
CW2 = 4
PAD2 = CW2 - 1
LRU_C = 8.0
RANK = 16
NEG = -1e30

U_FFN = 3 * NCHUNK
U_MIX_A = 1 + 2 * 8 + 2 * 6 + 6 + 4
U_LAYER_A = 2 * U_FFN + U_MIX_A
U_MIX_B = 1 + 2 * 6 + 8 + 4 + 8
U_LAYER_B = U_MIX_B + U_FFN
assert U_MIX_A % RING == 0 and U_MIX_B % RING == 0 and U_FFN % RING == 0
UNITS = DEPTH * (U_LAYER_A + U_LAYER_B)

A_LR = 4096
A_CHUNKS = {"gla_qk": 2560, "gla_v": 3072, "gla_r": 3584, "conv_a": 1536, "conv_g": 2048,
            "sb_q": 0, "sb_k": 512, "sb_v": 1024}
A_GATES = 4112
A_SECTIONS = (2, 0, 1)
B_FF = 2048
B_CHUNKS = {"fox_q": 512, "fox_k": 1024, "lru_xy": 0, "fox_v": 1536, "ret_qk": 2056, "ret_vg": 2568}

CONST = {}


def _constants():
    i = np.arange(P)
    parts = {
        "ident": np.eye(P),
        "ones": np.ones((P, P)),
        "tri_ge": (i[:, None] >= i[None, :]) * 1.0,
        "tri_le": (i[:, None] <= i[None, :]) * 1.0,
        "sb_keep": (i[:, None] < i[None, :]) * 1.0,
        "sb_neg": np.where(i[:, None] < i[None, :], 0.0, NEG),
        "gla_suffix": ((i[:, None] > i[None, :]) & (i[:, None] // GLA_CHUNK == i[None, :] // GLA_CHUNK)) * 1.0,
        "gla_chunk": (i[:, None] // GLA_CHUNK == np.arange(2)[None, :]) * 1.0,
        "fox_neg": np.where(i[None, :] <= i[:, None], 0.0, NEG),
    }
    log_gamma = np.log1p(-np.exp2(-5.0 - np.arange(4)))
    diff = np.arange(T)[None, :] - i[:, None]
    decay = np.where(diff[:, None, :] >= 0, np.exp(log_gamma[None, :, None] * np.maximum(diff, 0)[:, None, :]), 0.0)
    parts["ret_decay"] = (decay * 64 ** -0.5).reshape(P, 4 * T)
    freq = (np.float32(10000.0) ** (-np.arange(32, dtype=np.float32) / np.float32(32))).astype(np.float32)
    parts["inv_freq"] = np.tile(freq, (P, 1))
    sel = np.zeros((P, 8, P))
    for h in range(8):
        sel[h, h, :] = -1.0
        sel[64 + h, h, :] = -1.0
    parts["fox_pick"] = sel.reshape(P, 8 * P)
    at = 0
    for name, a in parts.items():
        CONST[name] = (at, a.shape[1])
        at += a.shape[1]
    return np.concatenate([a.astype(np.float32) for a in parts.values()], axis=1)


CONST_ARRAY = _constants()

PACK_A = {"conv_w": (0, 4 * CW), "conv_b": (124, 4), "ln_g": (128, 4), "ln_b": (132, 4), "gla_g": (136, 4),
          "w_alpha": (140, 256)}
PACK_A_W = 396
PACK_B = {"conv_w": (0, 8), "conv_b": (8, 2), "b_r": (10, 2), "b_i": (12, 2), "lam": (14, 2), "fox_b": (16, 8),
          "w_r": (24, 256), "w_i": (280, 256)}
PACK_B_W = 536


class Signals:

    def __init__(self, make, counted):
        self.make, self.counted = make, counted
        self.sems, self.seen = {}, {}

    def _sem(self, stage):
        if stage not in self.sems:
            self.sems[stage] = self.make(stage)
        return self.sems[stage]

    def done(self, stage, step):
        steps = self.seen.setdefault(stage, [])
        assert step not in steps, (stage, step)
        steps.append(step)
        return self._sem(stage), 1

    def after(self, stage, step, layer):
        steps = self.counted.get(stage) if self.counted else None
        if steps is None:
            assert not self.counted, stage
            return self._sem(stage), layer + 1
        return self._sem(stage), layer * len(steps) + steps.index(step) + 1


def build(nc, d, out, counted):
    with ExitStack() as ctx:
        return _program(ctx, nc, d, out, counted)


def _program(ctx, nc, d, out, counted):
    def sb(name, shape, dt=F32):
        return ctx.enter_context(nc.sbuf_tensor(name, shape, dt))

    def sem(name):
        return ctx.enter_context(nc.semaphore(name))

    S = Signals(sem, counted)
    done, after = S.done, S.after

    ps = ctx.enter_context(nc.psum_tensor("ps", [P, 8, 512], F32))
    x = sb("x", [P, TT, D])
    raw = sb("raw", [P, RING, 2048])
    w_hi = sb("w_hi", [P, RING, 2048], F32R)
    w_lo = sb("w_lo", [P, RING, 2048], F32R)
    hT_hi = sb("hT_hi", [P, KD, T], F32R)
    hT_lo = sb("hT_lo", [P, KD, T], F32R)
    bT_hi = sb("bT_hi", [P, KD + 2, T], F32R)
    bT_lo = sb("bT_lo", [P, KD + 2, T], F32R)
    pre_g = sb("pre_g", [P, D])
    post_g = sb("post_g", [P, D])
    rope_tables = sb("rope_tables", [P, TT * 64])
    const = sb("const", [P, CONST_ARRAY.shape[1]])
    pack = sb("pack", [P, max(PACK_A_W, PACK_B_W)])
    stat = sb("stat", [P, 128])
    SCRATCH = 17200
    scratch = sb("scratch", [P, SCRATCH])

    def konst(name):
        at, w = CONST[name]
        return const[:, at:at + w]

    ident = konst("ident")

    def packed(table, name):
        at, w = table[name]
        return pack[:, at:at + w]

    stat_at = [0]

    def column(n):
        stat_at[0] += n
        return stat[:, stat_at[0] - n:stat_at[0]]

    ss_in, std_in, rstd_in = column(TT), column(TT), column(TT)
    ss_out, bias_out, std_out, rstd_out = column(2 * TT), column(TT), column(TT), column(TT)
    ss_mem, std_mem, rstd_mem = column(TT), column(TT), column(TT)
    root_warm = column(1)

    class Carve:

        def __init__(self, at):
            self.at = at

        def __call__(self, n):
            self.at += n
            assert self.at <= SCRATCH, self.at
            return scratch[:, self.at - n:self.at]

    shared = Carve(0)
    wide = shared(2048)
    xn = wide.rearrange("p (t n) -> p t n", t=TT)
    pairbuf = shared(1024)
    sil = pairbuf[:, 0:512].rearrange("p (t n) -> p t n", t=TT)
    hid = pairbuf[:, 512:1024].rearrange("p (t n) -> p t n", t=TT)

    a_mem = Carve(shared.at)
    gqk_f, gv_f, gr_f, gqT_f = a_mem(1024), a_mem(1024), a_mem(1024), a_mem(512)
    gqk = gqk_f.rearrange("p (t n) -> p t n", t=TT)
    gv = gv_f.rearrange("p (t n) -> p t n", t=TT)
    gr = gr_f.rearrange("p (t n) -> p t n", t=TT)
    gqT = gqT_f.rearrange("p (c t) -> p c t", c=2)
    sbqT = gqk_f.rearrange("p (c t) -> p c t", c=4)
    sbkT = gv_f.rearrange("p (c t) -> p c t", c=4)
    sbv = gr
    uT = a_mem(4 * (T + CPAD)).rearrange("p (c t) -> p c t", c=4)
    conv_y_f = a_mem(1024)
    conv_y = conv_y_f.rearrange("p (c t) -> p c t", c=4)
    sb_sp = a_mem(768)
    sg = a_mem(2048).rearrange("p (h t n) -> p h t n", h=2, t=TT)
    merged_f = a_mem(2048)
    merged = merged_f.rearrange("p (t n) -> p t n", t=TT)
    lr_rows = a_mem(32).rearrange("p (t r) -> p t r", t=TT)
    lrT = a_mem(256)
    lam = a_mem(8).rearrange("p (c n) -> p c n", c=2)
    nla, gdec = pairbuf[:, 0:512], pairbuf[:, 512:1024]
    gstate = sg[:, 0, :, :].rearrange("p t n -> p (t n)").rearrange("p (c n v) -> p c n v", c=2, n=4)
    go_f, gsq_f = merged_f[:, 0:1024], merged_f[:, 1024:2048]
    conv_u = wide[:, 0:1024].rearrange("p (t n) -> p t n", t=TT)
    conv_s = wide[:, 1024:2048].rearrange("p (t n) -> p t n", t=TT)
    sb_q, sb_k = conv_u, conv_s
    sb_z, sb_e = wide[:, 0:768], wide[:, 768:1536]
    conv_n = pairbuf.rearrange("p (t n) -> p t n", t=TT)
    ssg, stdg, rstdg = column(8), column(8), column(8)
    cmu, css, cstd, crstd = column(TT), column(TT), column(TT), column(TT)

    b_mem = Carve(shared.at)
    fqk_f = b_mem(2048)
    fq = fqk_f[:, 0:1024].rearrange("p (t n) -> p t n", t=TT)
    fk = fqk_f[:, 1024:2048].rearrange("p (t n) -> p t n", t=TT)
    rqk = fq
    rope = fk
    ret_s = fqk_f.rearrange("p (h n) -> p h n", h=4)
    fqkT_f = b_mem(2048)
    fqT = fqkT_f[:, 0:1024].rearrange("p (c t) -> p c t", c=4)
    fkT = fqkT_f[:, 1024:2048].rearrange("p (c t) -> p c t", c=4)
    kmT = fqkT_f.rearrange("p (c m) -> p c m", c=KD)
    fvrT_f = b_mem(2048)
    fv_f, rT_f = fvrT_f[:, 0:1024], fvrT_f[:, 1024:2048]
    fv = fv_f.rearrange("p (t n) -> p t n", t=TT)
    rT = rT_f.rearrange("p (c t) -> p c t", c=4)
    rv_f, rg_f = b_mem(512), b_mem(512)
    rv = rv_f.rearrange("p (t n) -> p t n", t=TT)
    rg = rg_f.rearrange("p (t n) -> p t n", t=TT)
    fl_f = b_mem(1024)
    fl = fl_f.rearrange("p (h s) -> p h s", h=4)
    fpT_f = b_mem(1024)
    fpT = fpT_f.rearrange("p (b t) -> p b t", b=8)
    vm = b_mem(2048).rearrange("p (m n) -> p m n", m=TT)
    lxT = b_mem(2 * (T + PAD2)).rearrange("p (c t) -> p c t", c=2)
    lyT = b_mem(512)
    flog, fcum = b_mem(16).rearrange("p (t h) -> p t h", t=TT), b_mem(16).rearrange("p (t h) -> p t h", t=TT)
    ftmp = b_mem(16)
    fcT = b_mem(256)
    sin, cos = rope_tables[:, 0:64], rope_tables[:, 64:128]
    lru_c, lru_t, lsp = column(2), column(2), column(2)
    fmax, fden, frd = column(4), column(4), column(4)
    rstat, rstat2, rstat3 = column(8), column(8), column(8)
    lxy = pairbuf.rearrange("p (t n) -> p t n", t=TT)
    ry_f, rsq_f = pairbuf[:, 0:512], pairbuf[:, 512:1024]
    lru = [wide[:, 512 * n:512 * n + 512] for n in range(4)]
    km = xn
    cq = xn
    cqT = fqk_f.rearrange("p (c t) -> p c t", c=KD)
    cp = [fl_f.rearrange("p (h m) -> p h m", h=4), fpT_f.rearrange("p (h m) -> p h m", h=4)]
    cpT = fvrT_f.rearrange("p (b t) -> p b t", b=8)
    cmax, cden, crd = column(8), column(8), column(8)

    both_a, both_b = gr_f, fl_f
    x_pre = fqk_f.rearrange("p (t n) -> p t n", t=TT)
    out_a = sg.rearrange("p h t n -> p (h t n)").rearrange("p (t n) -> p t n", t=TT)
    out_b = fvrT_f.rearrange("p (t n) -> p t n", t=TT)
    mem_rows, mem_g, mem_sq = merged, conv_y_f, gr_f
    positions = ctx.enter_context(nc.sbuf_tensor("positions", [P, TT], I32))[:, :]

    raw_landed = [sem(f"raw_landed{i}") for i in range(RING)]
    high_ready, low_ready, unit_done = sem("high_ready"), sem("low_ready"), sem("unit_done")
    pre_loaded, post_loaded, pack_loaded = sem("pre_gain_loaded"), sem("post_gain_loaded"), sem("pack_loaded")
    ident_loaded, x_loaded = sem("ident_loaded"), [sem(f"x_loaded{t}") for t in range(TT)]
    x_ready, sq_in, std_ready, rstd_ready = sem("x_ready"), sem("sq_in"), sem("std_ready"), sem("rstd_ready")
    h_ready, h_turned, hT_hi_ready, hT_ready = sem("h_ready"), sem("h_turned"), sem("hT_hi_ready"), sem("hT_ready")
    sq_out, sq_bias, std_out_ready, rstd_out_ready = sem("sq_out"), sem("sq_bias"), sem("std_out"), sem("rstd_out")
    out_copied, prepared, weighted, scaled = sem("out_copied"), sem("prepared"), sem("out_weighted"), sem("out_scaled")
    ffn_out, root_loaded, const_loaded = sem("ffn_out"), sem("root_loaded"), sem("const_loaded")
    silu_ready, hid_ready, hid_turned = sem("silu_ready"), sem("hid_ready"), sem("hid_turned")
    gT_hi_ready, gT_ready = sem("gT_hi_ready"), sem("gT_ready")
    stored, memory_loaded = sem("stored"), sem("memory_loaded")
    raw_free, gla_free = sem("raw_free"), sem("gla_free")

    CREDIT = RING

    class Layer:

        def __init__(self, block, l):
            self.l = l
            self.b = block == "B"
            self.unit0 = l * U_LAYER_B + DEPTH * U_LAYER_A if self.b else l * U_LAYER_A
            self.turn0 = l * (U_LAYER_B // RING) + DEPTH * U_LAYER_A // RING if self.b else l * (U_LAYER_A // RING)
            self.sub0 = l * 3 + 3 * DEPTH if self.b else l * 3

        def done_units(self, k):
            return self.unit0 + (k + 1 + CREDIT)

        def turn(self, k):
            return self.turn0 + (k // RING + 1)

        def ffn(self, n):
            return self.l + 2 * DEPTH if self.b else self.l * 2 + n

        def sub(self, j, per, n):
            return self.sub0 * per + (per * j + n)

    class Chunk(Layer):

        def __init__(self, L, c):
            self.l, self.b, self.sub0 = L.l, L.b, L.sub0
            self.unit0 = L.unit0 + (c - 2) * RING
            self.turn0 = L.turn0 + (c - 2)

    block = ctx.enter_context(nc.Block())

    @block.sync
    def _(sp):
        def unit(L, k, halves):
            sp.wait_ge(low_ready, L.unit0 + (k + 1))
            sp.sem_inc(raw_free, 1)
            for dst, src in halves:
                sp.dma_start(dst, src).then_inc(raw_landed[k % RING], 16)

        def rows(w, l, k0, n, c0, width):
            return w[bass.ds(l, 1), k0:k0 + n * P, c0:c0 + width].rearrange("o (k p) n -> p (o k) n", p=P)

        def square(L, k, w, k0, c0):
            dst = raw[:, k % RING, :].rearrange("p (k n) -> p k n", k=4)
            unit(L, k, [(dst[:, 2 * i:2 * i + 2, :], rows(w, L.l, k0 + 2 * P * i, 2, c0, 512)) for i in range(2)])

        def narrow(L, k, w, c0, width):
            dst = raw[:, k % RING, 0:KD * width].rearrange("p (k n) -> p k n", k=KD)
            unit(L, k, [(dst[:, 4 * i:4 * i + 4, :], rows(w, L.l, 512 * i, 4, c0, width)) for i in range(2)])

        def gate_up(L, k, kh, wg, wu, c):
            dst = raw[:, k % RING, :].rearrange("p (k g n) -> p k g n", k=4, g=2)
            halves = []
            for g, w in enumerate((wg, wu)):
                src = w[bass.ds(L.l, 1), 512 * kh:512 * kh + 512, bass.ds(c * FC, FC)]
                halves.append((dst[:, :, g, :], src.rearrange("o (k p) n -> p (o k) n", p=P)))
            unit(L, k, halves)

        def down(L, k, wd, c):
            dst = raw[:, k % RING, :].rearrange("p (k n) -> p k n", k=2)
            src = wd[bass.ds(L.l, 1), bass.ds(c * FC, FC), :].rearrange("o (k p) n -> p (o k) n", p=P)
            unit(L, k, [(dst[:, i:i + 1, :], src[:, i:i + 1, :]) for i in range(2)])

        def ffn(L, k0, wg, wu, wd):
            for kh in range(2):
                gate_up(L, k0 + kh, kh, wg, wu, 0)

            def chunk(c, k, L=L):
                gate_up(L, k, 0, wg, wu, c)
                gate_up(L, k + 1, 1, wg, wu, c)
                down(L, k + 2, wd, c - 1)

            chunk(1, k0 + 2)
            with sp.Fori(2, NCHUNK - 1) as c:
                chunk(c, k0 + 5, Chunk(L, c))
            chunk(NCHUNK - 1, k0 + U_FFN - 4)
            down(L, k0 + U_FFN - 1, wd, NCHUNK - 1)

        sp.dma_start(const[:, 0:P], d["const"][:, 0:P]).then_inc(ident_loaded, 16)
        with sp.Fori(0, DEPTH) as l:
            L = Layer("A", l)
            ffn(L, 0, d["ffn1_w_gate"], d["ffn1_w_up"], d["ffn1_w_down"])
            k = U_FFN
            for n, c0 in enumerate(A_CHUNKS.values()):
                for kh in range(2):
                    square(L, k, d["w_in"], 512 * kh, c0)
                    k += 1
                    if (n, kh) == (0, 0):
                        narrow(L, k, d["w_in"], A_LR, RANK)
                        k += 1
            for b in A_SECTIONS:
                for half in range(2):
                    for kh in range(2):
                        square(L, k, d["w_in"], 512 * kh, A_GATES + b * D + 512 * half)
                        k += 1
                for half in range(2):
                    square(L, k, d["w_branch"], b * BW, 512 * half)
                    k += 1
            for kh in range(2):
                for half in range(2):
                    square(L, k, d["w_out"], 512 * kh, 512 * half)
                    k += 1
            assert k == U_FFN + U_MIX_A
            ffn(L, k, d["ffn2_w_gate"], d["ffn2_w_up"], d["ffn2_w_down"])
        with sp.Fori(0, DEPTH) as l:
            L = Layer("B", l)
            k = 0
            for n, c0 in enumerate(B_CHUNKS.values()):
                for kh in range(2):
                    square(L, k, d["w_in_2"], 512 * kh, c0)
                    k += 1
                    if (n, kh) == (0, 0):
                        narrow(L, k, d["w_in_2"], B_FF, 8)
                        k += 1
            for name in ("w_cv_2", "w_ck_2"):
                for half in range(2):
                    for kh in range(2):
                        square(L, k, d[name], 512 * kh, 512 * half)
                        k += 1
            for name in ("w_out_2", "w_cq_2", "w_co_2"):
                for kh in range(2):
                    for half in range(2):
                        square(L, k, d[name], 512 * kh, 512 * half)
                        k += 1
            assert k == U_MIX_B
            ffn(L, k, d["w_gate_2"], d["w_up_2"], d["w_down_2"])
        last = Layer("B", DEPTH)
        for k in range(AHEAD):
            dst = raw[:, k, :].rearrange("p (k n) -> p k n", k=4)
            src = d["w_co_2"][DEPTH - 1, 0:512, 512 * k:512 * k + 512].rearrange("(k p) n -> p k n", p=P)
            unit(last, k, [(dst[:, 2 * i:2 * i + 2, :], src[:, 2 * i:2 * i + 2, :]) for i in range(2)])
        for t in range(TT):
            sp.wait_ge(x_ready, 2 * 6 * DEPTH + t + 1)
            sp.dma_start(out[0, t * P:(t + 1) * P, :], x[:, t, :]).then_inc(stored, 16)
        sp.wait_ge(stored, 16 * TT)

    @block.gpsimd
    def _(pool):
        nc.gpsimd.sem_inc(low_ready, CREDIT)
        total = UNITS + AHEAD

        def low(slot, u):
            pool.wait_ge(high_ready, u + 1)
            nc.gpsimd.tensor_tensor(w_lo[:, slot, :], raw[:, slot, :], w_hi[:, slot, :].bitcast(F32),
                                    ALU.subtract).then_inc(low_ready, 1)

        with pool.Fori(0, total // RING) as r:
            for slot in range(RING):
                low(slot, r * RING + slot)
        for slot in range(total % RING):
            low(slot, total - total % RING + slot)

    @block.tensor
    def _(pe):
        def products(left, tiles, slot, view, bank, start, stop, before=None, halves=1, mark=None):
            hi, lo = left
            parts = [view(w[:, slot, :]) for w in (w_hi, w_lo)]
            passes = ((hi, 0), (hi, 1), (lo, 0))
            for t in range(TT):
                for half in range(halves):
                    for i, k in enumerate(tiles):
                        if before and half == 0:
                            before(t, i)
                        for n, (act, part) in enumerate(passes):
                            w = parts[part][:, i, :]
                            if halves > 1:
                                w = w[:, 512 * half:512 * half + 512]
                            mm = nc.tensor.matmul(bank(t, half), act[:, k, t * P:(t + 1) * P], w,
                                                  start=start and i == 0 and n == 0,
                                                  stop=stop and i == len(tiles) - 1 and n == 2)
                    if mark and (t, half) != (TT - 1, halves - 1):
                        mm.then_inc(*mark(t))
            return mm

        def weights(L, k):
            pe.wait_ge(low_ready, L.done_units(k))

        by4 = lambda w: w.rearrange("p (k n) -> p k n", k=4)
        by2 = lambda w: w.rearrange("p (k n) -> p k n", k=2)
        hT, bT = (hT_hi, hT_lo), (bT_hi, bT_lo)

        def first(wait):
            return lambda t, i: wait(t) if i == 0 else None

        def left_ready(L, j, kh):
            return first(lambda t: pe.wait_ge(hT_ready, L.sub(j, 4, 2 * t + kh + 1)))

        def rows_follow(L, j):
            def before(t, i):
                if (t, i) in ((0, 2), (1, 0)):
                    norm_turn(L, j, 1, t)
                left_ready(L, j, 0)(t, i)
            return before

        def square(L, k, left, first, bank, start, stop, before=None, mark=None):
            weights(L, k)
            products(left, range(first, first + 4), k % RING, by4, bank, start, stop, before, 1,
                     mark).then_inc(unit_done, 1)

        def norm_turn(L, j, t, kh):
            pe.wait_ge(h_ready, L.sub(j, 4, 2 * t + kh + 1))
            for c in range(4):
                mm = nc.tensor.transpose(ps[:, 6 - 2 * t + kh, c * P:(c + 1) * P],
                                         xn[:, t, (4 * kh + c) * P:(4 * kh + c + 1) * P], ident)
            mm.then_inc(h_turned, 1)

        def rows_lead(L, j):
            for kh in range(2):
                norm_turn(L, j, 0, kh)

        def banks_free(L, j, t):
            pe.wait_ge(out_copied, L.sub(j, 2, t + 1))

        def turn(src, banks, blocks=4):
            for c in range(blocks):
                for t in range(TT):
                    at = (c % 2) * T + t * P
                    mm = nc.tensor.transpose(ps[:, banks + c // 2, at:at + P], src[:, t, c * P:(c + 1) * P], ident)
            return mm

        def ffn(L, n, j, k0):
            f = L.ffn(n)
            mid = lambda t, half: ps[:, 6 + t, :]
            acc = lambda t, half: ps[:, 2 * t + half, :]

            def gate_up(M, k):
                for kh in range(2):
                    square(M, k + kh, hT, 4 * kh, mid, kh == 0, kh == 1)

            def hidden(c):
                pe.wait_ge(hid_ready, f * NCHUNK + (c + 1))
                for i in range(2):
                    for t in range(TT):
                        mm = nc.tensor.transpose(ps[:, 4, i * T + t * P:i * T + (t + 1) * P],
                                                 hid[:, t, i * P:(i + 1) * P], ident)
                mm.then_inc(hid_turned, 1)

            def down(M, k, c, start, before=None, left=bT, tiles=(KD, KD + 1), mark=None):
                weights(M, k)
                pe.wait_ge(gT_ready, f * NCHUNK + (c + 1))
                products(left, tiles, k % RING, by2, acc, start, mark is not None, before, 2, mark).then_inc(unit_done, 1)

            square(L, k0, hT, 0, mid, True, False, rows_follow(L, j))
            square(L, k0 + 1, hT, 4, mid, False, True, left_ready(L, j, 1))
            hidden(0)
            if n:
                square(L, k0 + 2, hT, 0, mid, True, False)
                for t in range(TT):
                    banks_free(L, j, t)
                memory_turn(L.l)
                square(L, k0 + 3, hT, 4, mid, False, True)
                pe.wait_ge(*after("memory_low", "t1k1", L.l))
            else:
                gate_up(L, k0 + 2)
                for t in range(TT):
                    banks_free(L, j, t)
            down(L, k0 + 4, 0, True)
            with pe.Fori(2, NCHUNK - 1) as c:
                M = Chunk(L, c)
                hidden(c - 1)
                gate_up(M, k0 + 5)
                down(M, k0 + 7, c - 1, False)
            end, c = k0 + U_FFN - 1, NCHUNK - 1
            hidden(c - 1)
            gate_up(L, end - 3)
            down(L, end - 1, c - 1, False, first(lambda t: hidden(c) if t else None))
            down(L, end, c, False, None, hT, (0, 1), lambda t: (ffn_out, 1))
            rows_lead(L, j + 1)

        def pair(n):
            return lambda t, half: ps[:, 2 * (n % 2) + t, :]

        def narrow(L, k, width, j):
            weights(L, k)
            view = lambda w: w[:, 0:KD * width].rearrange("p (k n) -> p k n", k=KD)

            products(hT, range(KD), k % RING, view, lambda t, half: ps[:, 6, t * width:(t + 1) * width], True, True,
                     left_ready(L, j, 1)).then_inc(unit_done, 1)

        def gla_rank(l):
            pe.wait_ge(*after("gla_rank", "rows", l))
            for t in range(TT):
                mm = nc.tensor.transpose(ps[0:RANK, 6, P + t * P:P + (t + 1) * P], lr_rows[:, t, :], ident)
            mm.then_inc(*done("gla_rank_turned", "turned"))

        def gla_alpha(l):
            pe.wait_ge(const_loaded, 16 * 4)
            pe.wait_ge(*after("gla_rank", "turned", l))
            pe.wait_ge(pack_loaded, l * 16 + 16)
            for t in range(TT):
                mm = nc.tensor.matmul(ps[:, 7, t * T:(t + 1) * T], lrT[0:RANK + 1, t * P:(t + 1) * P],
                                      packed(PACK_A, "w_alpha")[0:RANK + 1, :], start=True, stop=True)
            mm.then_inc(*done("gla_alpha", "logits"))

        def gla_decays(l):
            pe.wait_ge(*after("gla_in", "qk", l))
            for c in range(2):
                for t in range(TT):
                    mm = nc.tensor.transpose(ps[:, 6, c * T + t * P:c * T + (t + 1) * P], gqk[:, t, c * P:(c + 1) * P],
                                             ident)
            mm.then_inc(*done("gla_turned", "q"))
            pe.wait_ge(*after("gla_keep", "softplus", l))
            for t in range(TT):
                nc.tensor.matmul(ps[:, 4, t * T:(t + 1) * T], konst("gla_suffix"), nla[:, t * T:(t + 1) * T],
                                 start=True, stop=True)
            for c in range(2):
                for t in range(TT):
                    mm = nc.tensor.matmul(ps[:, 5, 4 * c + 2 * t:4 * c + 2 * t + 2],
                                          nla[:, t * T + c * P:t * T + (c + 1) * P], konst("gla_chunk"),
                                          start=True, stop=True)
            mm.then_inc(*done("gla_sums", "sums"))

        def gla_updates(l):
            pe.wait_ge(*after("gla_decay", "keys", l))
            pe.wait_ge(*after("gla_in", "v", l))
            pe.wait_ge(*after("gla_decay", "q", l))
            pe.sem_inc(gla_free, 1)
            for half in range(2):
                rows = slice(64 * half, 64 * half + 64)
                for t in range(TT):
                    for c in range(2):
                        for e in range(2):
                            h = 2 * c + e
                            mm = nc.tensor.matmul(
                                ps[64 * e:64 * e + 64, 6 + half, (2 * c + t) * P:(2 * c + t + 1) * P],
                                gdec[rows, t * T + h * 64:t * T + h * 64 + 64], gv[rows, t, h * P:(h + 1) * P],
                                start=True, stop=True)
            mm.then_inc(*done("gla_updates", "updates"))

        def gla_reads(l):
            pe.wait_ge(*after("gla_state", "last", l))
            pe.sem_inc(gla_free, 1)
            for e in range(2):
                rows = slice(64 * e, 64 * e + 64)
                for n in range(4):
                    t, half = n // 2, n % 2
                    for c in range(2):
                        mm = nc.tensor.matmul(
                            ps[64 * half:64 * half + 64, 4 + e, (2 * t + c) * P:(2 * t + c + 1) * P],
                            gqT[rows, c, n * 64:n * 64 + 64], gstate[rows, c, n, :], start=True, stop=True)
            mm.then_inc(*done("gla_reads", "reads"))

        def conv_turn(l):
            pe.wait_ge(*after("conv_glu", "glu", l))
            turn(conv_u, 6).then_inc(*done("conv_turned", "u"))

        def sb_turn_q(l):
            pe.wait_ge(*after("sb_in", "q", l))
            pe.wait_ge(*after("gla_out", "rows", l))
            turn(sb_q, 4).then_inc(*done("sb_turned", "q"))

        def gla_turn(l):
            pe.wait_ge(*after("gla_out", "gated", l))
            pe.wait_ge(*after("conv_glu", "u", l))
            turn(go_f.rearrange("p (t n) -> p t n", t=TT), 6).then_inc(*done("gla_out_turned", "turned"))

        def sb_turn_k(l):
            pe.wait_ge(*after("sb_in", "k", l))
            pe.wait_ge(*after("sb_in", "qT", l))
            turn(sb_k, 4).then_inc(*done("sb_turned", "k"))

        def sb_logits(l, c):
            pe.wait_ge(*after("sb_in", "kT", l))
            if c:
                pe.wait_ge(*after("sb_weights", f"abs{c - 1}", l))
            for e in range(2):
                r = slice(64 * e, 64 * e + 64)
                nc.tensor.matmul(ps[:, 4 + e, 0:256], sbkT[r, c, 0:P], sbqT[r, c, :], start=True, stop=True)
                mm = nc.tensor.matmul(ps[:, 4 + e, 256:384], sbkT[r, c, P:T], sbqT[r, c, P:T], start=True, stop=True)
            mm.then_inc(*done("sb_logits", f"logits{c}"))

        def sb_sums(l, c):
            pe.wait_ge(*after("sb_keep", f"masked{c}", l))
            if c:
                pe.wait_ge(*after("sb_keep", f"exponent{c - 1}", l))
                pe.wait_ge(*after("sb_out_low", f"out{c - 1}", l))
            else:
                pe.wait_ge(*after("gla_out_low", "out", l))
            for e in range(2):
                s = sb_sp[:, e * 384:(e + 1) * 384]
                nc.tensor.matmul(ps[:, 6 + e, 256:384], konst("tri_ge"), s[:, 256:384], start=True, stop=True)
                nc.tensor.matmul(ps[:, 6 + e, 0:256], konst("tri_ge"), s[:, 0:256], start=True, stop=False)
                mm = nc.tensor.matmul(ps[:, 6 + e, P:256], konst("ones"), s[:, 256:384], start=False, stop=True)
            mm.then_inc(*done("sb_sums", f"sums{c}"))

        def sb_out(l, c):
            pe.wait_ge(*after("sb_weights", f"weights{c}", l))
            for e in range(2):
                w = sb_e[:, e * 384:(e + 1) * 384]
                r, h = slice(64 * e, 64 * e + 64), 2 * c + e
                v = sbv[:, :, h * 64:h * 64 + 64]
                nc.tensor.matmul(ps[r, 6, 384:512], v[:, 0, :], w[:, 0:P], start=True, stop=True)
                nc.tensor.matmul(ps[r, 7, 384:512], v[:, 0, :], w[:, P:256], start=True, stop=False)
                mm = nc.tensor.matmul(ps[r, 7, 384:512], v[:, 1, :], w[:, 256:384], start=False, stop=True)
            mm.then_inc(*done("sb_out", f"out{c}"))

        def conv_rows(l):
            pe.wait_ge(*after("conv_taps", f"tap{CW - 1}_3", l))
            pe.wait_ge(*after("sb_out_low", "out3", l))
            for t in range(TT):
                for c in range(4):
                    mm = nc.tensor.transpose(ps[:, 6 + t, c * P:(c + 1) * P], conv_y[:, c, t * P:(t + 1) * P], ident)
            mm.then_inc(*done("conv_rows", "rows"))

        def conv_normed(l):
            pe.wait_ge(*after("conv_norm", "normed1", l))
            pe.wait_ge(*after("sb_weights", "abs3", l))
            turn(conv_n, 4).then_inc(*done("conv_normed", "turned"))

        def merged_turn(l, kh):
            if kh == 0:
                pe.wait_ge(*after("conv_out", "act3", l))
            pe.wait_ge(*after("merge", f"branch2_{kh}", l))
            for t in range(TT):
                for c in range(4):
                    mm = nc.tensor.transpose(ps[:, 4 + 2 * kh + t, c * P:(c + 1) * P],
                                             merged[:, t, (4 * kh + c) * P:(4 * kh + c + 1) * P], ident)
                mm.then_inc(*done("merged_turned", f"k{kh}t{t}"))

        def mixer_a(L):
            l, k = L.l, U_FFN
            evicted = list(A_CHUNKS)
            steps = {("gla_qk", 1): [gla_rank], ("gla_v", 1): [gla_alpha], ("gla_r", 1): [gla_decays],
                     ("conv_a", 1): [gla_updates], ("conv_g", 1): [gla_reads], ("sb_q", 0): [conv_turn],
                     ("sb_k", 0): [sb_turn_q], ("sb_k", 1): [gla_turn], ("sb_v", 0): [sb_turn_k]}
            for n, name in enumerate(evicted):
                if n < 2:
                    banks_free(L, 1, n)
                else:
                    prev = evicted[n - 2]
                    pe.wait_ge(*after(f"{prev.split('_')[0]}_in", prev.split("_")[1], l))
                for kh in range(2):
                    square(L, k, hT, 4 * kh, pair(n), kh == 0, kh == 1, rows_follow(L, 1) if (n, kh) == (0, 0) else None)
                    k += 1
                    if (n, kh) == (0, 0):
                        narrow(L, k, RANK, 1)
                        k += 1
                    for step in steps.get((name, kh), ()):
                        step(l)
            first_of_branch = {2: 0, 0: 4, 1: 0}
            for i, b in enumerate(A_SECTIONS):
                for half in range(2):
                    if i:
                        pe.wait_ge(*after("merge", f"branch{i - 1}_{half}", l))
                    else:
                        pe.wait_ge(*after("sb_in", "v" if half else "k", l))
                    for kh in range(2):
                        square(L, k, hT, 4 * kh, pair(half), kh == 0, kh == 1)
                        k += 1
                        n = 6 * i + 2 * half + kh
                        if n % 2 == 0 and 2 <= n <= 8:
                            sb_out(l, n // 2 - 1)
                        if n % 2 == 0 and n < 8:
                            sb_logits(l, n // 2)
                        if n % 2 == 1 and n < 8:
                            sb_sums(l, n // 2)
                        if n == 14:
                            conv_normed(l)
                pe.wait_ge(*after(("gla_out_low", "sb_out_low", "conv_out_low")[i], ("out", "out3", "out")[i], l))
                for half in range(2):
                    pe.wait_ge(*after("gates", f"gate{i}_{half}", l))
                    square(L, k, bT, first_of_branch[b], pair(half), True, True,
                           first(lambda t: merged_turn(l, 0) if t else None) if i == 2 and half else None)
                    k += 1
                    n = 6 * i + 4 + half
                    if n in (4,):
                        sb_out(l, 1)
                        sb_logits(l, 2)
                    if n == 5:
                        sb_sums(l, 2)
                    if n == 11:
                        conv_rows(l)
            def before(kh, half):
                def wait(t):
                    pe.wait_ge(*after("merged_low", f"k{kh}t{t}", l))
                    if t:
                        pe.wait_ge(*after("merge", "branch2_1", l))
                return first(wait)

            for kh in range(2):
                for half in range(2):
                    square(L, k, hT, 4 * kh, lambda t, _, half=half: ps[:, 2 * t + half, :], kh == 0, kh == 1,
                           before(kh, half), (lambda t: done("mix_a_out", "t0")) if kh and half else None)
                    k += 1
                    if (kh, half) == (0, 0):
                        merged_turn(l, 1)
            rows_lead(L, 2)

        def memory_turn(l):
            for t in range(TT):
                pe.wait_ge(*after("memory_rows", f"normed{t}", l))
                for kh in range(2):
                    for c in range(4):
                        mm = nc.tensor.transpose(ps[:, 2 * t + kh, c * P:(c + 1) * P],
                                                 mem_rows[:, t, (4 * kh + c) * P:(4 * kh + c + 1) * P], ident)
                    mm.then_inc(*done("memory_turned", f"t{t}k{kh}"))

        def fox_decay(l):
            pe.wait_ge(*after("fox_gate", "log", l))
            nc.tensor.matmul(ps[:, 7, 0:8], konst("tri_le"), flog[:, 0, :], start=True, stop=True)
            nc.tensor.matmul(ps[:, 7, 8:16], konst("ones"), flog[:, 0, :], start=True, stop=False)
            nc.tensor.matmul(ps[:, 7, 8:16], konst("tri_le"), flog[:, 1, :], start=False, stop=True)
            for r in (0, 64):
                nc.tensor.matmul(ps[r:r + 8, 7, 128:256], flog[:, 0, :], konst("tri_le"), start=True, stop=True)
                nc.tensor.matmul(ps[r:r + 8, 7, 256:384], flog[:, 0, :], konst("ones"), start=True, stop=False)
                mm = nc.tensor.matmul(ps[r:r + 8, 7, 256:384], flog[:, 1, :], konst("tri_le"), start=False, stop=True)
            mm.then_inc(*done("fox_decay", "sums"))

        def fox_turn(l, which):
            pe.wait_ge(*after("fox_in", which, l))
            if which == "k":
                pe.wait_ge(*after("fox_gate", "rows", l))
            turn(fq if which == "q" else fk, 4 if which == "q" else 6).then_inc(*done("fox_turned", which))

        def lru_turn(l):
            pe.wait_ge(*after("lru_in", "xy", l))
            pe.wait_ge(*after("fox_in", "qT", l))
            turn(lxy, 4).then_inc(*done("lru_turned", "xy"))

        def fox_logits(l, g):
            t, n = g // 2, P * (g // 2 + 1)
            if g == 0:
                pe.wait_ge(*after("fox_in", "kT", l))
                pe.wait_ge(*after("fox_gate", "rows", l))
            elif g == 1:
                pe.wait_ge(*after("fox_rows", "rows0", l))
            elif g == 2:
                pe.wait_ge(*after("ret_scores", "scores1", l))
            else:
                pe.wait_ge(*after("fox_rows", "rows2", l))
            for i in range(2):
                c = 2 * (g % 2) + i
                for e in range(2):
                    r, h = 64 * e, 2 * c + e
                    bank = ps[:, 6 + e, i * T:i * T + n]
                    pick = konst("fox_pick").rearrange("p (h q) -> p h q", h=8)
                    nc.tensor.matmul(bank, pick[r:r + 8, h, :], fcT[r:r + 8, 0:n], start=True, stop=False)
                    mm = nc.tensor.matmul(bank, fqT[r:r + 64, c, t * P:(t + 1) * P], fkT[r:r + 64, c, 0:n],
                                          start=False, stop=True)
            mm.then_inc(*done("fox_logits", f"logits{g}"))

        def lru_gates(l):
            pe.wait_ge(*after("lru_conv", f"tap{CW2 - 1}_1", l))
            for g, name in enumerate(("w_r", "w_i")):
                w = packed(PACK_B, name).rearrange("p (c n) -> p c n", c=2)
                for c in range(2):
                    mm = nc.tensor.matmul(ps[:, 4 + g, c * T:(c + 1) * T], w[:, c, :], lru[0][:, c * T:(c + 1) * T],
                                          start=True, stop=True)
            mm.then_inc(*done("lru_gates", "logits"))

        def fox_turn_p(l, g):
            pe.wait_ge(*after("fox_rows", f"weights{g}", l))
            if g == 0:
                pe.wait_ge(*after("lru_act", "i1", l))
            else:
                pe.wait_ge(*after("fox_out_low", f"out{g - 1}", l))
            for s in range(g // 2 + 1):
                for b in range(4):
                    mm = nc.tensor.transpose(ps[:, 4 + s, b * P:(b + 1) * P], fl[:, b, s * P:(s + 1) * P], ident)
            mm.then_inc(*done("fox_p_turned", f"turned{g}"))

        def fox_out(l, g):
            pe.wait_ge(*after("fox_p", f"copied{g}", l))
            pe.wait_ge(*after("fox_in", "v", l))
            for i in range(2):
                for e in range(2):
                    h = 2 * (2 * (g % 2) + i) + e
                    for s in range(g // 2 + 1):
                        mm = nc.tensor.matmul(ps[64 * e:64 * e + 64, 4, i * P:(i + 1) * P], fv[:, s, h * 64:h * 64 + 64],
                                              fpT[:, 4 * s + 2 * i + e, :], start=s == 0, stop=s == g // 2)
            mm.then_inc(*done("fox_out", f"out{g}"))

        def ret_turn(l):
            pe.wait_ge(*after("ret_rope", "rotated", l))
            pe.wait_ge(*after("fox_rows", "rows1", l))
            turn(rope, 6).then_inc(*done("ret_turned", "qk"))

        def ret_scores(l, c):
            if c == 0:
                pe.wait_ge(*after("ret_rope", "qkT", l))
            else:
                pe.wait_ge(*after("ret_scores", "scores0", l))
            for e in range(2):
                r = slice(64 * e, 64 * e + 64)
                q, kk = rT[r, c, :], rT[r, 2 + c, :]
                nc.tensor.matmul(ps[:, 6 + e, 0:256], kk[:, 0:P], q, start=True, stop=True)
                mm = nc.tensor.matmul(ps[:, 6 + e, 256:384], kk[:, P:T], q[:, P:T], start=True, stop=True)
            mm.then_inc(*done("ret_dots", f"dots{c}"))

        def ret_rows(l):
            pe.wait_ge(*after("ret_scores", "scores1", l))
            pe.wait_ge(*after("ret_in", "v", l))
            pe.wait_ge(*after("fox_rows", "rows3", l))
            for t in range(TT):
                for h in range(4):
                    o = ps[:, 6, t * 256 + h * 64:t * 256 + h * 64 + 64]
                    if t == 0:
                        mm = nc.tensor.matmul(o, ret_s[:, h, 0:P], rv[:, 0, h * 64:h * 64 + 64], start=True, stop=True)
                    else:
                        nc.tensor.matmul(o, ret_s[:, h, P:T], rv[:, 0, h * 64:h * 64 + 64], start=True, stop=False)
                        mm = nc.tensor.matmul(o, ret_s[:, h, T:384], rv[:, 1, h * 64:h * 64 + 64], start=False, stop=True)
            mm.then_inc(*done("ret_rows", "rows"))

        def ret_back(l):
            pe.wait_ge(*after("ret_norm", "gated", l))
            turn(ry_f.rearrange("p (t n) -> p t n", t=TT), 6, 2).then_inc(*done("ret_back", "turned"))

        def keys_turn(l, half):
            pe.wait_ge(*after("memory_in", f"k{half}", l))
            if half == 0:
                pe.wait_ge(*after("fox_out_low", "out3", l))
            else:
                pe.wait_ge(*after("ret_out_low", "out", l))
            turn(km[:, :, half * 512:half * 512 + 512], 4 + 2 * half).then_inc(*done("keys_turned", f"k{half}"))

        def mixer_b(L):
            l = L.l
            k = 0
            chunks = [("fox_q", 512), ("fox_k", 0), ("lru_xy", 0), ("fox_v", 0), ("ret_qk", 0), ("ret_vg", 0)]
            read = [("fox_in", "q"), ("fox_in", "k"), ("lru_in", "xy"), ("fox_in", "v"), ("ret_in", "qk"),
                    ("ret_in", "g"), ("memory_in", "v0"), ("memory_in", "v1"), ("memory_in", "k0"), ("memory_in", "k1")]
            steps = {0: [], 1: [fox_decay, lambda l: fox_turn(l, "q")], 2: [lambda l: fox_turn(l, "k")],
                     3: [lru_turn, lambda l: fox_logits(l, 0)], 4: [lru_gates, lambda l: fox_logits(l, 1)],
                     5: [lambda l: fox_turn_p(l, 0), ret_turn]}
            for n in range(len(chunks)):
                if n < 2:
                    banks_free(L, 0, n)
                else:
                    pe.wait_ge(*after(*read[n - 2], l))
                for kh in range(2):
                    square(L, k, hT, 4 * kh, pair(n), kh == 0, kh == 1, rows_follow(L, 0) if (n, kh) == (0, 0) else None)
                    k += 1
                    if (n, kh) == (0, 0):
                        narrow(L, k, 8, 0)
                        k += 1
                for step in steps[n]:
                    step(l)
            memory_steps = [[lambda: fox_out(l, 0), lambda: ret_scores(l, 0)], [lambda: fox_turn_p(l, 1), lambda: ret_scores(l, 1)],
                            [lambda: fox_out(l, 1), lambda: fox_logits(l, 2)], [lambda: fox_turn_p(l, 2), lambda: fox_logits(l, 3)],
                            [lambda: fox_out(l, 2), lambda: ret_rows(l)], [lambda: fox_turn_p(l, 3)],
                            [lambda: fox_out(l, 3), lambda: ret_back(l)], [lambda: keys_turn(l, 0)]]
            for n in range(4):
                pe.wait_ge(*after(*read[4 + n], l))
                for kh in range(2):
                    square(L, k, bT, 4 * kh, pair(n), kh == 0, kh == 1)
                    k += 1
                    for step in memory_steps[2 * n + kh]:
                        step()
            acc = lambda half: (lambda t, _: ps[:, 2 * t + half, :])
            pe.wait_ge(*after("lru_low", "out", l))
            pe.wait_ge(*after("memory_in", "k1", l))
            for kh in range(2):
                if kh:
                    pe.wait_ge(*after("ret_out_low", "out", l))
                else:
                    pe.wait_ge(*after("fox_out_low", "out3", l))
                for half in range(2):
                    square(L, k, hT, 4 * kh, acc(half), kh == 0, kh == 1, None,
                           (lambda t: done("mix_b_out", "t0")) if kh and half else None)
                    k += 1
                    if kh and not half:
                        keys_turn(l, 1)
            rows_lead(L, 1)
            assert k == 25

        def cross(L):
            l, k = L.l, 25
            acc = lambda half: (lambda t, _: ps[:, 2 * t + half, :])
            for t in range(TT):
                banks_free(L, 1, t)
            for kh in range(2):
                for half in range(2):
                    square(L, k, hT, 4 * kh, acc(half), kh == 0, kh == 1,
                           rows_follow(L, 1) if k == 25 else left_ready(L, 1, kh))
                    k += 1
            for half in range(2):
                for t in range(TT):
                    pe.wait_ge(*after("cross_in", f"q{t}", l))
                pe.wait_ge(*after("memory_keys", "k1", l))
                turn(cq[:, :, half * 512:half * 512 + 512], 4 + 2 * half).then_inc(*done("cross_turned", f"q{half}"))
            for t in range(TT):
                pe.wait_ge(*after("cross_in", "qT1", l))
                for h in range(4):
                    for i in range(2):
                        c = 2 * h + i
                        mm = nc.tensor.matmul(ps[:, 2 * t + h // 2, (h % 2) * T:(h % 2 + 1) * T],
                                              cqT[:, c, t * P:(t + 1) * P], kmT[:, c, :], start=i == 0, stop=i == 1)
                mm.then_inc(*done("cross_logits", f"logits{t}"))
            for t in range(TT):
                pe.wait_ge(*after("cross_rows", f"weights{t}", l))
                for m in range(2):
                    for h in range(4):
                        mm = nc.tensor.transpose(ps[:, 4 + 2 * t + m, h * P:(h + 1) * P], cp[t][:, h, m * P:(m + 1) * P],
                                                 ident)
                mm.then_inc(*done("cross_p_turned", f"turned{t}"))
            for t in range(TT):
                pe.wait_ge(*after("cross_p", f"copied{t}", l))
            for c in range(KD):
                for m in range(2):
                    mm = nc.tensor.matmul(ps[:, c // 2, (c % 2) * T:(c % 2 + 1) * T], vm[:, m, c * P:(c + 1) * P],
                                          cpT[:, 4 * m + c // 2, :], start=m == 0, stop=m == 1)
                if c % 2:
                    mm.then_inc(*done("cross_out", f"out{c // 2}"))
            for kh in range(2):
                pe.wait_ge(*after("cross_out_low", "out3" if kh == 0 else "out3", l))
                for half in range(2):
                    square(L, k, hT, 4 * kh, acc(half), kh == 0, kh == 1, None,
                           (lambda t: done("cross_half", "t0")) if kh and half else None)
                    k += 1
            rows_lead(L, 2)
            assert k == U_MIX_B

        nc.tensor.sem_inc(unit_done, CREDIT)
        pe.wait_ge(ident_loaded, 16)
        rows_lead(Layer("A", 0), 0)
        with pe.Fori(0, DEPTH) as l:
            L = Layer("A", l)
            ffn(L, 0, 0, 0)
            mixer_a(L)
            ffn(L, 1, 2, U_FFN + U_MIX_A)
        with pe.Fori(0, DEPTH) as l:
            L = Layer("B", l)
            mixer_b(L)
            cross(L)
            ffn(L, 0, 2, U_MIX_B)
        for kh in range(2):
            norm_turn(Layer("B", DEPTH), 0, 1, kh)

    @block.scalar
    def _(act):
        def high(L, k):
            slot = k % RING
            act.wait_ge(raw_landed[slot], L.turn(k) * 32)
            act.wait_ge(unit_done, L.unit0 + (k + 1))
            nc.scalar.activation(w_hi[:, slot, :], raw[:, slot, :], ACT.Copy).then_inc(high_ready, 1)

        def multiplied(L, k):
            act.wait_ge(unit_done, L.done_units(k))

        def rows_of(L):
            return out_b if L.b else out_a

        def norm_in(L, j):
            for t in range(TT):
                act.wait_ge(x_ready, L.sub(j, 2, t + 1))
                nc.scalar.activation(rows_of(L)[:, t, :], x[:, t, :], ACT.Square,
                                     accum_out=ss_in[:, t:t + 1]).then_inc(sq_in, 1)
            gain(post_g, L.sub0 + j, 1, post_loaded)
            gain(pre_g, L.sub0 + (j + 1), 0, pre_loaded)
            for t in range(TT):
                act.wait_ge(sq_in, L.sub(j, 2, t + 1))
                nc.scalar.activation(std_in[:, t:t + 1], ss_in[:, t:t + 1], ACT.Sqrt, bias=EPS,
                                     scale=1.0 / D).then_inc(std_ready, 1)

        def rms_ready(L, j):
            act.wait_ge(rstd_ready, L.sub(j, 2, TT))

        def gain(dst, s, side, loaded):
            act.dma_start(dst[:, :], d["gains"][bass.ds(s, 1), side, :].partition_broadcast(P)).then_inc(loaded, 16)

        def turned(L, j, t, kh):
            act.wait_ge(h_turned, L.sub(j, 4, 2 * t + kh + 1))
            nc.scalar.activation(hT_hi[:, 4 * kh:4 * kh + 4, t * P:(t + 1) * P],
                                 ps[:, 6 - 2 * t + kh, :].rearrange("p (c n) -> p c n", c=4),
                                 ACT.Copy).then_inc(hT_hi_ready, 1)

        def root(L, j):
            act.wait_ge(ident_loaded, 16)
            nc.scalar.activation(root_warm, ident[:, 0:1], ACT.Sqrt).then_inc(root_loaded, 1)
            act.wait_ge(root_loaded, L.sub(j, 1, 1))

        def norm_out(L, j, complete, half):
            m = 4.0 if half else 1.0
            def over(t):
                act.wait_ge(rstd_out_ready, L.sub(j, 2, t + 1))
                nc.scalar.activation(rows_of(L)[:, t, :].rearrange("p (h n) -> p h n", h=2), ps[:, 2 * t:2 * t + 2, :],
                                     ACT.Copy, scale=rstd_out[:, t:t + 1]).then_inc(out_copied, 1)

            def squares(t, h):
                act.wait_ge(*complete(t, h))
                if t:
                    act.wait_ge(sq_out, L.sub(j, 4, h + 1))
                nc.scalar.activation(pairbuf[:, 512 * h:512 * h + 512], ps[:, 2 * t + h, :], ACT.Square,
                                     accum_out=ss_out[:, 2 * t + h:2 * t + h + 1]).then_inc(sq_out, 1)

            def root_mean(t):
                act.wait_ge(sq_out, L.sub(j, 4, 2 * t + 2))
                act.wait_ge(sq_bias, L.sub(j, 2, t + 1))
                nc.scalar.activation(std_out[:, t:t + 1], ss_out[:, 2 * t + 1:2 * t + 2], ACT.Sqrt,
                                     bias=bias_out[:, t:t + 1], scale=m / D).then_inc(std_out_ready, 1)

            squares(0, 0)
            squares(0, 1)
            root_mean(0)
            squares(1, 0)
            over(0)
            squares(1, 1)
            root_mean(1)
            for kh in range(2):
                turned(L, j + 1, 0, kh)
            over(1)
            for kh in range(2):
                turned(L, j + 1, 1, kh)

        def ffn(L, n, j, k0):
            f = L.ffn(n)

            def silu(M, k, c):
                multiplied(M, k)
                for t in range(TT):
                    silu_t = nc.scalar.activation(sil[:, t, :], ps[:, 6 + t, 0:FC], ACT.Silu, scale=rstd_in[:, t:t + 1])
                silu_t.then_inc(silu_ready, 1)

            def hidden(c, dst=bT_hi[:, KD:KD + 2, :]):
                act.wait_ge(hid_turned, f * NCHUNK + (c + 1))
                nc.scalar.activation(dst, ps[:, 4, :].rearrange("p (i t) -> p i t", i=2),
                                     ACT.Copy).then_inc(gT_hi_ready, 1)

            def chunk(M, k, c):
                hidden(c - 1)
                high(M, k + AHEAD)
                high(M, k + 1 + AHEAD)
                silu(M, k + 1, c)
                high(M, k + 2 + AHEAD)

            high(L, k0 + AHEAD)
            norm_in(L, j)
            if n:
                memory_std(L.l)
            high(L, k0 + 1 + AHEAD)
            rms_ready(L, j)
            silu(L, k0 + 1, 0)
            if n:
                hidden(0)
                high(L, k0 + 2 + AHEAD)
                memory_high(L.l)
                high(L, k0 + 3 + AHEAD)
                silu(L, k0 + 3, 1)
                high(L, k0 + 4 + AHEAD)
            else:
                chunk(L, k0 + 2, 1)
            with act.Fori(2, NCHUNK - 1) as c:
                chunk(Chunk(L, c), k0 + 5, c)
            end, c = k0 + U_FFN - 1, NCHUNK - 1
            hidden(c - 1)
            high(L, end - 3 + AHEAD)
            high(L, end - 2 + AHEAD)
            silu(L, end - 2, c)
            hidden(c, hT_hi[:, 0:2, :])
            root(L, j)
            high(L, end - 1 + AHEAD)
            high(L, end + AHEAD)
            norm_out(L, j, lambda t, h: (unit_done, L.done_units(end)) if t and h else (ffn_out, f * 3 + (2 * t + h + 1)),
                     not L.b)

        def copy(dst, src, stage, step, scale=1.0, func=ACT.Copy):
            nc.scalar.activation(dst, src, func, scale=scale).then_inc(*done(stage, step))

        def rows(dst, src, stage, step, func=ACT.Copy):
            for t in range(TT):
                last = nc.scalar.activation(dst[:, t, :], src[:, t, :], func, scale=rstd_in[:, t:t + 1])
            last.then_inc(*done(stage, step))

        def mixed(L, k, stage):
            return lambda t, h: ((unit_done, L.done_units(k - 1)) if not h else
                                 (unit_done, L.done_units(k)) if t else after(stage, "t0", L.l))

        def chunk_rows(n):
            return ps[:, 2 * (n % 2):2 * (n % 2) + 2, :]

        def two(bank):
            return ps[:, bank:bank + 2, :].rearrange("p b (c t) -> p (b c) t", c=2)

        def gla_alpha(l):
            act.wait_ge(*after("gla_alpha", "logits", l))
            nc.scalar.activation(gdec, ps[:, 7, :], ACT.Abs).then_inc(*done("gla_soft", "abs"))
            act.wait_ge(*after("gla_soft", "abs", l))
            nc.scalar.activation(gdec, gdec, ACT.Exp, scale=-1.0).then_inc(*done("gla_soft", "exp"))
            act.wait_ge(*after("gla_soft", "exp", l))
            nc.scalar.activation(gdec, gdec, ACT.Ln, bias=1.0).then_inc(*done("gla_soft", "ln"))

        def gla_decays(l):
            act.wait_ge(*after("gla_sums", "sums", l))
            nc.scalar.activation(gdec, ps[:, 4, :], ACT.Exp, scale=-1.0 / TAU).then_inc(*done("gla_exp", "to_end"))
            nc.scalar.activation(lam.rearrange("p c n -> p (c n)"), ps[:, 5, 0:8], ACT.Exp,
                                 scale=-1.0 / TAU).then_inc(*done("gla_exp", "chunk"))

        def gla_std(l):
            act.wait_ge(*after("gla_out", "sums", l))
            nc.scalar.activation(stdg, ssg, ACT.Sqrt, bias=EPS, scale=1.0 / P).then_inc(*done("gla_std", "std"))

        def gla_out(l):
            act.wait_ge(*after("gla_out_turned", "turned", l))
            for c in range(4):
                nc.scalar.activation(bT_hi[:, c, :], two(6)[:, c, :], ACT.Copy,
                                     scale=packed(PACK_A, "gla_g")[:, c:c + 1]).then_inc(*done("gla_out_high", f"out{c}"))

        def sb_weights(l, c):
            act.wait_ge(*after("sb_logits", f"logits{c}", l))
            nc.scalar.activation(sb_z.rearrange("p (e n) -> p e n", e=2), ps[:, 4:6, 0:384],
                                 ACT.Copy).then_inc(*done("sb_weights", f"copied{c}"))
            nc.scalar.activation(sb_e.rearrange("p (e n) -> p e n", e=2), ps[:, 4:6, 0:384],
                                 ACT.Abs).then_inc(*done("sb_weights", f"abs{c}"))
            act.wait_ge(*after("sb_weights", f"abs{c}", l))
            nc.scalar.activation(sb_e, sb_e, ACT.Exp, scale=-1.0).then_inc(*done("sb_weights", f"exp{c}"))
            act.wait_ge(*after("sb_weights", f"exp{c}", l))
            nc.scalar.activation(sb_e, sb_e, ACT.Ln, bias=1.0).then_inc(*done("sb_weights", f"ln{c}"))

        def sb_exp(l, c):
            act.wait_ge(*after("sb_keep", f"exponent{c}", l))
            nc.scalar.activation(sb_e, sb_z, ACT.Exp).then_inc(*done("sb_weights", f"weights{c}"))

        def sb_out(l, c):
            act.wait_ge(*after("sb_out", f"out{c}", l))
            nc.scalar.activation(bT_hi[:, 4 + c, :].rearrange("p (t n) -> p t n", t=TT), ps[:, 6:8, 384:512],
                                 ACT.Copy).then_inc(*done("sb_out_high", f"out{c}"))

        def conv_std(l):
            for t in range(TT):
                act.wait_ge(*after("conv_norm", f"centred{t}", l))
                nc.scalar.activation(conv_y_f[:, t * 512:(t + 1) * 512], conv_n[:, t, :], ACT.Square,
                                     accum_out=css[:, t:t + 1]).then_inc(*done("conv_std", f"sum{t}"))
            for t in range(TT):
                act.wait_ge(*after("conv_std", f"sum{t}", l))
                nc.scalar.activation(cstd[:, t:t + 1], css[:, t:t + 1], ACT.Sqrt, bias=EPS,
                                     scale=1.0 / BW).then_inc(*done("conv_std", f"std{t}"))

        def conv_out(l):
            act.wait_ge(*after("conv_normed", "turned", l))
            for c in range(4):
                nc.scalar.activation(conv_y[:, c, :], two(4)[:, c, :], ACT.Silu, bias=packed(PACK_A, "ln_b")[:, c:c + 1],
                                     scale=packed(PACK_A, "ln_g")[:, c:c + 1]).then_inc(*done("conv_out", f"act{c}"))
            act.wait_ge(*after("conv_out", "act3", l))
            multiplied_gla = U_FFN + 17 + 5
            act.wait_ge(unit_done, Layer("A", l).done_units(multiplied_gla))
            nc.scalar.activation(bT_hi[:, 0:4, :], conv_y, ACT.Copy).then_inc(*done("conv_out", "high"))

        def merged_high(l, kh):
            for t in range(TT):
                act.wait_ge(*after("merged_turned", f"k{kh}t{t}", l))
                nc.scalar.activation(hT_hi[:, 4 * kh:4 * kh + 4, t * P:(t + 1) * P],
                                     ps[:, 4 + 2 * kh + t, :].rearrange("p (c n) -> p c n", c=4),
                                     ACT.Copy).then_inc(*done("merged_high", f"k{kh}t{t}"))

        def mixer_a(L):
            l, k = L.l, U_FFN
            high(L, k + AHEAD)
            norm_in(L, 1)
            act.dma_start(pack[:, 0:PACK_A_W], d["pack_a"][bass.ds(l, 1), :, :].rearrange("o p n -> p (o n)")).then_inc(
                pack_loaded, 16)
            rms_ready(L, 1)
            k += 1
            plan = {"gla_qk": (gqk, "gla_in", "qk", ACT.Copy), "gla_v": (gv, "gla_in", "v", ACT.Copy),
                    "gla_r": (gr, "gla_in", "r", ACT.Silu), "conv_a": (conv_u, "conv_in", "a", ACT.Copy),
                    "conv_g": (conv_s, "conv_in", "g", ACT.Sigmoid), "sb_q": (sb_q, "sb_in", "q", ACT.Copy),
                    "sb_k": (sb_k, "sb_in", "k", ACT.Copy), "sb_v": (sbv, "sb_in", "v", ACT.Copy)}
            for n, name in enumerate(A_CHUNKS):
                high(L, k + AHEAD)
                if name == "gla_r":
                    gla_alpha(l)
                if name == "conv_a":
                    gla_decays(l)
                if name == "sb_k":
                    act.wait_ge(*after("sb_turned", "q", l))
                    copy(sbqT, two(4), "sb_in", "qT", 64 ** -0.5)
                if name == "sb_v":
                    gla_out(l)
                    act.wait_ge(*after("sb_turned", "k", l))
                    copy(sbkT, two(4), "sb_in", "kT")
                if name == "sb_q":
                    gla_std(l)
                high(L, k + 1 + AHEAD)
                multiplied(L, k + 1)
                dst, stage, step, func = plan[name]
                if name == "sb_q":
                    act.wait_ge(*after("conv_turned", "u", l))
                if name == "sb_v":
                    act.wait_ge(*after("gla_out", "gated", l))
                rows(dst, chunk_rows(n), stage, step, func)
                k += 2
            for i, b in enumerate(A_SECTIONS):
                for half in range(2):
                    for kh in range(2):
                        high(L, k + AHEAD)
                        n = 6 * i + 2 * half + kh
                        if n == 15:
                            conv_out(l)
                        if kh:
                            multiplied(L, k)
                            if i:
                                act.wait_ge(*after("merge", f"branch{i - 1}_{half}", l))
                            rows(sg[:, half, :, :], chunk_rows(half), "gates", f"gate{i}_{half}", ACT.Sigmoid)
                        if n < 12:
                            section_step(l, n)
                        if n == 12:
                            conv_std(l)
                        k += 1
                for half in range(2):
                    high(L, k + AHEAD)
                    section_step(l, 6 * i + 4 + half)
                    k += 1
            merged_high(l, 0)
            for n in range(4):
                high(L, k + AHEAD)
                if n == 0:
                    merged_high(l, 1)
                    memory_load(l)
                if n == 2:
                    root(L, 1)
                k += 1
            norm_out(L, 1, mixed(L, k - 1, "mix_a_out"), False)

        def section_step(l, n):
            if n % 2 == 0 and 2 <= n <= 8:
                sb_out(l, n // 2 - 1)
            if n % 2 == 0 and n < 8:
                sb_weights(l, n // 2)
            if n % 2 == 1 and n < 8:
                sb_exp(l, n // 2)

        def memory_load(l):
            act.dma_start(mem_rows[:, :, :], d["mem"][0, :, :].rearrange("(t p) n -> p t n", p=P)).then_inc(memory_loaded, 16)
            act.dma_start(mem_g, d["mem_g"][0:1, :].partition_broadcast(P)).then_inc(memory_loaded, 16)

        def memory_std(l):
            act.wait_ge(memory_loaded, l * 32 + 32)
            for t in range(TT):
                if t:
                    act.wait_ge(*after("memory_std", f"sum{t - 1}", l))
                nc.scalar.activation(mem_sq, mem_rows[:, t, :], ACT.Square,
                                     accum_out=ss_mem[:, t:t + 1]).then_inc(*done("memory_std", f"sum{t}"))
            for t in range(TT):
                act.wait_ge(*after("memory_std", f"sum{t}", l))
                nc.scalar.activation(std_mem[:, t:t + 1], ss_mem[:, t:t + 1], ACT.Sqrt, bias=EPS,
                                     scale=1.0 / D).then_inc(*done("memory_std", f"std{t}"))

        def memory_high(l):
            for t in range(TT):
                for kh in range(2):
                    act.wait_ge(*after("memory_turned", f"t{t}k{kh}", l))
                    nc.scalar.activation(bT_hi[:, 4 * kh:4 * kh + 4, t * P:(t + 1) * P],
                                         ps[:, 2 * t + kh, :].rearrange("p (c n) -> p c n", c=4),
                                         ACT.Copy).then_inc(*done("memory_high", f"t{t}k{kh}"))

        def rope():
            for name, table in (("sin", sin), ("cos", cos)):
                act.wait_ge(*after("rope_angles", name, 0))
                nc.scalar.activation(table, table, ACT.Sin).then_inc(*done("rope_tables", name))

        def fox_soft(l):
            act.wait_ge(*after("fox_gate", "logits", l))
            z = flog.rearrange("p t h -> p (t h)")
            nc.scalar.activation(ftmp, z, ACT.Abs).then_inc(*done("fox_soft", "abs"))
            act.wait_ge(*after("fox_soft", "abs", l))
            nc.scalar.activation(ftmp, ftmp, ACT.Exp, scale=-1.0).then_inc(*done("fox_soft", "exp"))
            act.wait_ge(*after("fox_soft", "exp", l))
            nc.scalar.activation(ftmp, ftmp, ACT.Ln, bias=1.0).then_inc(*done("fox_soft", "ln"))

        def lru_lambda(l):
            act.wait_ge(pack_loaded, l * 16 + (16 * DEPTH + 16))
            nc.scalar.activation(lru_t, packed(PACK_B, "lam"), ACT.Abs).then_inc(*done("lru_act", "abs"))
            act.wait_ge(*after("lru_act", "abs", l))
            nc.scalar.activation(lru_t, lru_t, ACT.Exp, scale=-1.0).then_inc(*done("lru_act", "lambda"))

        def lru_gates(l):
            act.wait_ge(*after("lru_gates", "logits", l))
            for g, (dst, bias) in enumerate(((lru[1], "b_r"), (lru[2], "b_i"))):
                for c in range(2):
                    nc.scalar.activation(dst[:, c * T:(c + 1) * T], ps[:, 4 + g, c * T:(c + 1) * T], ACT.Sigmoid,
                                         bias=packed(PACK_B, bias)[:, c:c + 1]).then_inc(*done("lru_act", f"{'ri'[g]}{c}"))

        def lru_decay(l):
            act.wait_ge(*after("lru_math", "log1", l))
            nc.scalar.activation(lru[3], lru[1], ACT.Tanh).then_inc(*done("lru_act", "tanh"))
            act.wait_ge(*after("lru_act", "tanh", l))
            nc.scalar.activation(lru[1], lru[1], ACT.Exp).then_inc(*done("lru_act", "decay"))
            act.wait_ge(*after("lru_turn", "y", l))
            nc.scalar.activation(lyT, lyT, ACT.Gelu_apprx_tanh).then_inc(*done("lru_act", "gelu"))

        def lru_root(l):
            act.wait_ge(*after("lru_math", "square", l))
            nc.scalar.activation(lru[3], lru[3], ACT.Sqrt).then_inc(*done("lru_act", "root"))

        def lru_high(l):
            act.wait_ge(*after("lru_math", "out", l))
            nc.scalar.activation(hT_hi[:, 0:2, :], lru[0].rearrange("p (c t) -> p c t", c=2),
                                 ACT.Copy).then_inc(*done("lru_act", "high"))

        def fox_exp(l, g):
            n = P * (g // 2 + 1)
            act.wait_ge(*after("fox_rows", f"max{g}", l))
            for b in range(4):
                nc.scalar.activation(fl[:, b, 0:n], fl[:, b, 0:n], ACT.Exp, bias=fmax[:, b:b + 1],
                                     accum_out=fden[:, b:b + 1]).then_inc(*done("fox_exp", f"g{g}h{b}"))

        def fox_p(l, g):
            act.wait_ge(*after("fox_p_turned", f"turned{g}", l))
            n = g // 2 + 1
            nc.scalar.activation(fpT[:, 0:4 * n, :], ps[:, 4:4 + n, :].rearrange("p s (b t) -> p (s b) t", b=4),
                                 ACT.Copy).then_inc(*done("fox_p", f"copied{g}"))

        def fox_tiles(w, g):
            c, t = 2 + 2 * (g % 2), g // 2
            return w[:, c:c + 2, t * P:(t + 1) * P]

        def fox_out(l, g):
            act.wait_ge(*after("fox_out", f"out{g}", l))
            nc.scalar.activation(fox_tiles(hT_hi, g), ps[:, 4, 0:256].rearrange("p (c t) -> p c t", c=2),
                                 ACT.Copy).then_inc(*done("fox_out_high", f"out{g}"))

        def ret_std(l):
            act.wait_ge(*after("ret_norm", "sums", l))
            nc.scalar.activation(rstat2, rstat, ACT.Sqrt, bias=EPS, scale=1.0 / 64).then_inc(*done("ret_std", "std"))

        def ret_out(l):
            act.wait_ge(*after("ret_back", "turned", l))
            nc.scalar.activation(hT_hi[:, 6:8, :], ps[:, 6, :].rearrange("p (c t) -> p c t", c=2),
                                 ACT.Copy).then_inc(*done("ret_out_high", "out"))

        def keys(l, half):
            act.wait_ge(*after("keys_turned", f"k{half}", l))
            copy(kmT[:, 4 * half:4 * half + 4, :], two(4 + 2 * half), "memory_keys", f"k{half}")

        def mixer_b(L):
            l = L.l
            high(L, AHEAD)
            norm_in(L, 0)
            act.dma_start(pack[:, 0:PACK_B_W], d["pack_b"][bass.ds(l, 1), :, :].rearrange("o p n -> p (o n)")).then_inc(
                pack_loaded, 16)
            rms_ready(L, 0)
            k = 1
            between = {0: lambda: (fox_soft(l), lru_lambda(l)),
                       2: lambda: (act.wait_ge(*after("fox_turned", "q", l)), copy(fqT, two(4), "fox_in", "qT", 64 ** -0.5)),
                       3: lambda: (act.wait_ge(*after("fox_turned", "k", l)), copy(fkT, two(6), "fox_in", "kT")),
                       4: lambda: fox_exp(l, 0),
                       5: lambda: lru_gates(l)}
            evicted = [(fq, "fox_in", "q"), (fk, "fox_in", "k"), (lxy, "lru_in", "xy"), (fv, "fox_in", "v"),
                       (rqk, "ret_in", "qk"), (rv, "ret_in", "v")]
            for n in range(6):
                high(L, k + AHEAD)
                if n in between:
                    between[n]()
                high(L, k + 1 + AHEAD)
                multiplied(L, k + 1)
                dst, stage, step = evicted[n]
                rows(dst, chunk_rows(n) if n < 5 else chunk_rows(n)[:, :, 0:256], stage, step)
                if n == 5:
                    rows(rg, chunk_rows(n)[:, :, 256:512], "ret_in", "g", ACT.Silu)
                k += 2
            steps = [lambda: (fox_p(l, 0), fox_exp(l, 1)),
                     lambda: (lru_decay(l), fox_out(l, 0)),
                     lambda: (fox_p(l, 1), lru_root(l)),
                     lambda: (fox_out(l, 1), fox_exp(l, 2)),
                     lambda: (lru_high(l), fox_p(l, 2), fox_exp(l, 3)),
                     lambda: (fox_out(l, 2), ret_std(l)),
                     lambda: fox_p(l, 3),
                     lambda: (ret_out(l), fox_out(l, 3))]
            for n in range(4):
                name = ("v0", "v1", "k0", "k1")[n]
                dst = (vm, km)[n // 2][:, :, (n % 2) * 512:(n % 2) * 512 + 512]
                for kh in range(2):
                    high(L, k + kh + AHEAD)
                    steps[2 * n + kh]()
                multiplied(L, k + 1)
                if name == "k0":
                    act.wait_ge(*after("lru_low", "out", l))
                copy(dst, chunk_rows(n), "memory_in", name)
                k += 2
            keys(l, 0)
            for n in range(4):
                high(L, k + AHEAD)
                if n == 3:
                    keys(l, 1)
                if n == 2:
                    root(L, 0)
                k += 1
            norm_out(L, 0, mixed(L, k - 1, "mix_b_out"), False)

        def cross(L):
            l, k = L.l, 25
            for n in range(4):
                high(L, k + AHEAD)
                if n == 0:
                    norm_in(L, 1)
                    rms_ready(L, 1)
                k += 1
            multiplied(L, k - 1)
            for t in range(TT):
                copy(cq[:, t, :].rearrange("p (h n) -> p h n", h=2), ps[:, 2 * t:2 * t + 2, :], "cross_in", f"q{t}",
                     rstd_in[:, t:t + 1])
            for half in range(2):
                act.wait_ge(*after("cross_turned", f"q{half}", l))
                copy(cqT[:, 4 * half:4 * half + 4, :], two(4 + 2 * half), "cross_in", f"qT{half}", 256 ** -0.5)
            for t in range(TT):
                act.wait_ge(*after("cross_max", f"max{t}", l))
                for h in range(4):
                    nc.scalar.activation(cp[t][:, h, :], ps[:, 2 * t + h // 2, (h % 2) * T:(h % 2 + 1) * T], ACT.Exp,
                                         bias=cmax[:, 4 * t + h:4 * t + h + 1],
                                         accum_out=cden[:, 4 * t + h:4 * t + h + 1]).then_inc(*done("cross_exp", f"t{t}h{h}"))
            for t in range(TT):
                act.wait_ge(*after("cross_p_turned", f"turned{t}", l))
                copy(cpT[:, :, t * P:(t + 1) * P],
                     ps[:, 4 + 2 * t:6 + 2 * t, :].rearrange("p m (h n) -> p (m h) n", h=4), "cross_p", f"copied{t}")
            for c in range(4):
                act.wait_ge(*after("cross_out", f"out{c}", l))
                copy(hT_hi[:, 2 * c:2 * c + 2, :], ps[:, c, :].rearrange("p (c t) -> p c t", c=2), "cross_out_high", f"out{c}")
            for n in range(4):
                high(L, k + AHEAD)
                if n == 2:
                    root(L, 1)
                k += 1
            norm_out(L, 1, mixed(L, k - 1, "cross_half"), False)

        act.dma_start(positions, d["positions"][:, :]).then_inc(const_loaded, 16)
        at, width = CONST["inv_freq"]
        act.dma_start(const[:, at:at + width], d["const"][:, at:at + width]).then_inc(const_loaded, 16)
        for t in range(TT):
            act.dma_start(x[:, t, :], d["x"][0, t * P:(t + 1) * P, :]).then_inc(x_loaded[t], 16)
            if t == 0:
                gain(pre_g, 0, 0, pre_loaded)
        nc.scalar.sem_inc(out_copied, TT)
        rope()
        for k in range(AHEAD):
            act.wait_ge(raw_landed[k], 32)
            nc.scalar.activation(w_hi[:, k, :], raw[:, k, :], ACT.Copy).then_inc(high_ready, 1)
            for kh in range(2):
                turned(Layer("A", 0), 0, k, kh)
        for at, end in ((P, at), (at + width, CONST_ARRAY.shape[1])):
            act.dma_start(const[:, at:end], d["const"][:, at:end]).then_inc(const_loaded, 16)
        with act.Fori(0, DEPTH) as l:
            L = Layer("A", l)
            ffn(L, 0, 0, 0)
            mixer_a(L)
            ffn(L, 1, 2, U_FFN + U_MIX_A)
        with act.Fori(0, DEPTH) as l:
            L = Layer("B", l)
            mixer_b(L)
            cross(L)
            ffn(L, 0, 2, U_MIX_B)
        act.wait_ge(pre_loaded, 16 * (6 * DEPTH + 1))

    @block.vector
    def _(dve):
        V = nc.vector

        def flat(w):
            return w.bitcast(F32)

        def multiplied(L, k):
            dve.wait_ge(unit_done, L.done_units(k))

        def norm_in(L, j):
            for t in range(TT):
                dve.wait_ge(std_ready, L.sub(j, 2, t + 1))
                V.reciprocal(rstd_in[:, t:t + 1], std_in[:, t:t + 1]).then_inc(rstd_ready, 1)
            dve.wait_ge(rstd_ready, L.sub(j, 2, TT))

        def prepare(L, j):
            dve.wait_ge(post_loaded, L.sub(j, 16, 16))
            dve.wait_ge(pre_loaded, L.sub(j, 16, 32))
            V.tensor_tensor(both_b if L.b else both_a, post_g[:, :], pre_g[:, :], ALU.mult).then_inc(prepared, 1)
            for t in range(TT):
                dve.wait_ge(x_ready, L.sub(j, 2, t + 1))
                V.tensor_tensor(x_pre[:, t, :], x[:, t, :], pre_g[:, :], ALU.mult).then_inc(prepared, 1)

        def low(L, j, t, kh):
            dve.wait_ge(hT_hi_ready, L.sub(j, 4, 2 * t + kh + 1))
            tiles = (slice(None), slice(4 * kh, 4 * kh + 4), slice(t * P, (t + 1) * P))
            V.tensor_tensor(hT_lo[tiles], ps[:, 6 - 2 * t + kh, :].rearrange("p (c n) -> p c n", c=4),
                            flat(hT_hi[tiles]), ALU.subtract).then_inc(hT_ready, 1)

        def norm_out(L, j, half):
            m = 4.0 if half else 1.0
            rows, both_g = (out_b, both_b) if L.b else (out_a, both_a)
            dve.wait_ge(prepared, L.sub(j, 3, 3))
            for t in range(TT):
                for h in range(2):
                    dve.wait_ge(sq_out, L.sub(j, 4, 2 * t + h + 1))
                    if h == 0:
                        V.tensor_scalar(bias_out[:, t:t + 1], ss_out[:, 2 * t:2 * t + 1], m / D, m * EPS, ALU.mult,
                                        ALU.add).then_inc(sq_bias, 1)
                    cols = slice(512 * h, 512 * h + 512)
                    V.tensor_tensor(xn[:, t, cols], ps[:, 2 * t + h, :], both_g[:, cols], ALU.mult).then_inc(weighted, 1)
                dve.wait_ge(std_out_ready, L.sub(j, 2, t + 1))
                V.reciprocal(rstd_out[:, t:t + 1], std_out[:, t:t + 1]).then_inc(rstd_out_ready, 1)
                if t:
                    low(L, j + 1, 0, 0)
                dve.wait_ge(rstd_out_ready, L.sub(j, 2, t + 1))
                for kh in range(2):
                    cols = slice(512 * kh, 512 * kh + 512)
                    dve.wait_ge(weighted, L.sub(j, 4, 2 * t + kh + 1))
                    V.scalar_tensor_tensor(xn[:, t, cols], xn[:, t, cols], rstd_out[:, t:t + 1], x_pre[:, t, cols], ALU.mult,
                                           ALU.add).then_inc(h_ready, 1)
            for t, kh in ((0, 1), (1, 0), (1, 1)):
                low(L, j + 1, t, kh)
            for t in range(TT):
                dve.wait_ge(out_copied, L.sub(j, 2, 2 + t + 1))
                V.tensor_tensor(rows[:, t, :], rows[:, t, :], post_g[:, :], ALU.mult).then_inc(scaled, 1)
                dve.wait_ge(scaled, L.sub(j, 2, t + 1))
                V.tensor_tensor(x[:, t, :], x[:, t, :], rows[:, t, :], ALU.add).then_inc(x_ready, 1)

        def ffn(L, n, j, k0):
            f = L.ffn(n)

            def hidden(c):
                dve.wait_ge(silu_ready, f * NCHUNK + (c + 1))
                for t in range(TT):
                    up = V.scalar_tensor_tensor(hid[:, t, :], ps[:, 6 + t, FC:2 * FC], rstd_in[:, t:t + 1], sil[:, t, :],
                                                ALU.mult, ALU.mult)
                up.then_inc(hid_ready, 1)

            def hidden_low(c, hi=bT_hi[:, KD:KD + 2, :], lo=bT_lo[:, KD:KD + 2, :]):
                dve.wait_ge(gT_hi_ready, f * NCHUNK + (c + 1))
                V.tensor_tensor(lo, ps[:, 4, :].rearrange("p (i t) -> p i t", i=2), flat(hi),
                                ALU.subtract).then_inc(gT_ready, 1)

            norm_in(L, j)
            if n:
                memory_rows(L.l)
            hidden(0)
            hidden_low(0)
            if n:
                memory_low(L.l)
            hidden(1)
            prepare(L, j)
            with dve.Fori(2, NCHUNK - 1) as c:
                hidden_low(c - 1)
                hidden(c)
            hidden_low(NCHUNK - 2)
            hidden(NCHUNK - 1)
            hidden_low(NCHUNK - 1, hT_hi[:, 0:2, :], hT_lo[:, 0:2, :])
            norm_out(L, j, not L.b)

        def two(bank):
            return ps[:, bank:bank + 2, :].rearrange("p b (c t) -> p (b c) t", c=2)

        def gla_rank_rows(L, k):
            l = L.l
            multiplied(L, k)
            for t in range(TT):
                V.tensor_scalar(lr_rows[:, t, :], ps[:, 6, t * RANK:(t + 1) * RANK], rstd_in[:, t:t + 1], None,
                                ALU.mult).then_inc(*done("gla_rank", "rows" if t else "rows0"))

        def gla_rank_turned(l):
            dve.wait_ge(*after("gla_rank_turned", "turned", l))
            V.tensor_copy(lrT[0:RANK, :], ps[0:RANK, 6, P:P + T]).then_inc(*done("gla_rank", "turned"))

        def gla_keep(l):
            dve.wait_ge(*after("gla_soft", "abs", l))
            V.tensor_scalar(nla, ps[:, 7, :], -1.0, 0.0, ALU.mult, ALU.max).then_inc(*done("gla_keep", "max"))
            dve.wait_ge(*after("gla_keep", "max", l))
            dve.wait_ge(*after("gla_soft", "ln", l))
            V.tensor_tensor(nla, nla, gdec, ALU.add).then_inc(*done("gla_keep", "softplus"))

        def gla_keys(l):
            dve.wait_ge(*after("gla_turned", "q", l))
            V.tensor_copy(gqT, ps[:, 6, :].rearrange("p (c t) -> p c t", c=2)).then_inc(*done("gla_decay", "q"))
            dve.wait_ge(*after("gla_exp", "to_end", l))
            dve.wait_ge(*after("gla_in", "qk", l))
            g = gdec.rearrange("p (t n) -> p t n", t=TT)
            V.tensor_tensor(g, g, gqk[:, :, 256:512], ALU.mult).then_inc(*done("gla_decay", "keys"))

        def gla_states(l):
            dve.wait_ge(*after("gla_updates", "updates", l))
            dve.wait_ge(*after("gla_exp", "chunk", l))
            for n in range(4):
                for c in range(2):
                    t, half = n // 2, n % 2
                    update = ps[:, 6 + half, (2 * c + t) * P:(2 * c + t + 1) * P]
                    step = "last" if (n, c) == (3, 1) else f"n{n}c{c}"
                    if n == 0:
                        V.tensor_copy(gstate[:, c, n, :], update).then_inc(*done("gla_state", step))
                    else:
                        dve.wait_ge(*after("gla_state", f"n{n - 1}c{c}", l))
                        V.scalar_tensor_tensor(gstate[:, c, n, :], gstate[:, c, n - 1, :], lam[:, c, n:n + 1], update,
                                               ALU.mult, ALU.add).then_inc(*done("gla_state", step))

        def gla_rows(l):
            dve.wait_ge(*after("gla_reads", "reads", l))
            o = go_f.rearrange("p (t c e v) -> p t c e v", t=TT, c=2, e=2)
            for e in range(2):
                V.tensor_scalar(o[:, :, :, e, :], ps[:, 4 + e, :].rearrange("p (t c v) -> p t c v", t=TT, c=2), 0.125, None,
                                ALU.mult).then_inc(*done("gla_out", "rows" if e else "rows_even"))
            dve.wait_ge(*after("gla_out", "rows", l))
            V.tensor_tensor(gsq_f, go_f, go_f, ALU.mult).then_inc(*done("gla_out", "squares"))
            dve.wait_ge(*after("gla_out", "squares", l))
            V.tensor_reduce(ssg, gsq_f.rearrange("p (h v) -> p h v", h=8), AX.X, ALU.add).then_inc(*done("gla_out", "sums"))

        def gla_gated(l):
            dve.wait_ge(*after("gla_std", "std", l))
            V.reciprocal(rstdg, stdg).then_inc(*done("gla_out", "rstd"))
            dve.wait_ge(*after("gla_in", "r", l))
            V.tensor_tensor(go_f, go_f, gr_f, ALU.mult).then_inc(*done("gla_out", "with_r"))
            dve.wait_ge(*after("gla_out", "with_r", l))
            o = go_f.rearrange("p (h v) -> p h v", h=8)
            V.tensor_tensor(o, o, rstdg.unsqueeze(2).broadcast_to([P, 8, P]), ALU.mult).then_inc(*done("gla_out", "gated"))

        def gla_low(l):
            for c in range(4):
                dve.wait_ge(*after("gla_out_high", f"out{c | 1}", l))
                V.scalar_tensor_tensor(bT_lo[:, c, :], two(6)[:, c, :], packed(PACK_A, "gla_g")[:, c:c + 1],
                                       flat(bT_hi[:, c, :]), ALU.mult, ALU.subtract).then_inc(
                    *done("gla_out_low", "out" if c == 3 else f"out{c}"))

        def conv_glu(l):
            dve.wait_ge(*after("conv_in", "g", l))
            V.tensor_tensor(conv_u, conv_u, conv_s, ALU.mult).then_inc(*done("conv_glu", "glu"))

        def conv_in(l):
            dve.wait_ge(*after("conv_turned", "u", l))
            V.tensor_copy(uT[:, :, CPAD:CPAD + T], two(6)).then_inc(*done("conv_glu", "u"))
            dve.wait_ge(*after("conv_glu", "u", l))

        def conv_taps(l, first, last):
            w = packed(PACK_A, "conv_w").rearrange("p (c w) -> p c w", c=4)
            for i in range(first, min(last, CW - 1) + 1):
                for c in range(4):
                    src = uT[:, c, i:i + T]
                    if i == 0:
                        V.tensor_scalar(conv_y[:, c, :], src, w[:, c, 0:1], packed(PACK_A, "conv_b")[:, c:c + 1], ALU.mult,
                                        ALU.add).then_inc(*done("conv_taps", f"tap0_{c}"))
                    else:
                        dve.wait_ge(*after("conv_taps", f"tap{i - 1}_{c}", l))
                        V.scalar_tensor_tensor(conv_y[:, c, :], src, w[:, c, i:i + 1], conv_y[:, c, :], ALU.mult,
                                               ALU.add).then_inc(*done("conv_taps", f"tap{i}_{c}"))

        def conv_centre(l):
            dve.wait_ge(*after("conv_rows", "rows", l))
            V.tensor_reduce(cmu, ps[:, 6:8, :], AX.X, ALU.add).then_inc(*done("conv_norm", "sums"))
            dve.wait_ge(*after("conv_norm", "sums", l))
            V.tensor_scalar(cmu, cmu, 1.0 / BW, None, ALU.mult).then_inc(*done("conv_norm", "means"))
            dve.wait_ge(*after("conv_norm", "means", l))
            for t in range(TT):
                V.tensor_scalar(conv_n[:, t, :], ps[:, 6 + t, :], cmu[:, t:t + 1], None,
                                ALU.subtract).then_inc(*done("conv_norm", f"centred{t}"))

        def conv_normed(l):
            for t in range(TT):
                dve.wait_ge(*after("conv_std", f"std{t}", l))
                V.reciprocal(crstd[:, t:t + 1], cstd[:, t:t + 1]).then_inc(*done("conv_norm", f"rstd{t}"))
                dve.wait_ge(*after("conv_norm", f"rstd{t}", l))
                V.tensor_scalar(conv_n[:, t, :], conv_n[:, t, :], crstd[:, t:t + 1], None,
                                ALU.mult).then_inc(*done("conv_norm", f"normed{t}"))

        def conv_low(l):
            dve.wait_ge(*after("conv_out", "high", l))
            V.tensor_tensor(bT_lo[:, 0:4, :], conv_y, flat(bT_hi[:, 0:4, :]), ALU.subtract).then_inc(*done("conv_out_low", "out"))

        def diagonal(w):
            return w.rearrange("p (e b n) -> p e b n", e=2, b=3)[:, :, 0::2, :]

        def mask(name):
            return konst(name).unsqueeze(1).unsqueeze(1).broadcast_to([P, 2, 2, P])

        def sb_keep(l, c):
            dve.wait_ge(*after("sb_weights", f"ln{c}", l))
            V.scalar_tensor_tensor(sb_sp, sb_z, 0.0, sb_e, ALU.max, ALU.add).then_inc(*done("sb_keep", f"softplus{c}"))
            dve.wait_ge(*after("sb_keep", f"softplus{c}", l))
            V.tensor_tensor(diagonal(sb_sp), diagonal(sb_sp), mask("sb_keep"), ALU.mult).then_inc(*done("sb_keep", f"masked{c}"))
            V.tensor_tensor(diagonal(sb_z), diagonal(sb_z), mask("sb_neg"), ALU.add).then_inc(*done("sb_keep", f"barred{c}"))

        def sb_exponent(l, c):
            dve.wait_ge(*after("sb_sums", f"sums{c}", l))
            dve.wait_ge(*after("sb_keep", f"barred{c}", l))
            z = sb_z.rearrange("p (e n) -> p e n", e=2)
            V.tensor_tensor(z, z, ps[:, 6:8, 0:384], ALU.subtract).then_inc(*done("sb_keep", f"exponent{c}"))

        def sb_low(l, c):
            dve.wait_ge(*after("sb_out_high", f"out{c}", l))
            tiles = lambda w: w[:, 4 + c, :].rearrange("p (t n) -> p t n", t=TT)
            V.tensor_tensor(tiles(bT_lo), ps[:, 6:8, 384:512], flat(tiles(bT_hi)),
                            ALU.subtract).then_inc(*done("sb_out_low", f"out{c}"))

        def merge(L, k, i, half):
            l = L.l
            multiplied(L, k)
            dve.wait_ge(*after("gates", f"gate{i}_{half}", l))
            out_, rows = merged[:, :, half * 512:half * 512 + 512], sg[:, half, :, :]
            if i == 0:
                V.tensor_tensor(out_, rows, ps[:, 2 * half:2 * half + 2, :], ALU.mult).then_inc(*done("merge", f"branch{i}_{half}"))
                return
            V.tensor_tensor(rows, rows, ps[:, 2 * half:2 * half + 2, :], ALU.mult).then_inc(*done("merge", f"gated{i}_{half}"))
            dve.wait_ge(*after("merge", f"gated{i}_{half}", l))
            V.tensor_tensor(out_, out_, rows, ALU.add).then_inc(*done("merge", f"branch{i}_{half}"))

        def merged_low(l, kh):
            for t in range(TT):
                dve.wait_ge(*after("merged_high", f"k{kh}t{t}", l))
                tiles = (slice(None), slice(4 * kh, 4 * kh + 4), slice(t * P, (t + 1) * P))
                V.tensor_tensor(hT_lo[tiles], ps[:, 4 + 2 * kh + t, :].rearrange("p (c n) -> p c n", c=4),
                                flat(hT_hi[tiles]), ALU.subtract).then_inc(*done("merged_low", f"k{kh}t{t}"))

        def mixer_a(L):
            l, k = L.l, U_FFN
            norm_in(L, 1)
            gla_rank_rows(L, k + 1)
            gla_rank_turned(l)
            gla_keep(l)
            gla_keys(l)
            gla_states(l)
            conv_glu(l)
            gla_rows(l)
            gla_gated(l)
            conv_in(l)
            taps = [0]

            def some_taps():
                conv_taps(l, taps[0], taps[0] + 1)
                taps[0] += 2

            for _ in range(2):
                some_taps()
            gla_low(l)
            for _ in range(3):
                some_taps()
            k += 17
            for n in range(18):
                i, m = n // 6, n % 6
                if n == 16:
                    conv_low(l)
                if n == 17:
                    merged_low(l, 0)
                if m >= 4:
                    merge(L, k + n, i, m - 4)
                if n % 2 == 0 and 2 <= n <= 8:
                    sb_low(l, n // 2 - 1)
                if n % 2 == 0 and n < 8:
                    sb_keep(l, n // 2)
                if n % 2 == 1 and n < 8:
                    sb_exponent(l, n // 2)
                if n < 11:
                    some_taps()
                if n == 12:
                    conv_centre(l)
                    conv_normed(l)
                if n == 13:
                    prepare(L, 1)
            assert taps[0] >= CW
            merged_low(l, 1)
            norm_out(L, 1, False)

        def memory_rows(l):
            for t in range(TT):
                dve.wait_ge(*after("memory_std", f"std{t}", l))
                V.reciprocal(rstd_mem[:, t:t + 1], std_mem[:, t:t + 1]).then_inc(*done("memory_rows", f"rstd{t}"))
                dve.wait_ge(*after("memory_rows", f"rstd{t}", l))
                V.scalar_tensor_tensor(mem_rows[:, t, :], mem_rows[:, t, :], rstd_mem[:, t:t + 1], mem_g, ALU.mult,
                                       ALU.mult).then_inc(*done("memory_rows", f"normed{t}"))

        def memory_low(l):
            for t in range(TT):
                for kh in range(2):
                    dve.wait_ge(*after("memory_high", f"t{t}k{kh}", l))
                    tiles = (slice(None), slice(4 * kh, 4 * kh + 4), slice(t * P, (t + 1) * P))
                    V.tensor_tensor(bT_lo[tiles], ps[:, 2 * t + kh, :].rearrange("p (c n) -> p c n", c=4),
                                    flat(bT_hi[tiles]), ALU.subtract).then_inc(*done("memory_low", f"t{t}k{kh}"))

        def rope_angles():
            ANGLE, WHOLE, POS = sb_sp[:, 0:64], sb_sp[:, 64:128], sb_sp[:, 128:128 + TT]
            dve.wait_ge(const_loaded, 16 * 2)
            V.tensor_copy(POS, positions).then_inc(*done("rope_angles", "positions"))
            dve.wait_ge(*after("rope_angles", "positions", 0))
            for t in range(TT):
                V.tensor_scalar(ANGLE[:, 32 * t:32 * t + 32], konst("inv_freq"), POS[:, t:t + 1], None,
                                ALU.mult).then_inc(*done("rope_angles", f"angles{t}"))
            dve.wait_ge(*after("rope_angles", f"angles{TT - 1}", 0))
            for name, table, quarter in (("sin", sin, 0.0), ("cos", cos, 0.25)):
                ROUND = 1.5 * 2 ** 23
                steps = [
                    lambda: V.tensor_scalar(WHOLE, ANGLE, 1.0 / (2 * np.pi), quarter, ALU.mult, ALU.add),
                    lambda: V.tensor_scalar(WHOLE, WHOLE, ROUND, None, ALU.add),
                    lambda: V.tensor_scalar(WHOLE, WHOLE, ROUND, None, ALU.subtract),
                    lambda: V.scalar_tensor_tensor(table, WHOLE, -TURN[0], ANGLE, ALU.mult, ALU.add),
                    lambda: V.scalar_tensor_tensor(table, WHOLE, -TURN[1], table, ALU.mult, ALU.add),
                    lambda: V.scalar_tensor_tensor(table, WHOLE, -TURN[2], table, ALU.mult, ALU.add),
                    lambda: V.tensor_scalar(table, table, quarter * 2 * np.pi, PI_BELOW, ALU.add, ALU.min),
                    lambda: V.tensor_scalar(table, table, -PI_BELOW, None, ALU.max)]
                for n, step in enumerate(steps):
                    label = name if n == len(steps) - 1 else f"{name}{n}"
                    step().then_inc(*done("rope_angles", label))
                    dve.wait_ge(*after("rope_angles", label, 0))

        def fox_gate(L):
            l = L.l
            multiplied(L, 1)
            dve.wait_ge(pack_loaded, l * 16 + (16 * DEPTH + 16))
            for t in range(TT):
                V.scalar_tensor_tensor(flog[:, t, :], ps[:, 6, t * 8:t * 8 + 8], rstd_in[:, t:t + 1], packed(PACK_B, "fox_b"),
                                       ALU.mult, ALU.add).then_inc(*done("fox_gate", "logits" if t else "logits0"))
            dve.wait_ge(*after("fox_soft", "ln", l))
            z = flog.rearrange("p t h -> p (t h)")
            V.scalar_tensor_tensor(z, z, 0.0, ftmp, ALU.min, ALU.subtract).then_inc(*done("fox_gate", "log"))

        def fox_sums(l):
            dve.wait_ge(*after("fox_decay", "sums", l))
            V.tensor_copy(fcum.rearrange("p t h -> p (t h)"), ps[:, 7, 0:16]).then_inc(*done("fox_gate", "sums"))
            V.tensor_copy(fcT[0:8, :], ps[0:8, 7, 128:384]).then_inc(*done("fox_gate", "rows0"))
            V.tensor_copy(fcT[64:72, :], ps[64:72, 7, 128:384]).then_inc(*done("fox_gate", "rows"))

        def lru_lambda(l):
            e, s, s2, acc = lru_t, lru_c, stat[:, 100:102], stat[:, 102:104]

            def then(ins, step):
                ins.then_inc(*done("lru_lambda", step))
                dve.wait_ge(*after("lru_lambda", step, l))

            then(V.tensor_scalar(lsp, packed(PACK_B, "lam"), -1.0, 0.0, ALU.mult, ALU.max), "max")
            dve.wait_ge(*after("lru_act", "lambda", l))
            then(V.tensor_scalar(s, e, 2.0, None, ALU.add), "two")
            then(V.reciprocal(s, s), "over")
            then(V.tensor_tensor(s, s, e, ALU.mult), "s")
            then(V.tensor_tensor(s2, s, s, ALU.mult), "s2")
            then(V.tensor_scalar(acc, s2, 1.0 / 17, 1.0 / 15, ALU.mult, ALU.add), "term15")
            for n in range(13, 0, -2):
                then(V.tensor_tensor(acc, acc, s2, ALU.mult), f"times{n}")
                then(V.tensor_scalar(acc, acc, 1.0 / n, None, ALU.add), f"term{n}")
            then(V.tensor_tensor(acc, acc, s, ALU.mult), "half")
            then(V.scalar_tensor_tensor(lsp, acc, 2.0, lsp, ALU.mult, ALU.add), "softplus")
            then(V.tensor_scalar(lsp, lsp, -LRU_C, None, ALU.mult), "scaled")

        def lru_conv(l):
            dve.wait_ge(*after("lru_turned", "xy", l))
            V.tensor_copy(lxT[:, :, PAD2:PAD2 + T], two(4)[:, 0:2, :]).then_inc(*done("lru_turn", "x"))
            V.tensor_copy(lyT.rearrange("p (c t) -> p c t", c=2), two(4)[:, 2:4, :]).then_inc(*done("lru_turn", "y"))
            dve.wait_ge(*after("lru_turn", "x", l))
            w = packed(PACK_B, "conv_w").rearrange("p (c w) -> p c w", c=2)
            for i in range(CW2):
                for c in range(2):
                    src, dst = lxT[:, c, i:i + T], lru[0][:, c * T:(c + 1) * T]
                    if i == 0:
                        V.tensor_scalar(dst, src, w[:, c, 0:1], packed(PACK_B, "conv_b")[:, c:c + 1], ALU.mult,
                                        ALU.add).then_inc(*done("lru_conv", f"tap0_{c}"))
                    else:
                        dve.wait_ge(*after("lru_conv", f"tap{i - 1}_{c}", l))
                        V.scalar_tensor_tensor(dst, src, w[:, c, i:i + 1], dst, ALU.mult,
                                               ALU.add).then_inc(*done("lru_conv", f"tap{i}_{c}"))

        def lru_log(l):
            dve.wait_ge(*after("lru_act", "i1", l))
            for c in range(2):
                r = lru[1][:, c * T:(c + 1) * T]
                V.tensor_scalar(r, r, lsp[:, c:c + 1], None, ALU.mult).then_inc(*done("lru_math", f"log{c}"))
            V.tensor_tensor(lru[2], lru[2], lru[0], ALU.mult).then_inc(*done("lru_math", "ix"))

        def lru_square(l):
            dve.wait_ge(*after("lru_act", "tanh", l))
            dve.wait_ge(*after("lru_math", "ix", l))
            V.tensor_scalar(lru[0], lru[3], -1.0, 1.0, ALU.mult, ALU.add).then_inc(*done("lru_math", "less"))
            dve.wait_ge(*after("lru_math", "less", l))
            V.reciprocal(lru[0], lru[0]).then_inc(*done("lru_math", "over"))
            dve.wait_ge(*after("lru_math", "over", l))
            V.scalar_tensor_tensor(lru[3], lru[3], -2.0, lru[0], ALU.mult, ALU.mult).then_inc(*done("lru_math", "square"))

        def lru_scan(l):
            dve.wait_ge(*after("lru_act", "root", l))
            V.tensor_tensor(lru[2], lru[2], lru[3], ALU.mult).then_inc(*done("lru_math", "u"))
            dve.wait_ge(*after("lru_math", "u", l))
            for c in range(2):
                s = slice(c * T, (c + 1) * T)
                V.tensor_tensor_scan(lru[3][:, s], lru[1][:, s], lru[2][:, s], 0.0, ALU.mult,
                                     ALU.add).then_inc(*done("lru_math", f"scan{c}"))
            dve.wait_ge(*after("lru_math", "scan1", l))
            dve.wait_ge(*after("lru_act", "gelu", l))
            V.tensor_tensor(lru[0], lru[3], lyT, ALU.mult).then_inc(*done("lru_math", "out"))

        def lru_low(l):
            dve.wait_ge(*after("lru_act", "high", l))
            V.tensor_tensor(hT_lo[:, 0:2, :], lru[0].rearrange("p (c t) -> p c t", c=2), flat(hT_hi[:, 0:2, :]),
                            ALU.subtract).then_inc(*done("lru_low", "out"))

        def fox_rows(l, g):
            t, n = g // 2, P * (g // 2 + 1)
            dve.wait_ge(*after("fox_logits", f"logits{g}", l))
            if g:
                dve.wait_ge(*after("fox_p_turned", f"turned{g - 1}", l))
            for i in range(2):
                for e in range(2):
                    b, h = 2 * i + e, 2 * (2 * (g % 2) + i) + e
                    src, decay = ps[:, 6 + e, i * T:i * T + n], fcum[:, t, h:h + 1]
                    label = f"rows{g}" if b == 3 else f"rows{g}_{b}"
                    if t:
                        V.tensor_scalar(fl[:, b, 0:P], src[:, 0:P], decay, None, ALU.add).then_inc(
                            *done("fox_rows", f"early{g}_{b}"))
                    V.scalar_tensor_tensor(fl[:, b, t * P:n], src[:, t * P:n], decay, konst("fox_neg"), ALU.add,
                                           ALU.add).then_inc(*done("fox_rows", label))
            dve.wait_ge(*after("fox_rows", f"rows{g}", l))
            V.tensor_reduce(fmax, fl[:, :, 0:n], AX.X, ALU.max).then_inc(*done("fox_rows", f"top{g}"))
            dve.wait_ge(*after("fox_rows", f"top{g}", l))
            V.tensor_scalar(fmax, fmax, -1.0, None, ALU.mult).then_inc(*done("fox_rows", f"max{g}"))

        def fox_weights(l, g):
            n = P * (g // 2 + 1)
            dve.wait_ge(*after("fox_exp", f"g{g}h3", l))
            V.reciprocal(frd, fden).then_inc(*done("fox_rows", f"over{g}"))
            dve.wait_ge(*after("fox_rows", f"over{g}", l))
            for b in range(4):
                V.tensor_scalar(fl[:, b, 0:n], fl[:, b, 0:n], frd[:, b:b + 1], None, ALU.mult).then_inc(
                    *done("fox_rows", f"weights{g}" if b == 3 else f"weights{g}_{b}"))

        def fox_low(l, g):
            dve.wait_ge(*after("fox_out_high", f"out{g}", l))
            c, t = 2 + 2 * (g % 2), g // 2
            tiles = (slice(None), slice(c, c + 2), slice(t * P, (t + 1) * P))
            V.tensor_tensor(hT_lo[tiles], ps[:, 4, 0:256].rearrange("p (c t) -> p c t", c=2), flat(hT_hi[tiles]),
                            ALU.subtract).then_inc(*done("fox_out_low", f"out{g}"))

        def ret_rope(l):
            dve.wait_ge(*after("ret_in", "qk", l))
            src = rqk.rearrange("p t (h u f) -> p t h u f", h=8, u=2)
            dst = rope.rearrange("p t (h u f) -> p t h u f", h=8, u=2)
            tmp = rsq_f.rearrange("p (t h f) -> p t h f", t=TT, h=8)
            for t in range(TT):
                wave = {"c": cos[:, 32 * t:32 * t + 32].unsqueeze(1).broadcast_to([P, 8, 32]),
                        "s": sin[:, 32 * t:32 * t + 32].unsqueeze(1).broadcast_to([P, 8, 32])}
                for u, (same, other, op) in enumerate((("c", "s", ALU.subtract), ("c", "s", ALU.add))):
                    V.tensor_tensor(dst[:, t, :, u, :], src[:, t, :, u, :], wave[same], ALU.mult).then_inc(
                        *done("ret_rope", f"same{t}{u}"))
                    if u:
                        dve.wait_ge(*after("ret_rope", f"sum{t}0", l))
                    V.tensor_tensor(tmp[:, t, :, :], src[:, t, :, 1 - u, :], wave[other], ALU.mult).then_inc(
                        *done("ret_rope", f"other{t}{u}"))
                    dve.wait_ge(*after("ret_rope", f"other{t}{u}", l))
                    V.tensor_tensor(dst[:, t, :, u, :], dst[:, t, :, u, :], tmp[:, t, :, :], op).then_inc(
                        *done("ret_rope", "rotated" if t and u else f"sum{t}{u}"))

        def ret_turned(l):
            dve.wait_ge(*after("ret_turned", "qk", l))
            V.tensor_copy(rT, two(6)).then_inc(*done("ret_rope", "qkT"))

        def ret_scores(l, c):
            dve.wait_ge(*after("ret_dots", f"dots{c}", l))
            decay = konst("ret_decay").rearrange("p (h n) -> p h n", h=4)[:, 2 * c:2 * c + 2, :]
            s = ret_s[:, 2 * c:2 * c + 2, :]
            V.tensor_tensor(s[:, :, 0:256], ps[:, 6:8, 0:256], decay, ALU.mult).then_inc(*done("ret_scores", f"first{c}"))
            V.tensor_tensor(s[:, :, 256:384], ps[:, 6:8, 256:384], decay[:, :, 0:P], ALU.mult).then_inc(
                *done("ret_scores", f"scores{c}"))

        def ret_norm(l):
            dve.wait_ge(*after("ret_rows", "rows", l))
            y = ry_f.rearrange("p (h v) -> p h v", h=8)
            V.tensor_reduce(rstat3, ps[:, 6, :].rearrange("p (h v) -> p h v", h=8), AX.X, ALU.add).then_inc(
                *done("ret_norm", "totals"))
            dve.wait_ge(*after("ret_norm", "totals", l))
            V.tensor_scalar(rstat3, rstat3, 1.0 / 64, None, ALU.mult).then_inc(*done("ret_norm", "means"))
            dve.wait_ge(*after("ret_norm", "means", l))
            V.tensor_tensor(y, ps[:, 6, :].rearrange("p (h v) -> p h v", h=8),
                            rstat3.unsqueeze(2).broadcast_to([P, 8, 64]), ALU.subtract).then_inc(*done("ret_norm", "centred"))
            dve.wait_ge(*after("ret_norm", "centred", l))
            V.tensor_tensor(rsq_f, ry_f, ry_f, ALU.mult).then_inc(*done("ret_norm", "squares"))
            dve.wait_ge(*after("ret_norm", "squares", l))
            V.tensor_reduce(rstat, rsq_f.rearrange("p (h v) -> p h v", h=8), AX.X, ALU.add).then_inc(*done("ret_norm", "sums"))

        def ret_gated(l):
            dve.wait_ge(*after("ret_std", "std", l))
            V.reciprocal(rstat3, rstat2).then_inc(*done("ret_norm", "over"))
            dve.wait_ge(*after("ret_in", "g", l))
            V.tensor_tensor(ry_f, ry_f, rg_f, ALU.mult).then_inc(*done("ret_norm", "with_g"))
            dve.wait_ge(*after("ret_norm", "with_g", l))
            y = ry_f.rearrange("p (h v) -> p h v", h=8)
            V.tensor_tensor(y, y, rstat3.unsqueeze(2).broadcast_to([P, 8, 64]), ALU.mult).then_inc(*done("ret_norm", "gated"))

        def ret_low(l):
            dve.wait_ge(*after("ret_out_high", "out", l))
            V.tensor_tensor(hT_lo[:, 6:8, :], ps[:, 6, :].rearrange("p (c t) -> p c t", c=2), flat(hT_hi[:, 6:8, :]),
                            ALU.subtract).then_inc(*done("ret_out_low", "out"))

        def mixer_b(L):
            l = L.l
            V.memset(lxT[:, :, 0:PAD2], 0.0).then_inc(*done("lru_turn", "pad"))
            norm_in(L, 0)
            fox_gate(L)
            fox_sums(l)
            lru_lambda(l)
            lru_conv(l)
            fox_rows(l, 0)
            fox_weights(l, 0)
            ret_rope(l)
            fox_rows(l, 1)
            lru_log(l)
            ret_turned(l)
            fox_weights(l, 1)
            lru_square(l)
            fox_low(l, 0)
            ret_scores(l, 0)
            ret_scores(l, 1)
            lru_scan(l)
            fox_low(l, 1)
            fox_rows(l, 2)
            fox_weights(l, 2)
            lru_low(l)
            fox_rows(l, 3)
            fox_weights(l, 3)
            fox_low(l, 2)
            ret_norm(l)
            ret_gated(l)
            ret_low(l)
            fox_low(l, 3)
            prepare(L, 0)
            dve.wait_ge(*after("memory_keys", "k1", l))
            norm_out(L, 0, False)

        def cross(L):
            l = L.l
            norm_in(L, 1)
            for t in range(TT):
                dve.wait_ge(*after("cross_logits", f"logits{t}", l))
                m = cmax[:, 4 * t:4 * t + 4]
                V.tensor_reduce(m, ps[:, 2 * t:2 * t + 2, :].rearrange("p b (h n) -> p (b h) n", h=2), AX.X,
                                ALU.max).then_inc(*done("cross_max", f"top{t}"))
                dve.wait_ge(*after("cross_max", f"top{t}", l))
                V.tensor_scalar(m, m, -1.0, None, ALU.mult).then_inc(*done("cross_max", f"max{t}"))
            for t in range(TT):
                dve.wait_ge(*after("cross_exp", f"t{t}h3", l))
                V.reciprocal(crd[:, 4 * t:4 * t + 4], cden[:, 4 * t:4 * t + 4]).then_inc(*done("cross_rows", f"over{t}"))
                dve.wait_ge(*after("cross_rows", f"over{t}", l))
                for h in range(4):
                    V.tensor_scalar(cp[t][:, h, :], cp[t][:, h, :], crd[:, 4 * t + h:4 * t + h + 1], None,
                                    ALU.mult).then_inc(*done("cross_rows", f"weights{t}" if h == 3 else f"weights{t}_{h}"))
            for c in range(4):
                dve.wait_ge(*after("cross_out_high", f"out{c}", l))
                V.tensor_tensor(hT_lo[:, 2 * c:2 * c + 2, :], ps[:, c, :].rearrange("p (c t) -> p c t", c=2),
                                flat(hT_hi[:, 2 * c:2 * c + 2, :]), ALU.subtract).then_inc(*done("cross_out_low", f"out{c}"))
            prepare(L, 1)
            norm_out(L, 1, False)

        V.memset(uT[:, :, 0:CPAD], 0.0).then_inc(*done("start", "pad"))
        V.memset(lrT[:, :], 1.0).then_inc(*done("start", "ones"))
        dve.wait_ge(*after("start", "ones", 0))
        rope_angles()
        dve.wait_ge(pre_loaded, 16)
        for t in range(TT):
            dve.wait_ge(x_loaded[t], 16)
            for kh in range(2):
                cols = slice(512 * kh, 512 * kh + 512)
                V.tensor_tensor(xn[:, t, cols], x[:, t, cols], pre_g[:, cols], ALU.mult).then_inc(h_ready, 1)
            for kh in range(2):
                low(Layer("A", 0), 0, t, kh)
        V.sem_inc(x_ready, TT)
        dve.wait_ge(const_loaded, 16 * 4)
        with dve.Fori(0, DEPTH) as l:
            L = Layer("A", l)
            ffn(L, 0, 0, 0)
            mixer_a(L)
            ffn(L, 1, 2, U_FFN + U_MIX_A)
        with dve.Fori(0, DEPTH) as l:
            L = Layer("B", l)
            mixer_b(L)
            cross(L)
            ffn(L, 0, 2, U_MIX_B)
        dve.wait_ge(hT_ready, 4 * (6 * DEPTH + 1))

    return S.seen


TURN = (6.28125, 0.0019350051879882812, 2 * np.pi - 6.28125 - 0.0019350051879882812)
PI_BELOW = 3.1415925


_WHOLE = ["x", "ffn1_w_gate", "ffn1_w_up", "ffn1_w_down", "ffn2_w_gate", "ffn2_w_up", "ffn2_w_down", "w_in", "w_branch",
          "w_out", "w_in_2", "w_cq_2", "w_ck_2", "w_cv_2", "w_co_2", "w_out_2", "w_gate_2", "w_up_2", "w_down_2"]


def _layout(inputs):
    get = lambda name: np.ascontiguousarray(np.asarray(inputs[name]))
    arrays = {name: get(name) for name in _WHOLE}
    arrays["w_branch"] = arrays["w_branch"].reshape(DEPTH, 3 * BW, D)
    gains = np.zeros((6 * DEPTH + 1, 2, D), np.float32)
    for l in range(DEPTH):
        for j in range(3):
            gains[3 * l + j, 0], gains[3 * l + j, 1] = get("norm_pre")[l, j], get("norm_post")[l, j]
        for j, name in enumerate(("mix", "cross", "ffn")):
            gains[3 * DEPTH + 3 * l + j, 0] = get(f"pre_{name}_g_2")[l]
            gains[3 * DEPTH + 3 * l + j, 1] = get(f"post_{name}_g_2")[l]
    arrays["gains"] = gains
    arrays["mem"], arrays["mem_g"] = get("mem_2"), get("mem_norm_g_2")[None, :]
    arrays["positions"] = np.ascontiguousarray(get("positions_2").reshape(TT, P).T)
    arrays["const"] = CONST_ARRAY

    def tiles(v):
        v = v.reshape(v.shape[:-1] + (-1, P))
        return np.moveaxis(np.moveaxis(v, -1, 0), -1, 1)

    a = np.zeros((DEPTH, P, PACK_A_W), np.float32)
    b = np.zeros((DEPTH, P, PACK_B_W), np.float32)

    def put(array, table, l, name, value):
        at, w = table[name]
        array[l, :value.shape[0], at:at + w] = value.reshape(value.shape[0], w)

    for l in range(DEPTH):
        put(a, PACK_A, l, "conv_w", tiles(get("conv_w")[l]))
        for name, source in (("conv_b", "conv_b"), ("ln_g", "conv_ln_g"), ("ln_b", "conv_ln_b"), ("gla_g", "gla_norm_g")):
            put(a, PACK_A, l, name, tiles(get(source)[l]))
        put(a, PACK_A, l, "w_alpha", np.concatenate([get("gla_w_alpha")[l], get("gla_b_alpha")[l][None, :]]))
        put(b, PACK_B, l, "conv_w", tiles(get("conv_w_2")[l]))
        for name, source in (("conv_b", "conv_b_2"), ("b_r", "b_rg_2"), ("b_i", "b_ig_2"), ("lam", "lru_lambda_2")):
            put(b, PACK_B, l, name, tiles(get(source)[l]))
        put(b, PACK_B, l, "fox_b", np.repeat(get("fox_b_f_2")[l][None, :], P, axis=0))
        for name, source in (("w_r", "w_rg_2"), ("w_i", "w_ig_2")):
            at, _ = PACK_B[name]
            for n in range(4):
                c, e = n // 2, n % 2
                b[l, 64 * e:64 * e + 64, at + c * P + 64 * e:at + c * P + 64 * e + 64] = get(source)[l, n]
    arrays["pack_a"], arrays["pack_b"] = a, b
    return arrays


def kernel(**inputs):
    import concourse.bacc as _bacc
    from concourse.bass_utils import run_bass_kernel_spmd

    arrays = _layout(inputs)
    counted = None
    for _ in range(2):
        nc = _bacc.Bacc("TRN2", target_bir_lowering=False, num_devices=1)
        d = {name: nc.dram_tensor(f"in_{name}", v.shape, I32 if name == "positions" else F32, kind="ExternalInput").ap()
             for name, v in arrays.items()}
        out = nc.dram_tensor("out", (1, T, D), F32, kind="ExternalOutput").ap()
        counted = build(nc, d, out, counted)
    result = run_bass_kernel_spmd(nc, [{f"in_{name}": v for name, v in arrays.items()}], core_ids=[0])
    return np.asarray(result.results[0]["out"])
```

```python
from contextlib import ExitStack

import numpy as np

import concourse.bass as bass
from concourse import mybir

F32 = mybir.dt.float32
F32R = mybir.dt.float32r
I32 = mybir.dt.int32
ALU = mybir.AluOpType
ACT = mybir.ActivationFunctionType
AX = mybir.AxisListType

P = 128
DEPTH = 2
T = 256
TT = T // P
D = 1024
KD = D // P
F = 2816
FC = 256
NCHUNK = F // FC
RING = 3
AHEAD = 2
PAST = AHEAD + 1
EPS = 1e-6
BW = 512
CW = 31
CPAD = CW - 1
GLA_CHUNK = 64
TAU = 16.0
CW2 = 4
PAD2 = CW2 - 1
LRU_C = 8.0
RANK = 16
NEG = -1e30

U_FFN = 3 * NCHUNK
U_MIX_A = 1 + 2 * 8 + 2 * 6 + 6 + 4
U_LAYER_A = 2 * U_FFN + U_MIX_A
U_MIX_B = 1 + 2 * 6 + 8 + 4 + 8
U_LAYER_B = U_MIX_B + U_FFN
assert U_MIX_A % RING == 0 and U_MIX_B % RING == 0 and U_FFN % RING == 0
UNITS = DEPTH * (U_LAYER_A + U_LAYER_B)

A_LR = 4096
A_CHUNKS = {"gla_qk": 2560, "gla_v": 3072, "gla_r": 3584, "conv_a": 1536, "conv_g": 2048,
            "sb_q": 0, "sb_k": 512, "sb_v": 1024}
A_GATES = 4112
A_SECTIONS = (2, 0, 1)
B_FF = 2048
B_CHUNKS = {"fox_q": 512, "fox_k": 1024, "lru_xy": 0, "fox_v": 1536, "ret_qk": 2056, "ret_vg": 2568}

CONST = {}


def _constants():
    i = np.arange(P)
    parts = {
        "ident": np.eye(P),
        "ones": np.ones((P, P)),
        "tri_ge": (i[:, None] >= i[None, :]) * 1.0,
        "tri_le": (i[:, None] <= i[None, :]) * 1.0,
        "sb_keep": (i[:, None] < i[None, :]) * 1.0,
        "sb_neg": np.where(i[:, None] < i[None, :], 0.0, NEG),
        "gla_suffix": ((i[:, None] > i[None, :]) & (i[:, None] // GLA_CHUNK == i[None, :] // GLA_CHUNK)) * 1.0,
        "gla_chunk": (i[:, None] // GLA_CHUNK == np.arange(2)[None, :]) * 1.0,
        "fox_neg": np.where(i[None, :] <= i[:, None], 0.0, NEG),
    }
    log_gamma = np.log1p(-np.exp2(-5.0 - np.arange(4)))
    diff = np.arange(T)[None, :] - i[:, None]
    decay = np.where(diff[:, None, :] >= 0, np.exp(log_gamma[None, :, None] * np.maximum(diff, 0)[:, None, :]), 0.0)
    parts["ret_decay"] = (decay * 64 ** -0.5).reshape(P, 4 * T)
    freq = (np.float32(10000.0) ** (-np.arange(32, dtype=np.float32) / np.float32(32))).astype(np.float32)
    parts["inv_freq"] = np.tile(freq, (P, 1))
    sel = np.zeros((P, 8, P))
    for h in range(8):
        sel[h, h, :] = -1.0
        sel[64 + h, h, :] = -1.0
    parts["fox_pick"] = sel.reshape(P, 8 * P)
    at = 0
    for name, a in parts.items():
        CONST[name] = (at, a.shape[1])
        at += a.shape[1]
    return np.concatenate([a.astype(np.float32) for a in parts.values()], axis=1)


CONST_ARRAY = _constants()

PACK_A = {"conv_w": (0, 4 * CW), "conv_b": (124, 4), "ln_g": (128, 4), "ln_b": (132, 4), "gla_g": (136, 4),
          "w_alpha": (140, 256), "b_alpha": (396, 256)}
PACK_A_W = 652
PACK_B = {"conv_w": (0, 8), "conv_b": (8, 2), "b_r": (10, 2), "b_i": (12, 2), "lam": (14, 2), "fox_b": (16, 8),
          "w_r": (24, 256), "w_i": (280, 256)}
PACK_B_W = 536


class Signals:

    def __init__(self, make, counted):
        self.make, self.counted = make, counted
        self.sems, self.seen = {}, {}

    def _sem(self, stage):
        if stage not in self.sems:
            self.sems[stage] = self.make(stage)
        return self.sems[stage]

    def done(self, stage, step):
        steps = self.seen.setdefault(stage, [])
        assert step not in steps, (stage, step)
        steps.append(step)
        return self._sem(stage), 1

    def after(self, stage, step, layer):
        steps = self.counted.get(stage) if self.counted else None
        if steps is None:
            assert not self.counted, stage
            return self._sem(stage), layer + 1
        return self._sem(stage), layer * len(steps) + steps.index(step) + 1


def build(nc, d, out, counted):
    with ExitStack() as ctx:
        return _program(ctx, nc, d, out, counted)


def _program(ctx, nc, d, out, counted):
    def sb(name, shape, dt=F32):
        return ctx.enter_context(nc.sbuf_tensor(name, shape, dt))

    def sem(name):
        return ctx.enter_context(nc.semaphore(name))

    S = Signals(sem, counted)
    done, after = S.done, S.after

    ps = ctx.enter_context(nc.psum_tensor("ps", [P, 8, 512], F32))
    x = sb("x", [P, TT, D])
    raw = sb("raw", [P, RING, 2048])
    w_hi = sb("w_hi", [P, RING, 2048], F32R)
    w_lo = sb("w_lo", [P, RING, 2048], F32R)
    hT_hi = sb("hT_hi", [P, KD, T], F32R)
    hT_lo = sb("hT_lo", [P, KD, T], F32R)
    bT_hi = sb("bT_hi", [P, KD + 2, T], F32R)
    bT_lo = sb("bT_lo", [P, KD + 2, T], F32R)
    pre_g = sb("pre_g", [P, D])
    post_g = sb("post_g", [P, D])
    rope_tables = sb("rope_tables", [P, TT * 64])
    const = sb("const", [P, CONST_ARRAY.shape[1]])
    pack = sb("pack", [P, max(PACK_A_W, PACK_B_W)])
    stat = sb("stat", [P, 128])
    SCRATCH = 17200
    scratch = sb("scratch", [P, SCRATCH])

    def konst(name):
        at, w = CONST[name]
        return const[:, at:at + w]

    ident = konst("ident")

    def packed(table, name):
        at, w = table[name]
        return pack[:, at:at + w]

    stat_at = [0]

    def column(n):
        stat_at[0] += n
        return stat[:, stat_at[0] - n:stat_at[0]]

    ss_in, std_in, rstd_in = column(TT), column(TT), column(TT)
    ss_out, bias_out, std_out, rstd_out = column(2 * TT), column(TT), column(TT), column(TT)
    ss_mem, std_mem, rstd_mem = column(TT), column(TT), column(TT)
    root_warm = column(1)

    class Carve:

        def __init__(self, at):
            self.at = at

        def __call__(self, n):
            self.at += n
            assert self.at <= SCRATCH, self.at
            return scratch[:, self.at - n:self.at]

    shared = Carve(0)
    wide = shared(2048)
    xn = wide.rearrange("p (t n) -> p t n", t=TT)
    pairbuf = shared(1024)
    sil = pairbuf[:, 0:512].rearrange("p (t n) -> p t n", t=TT)
    hid = pairbuf[:, 512:1024].rearrange("p (t n) -> p t n", t=TT)

    a_mem = Carve(shared.at)
    gqk_f, gv_f, gr_f, gqT_f = a_mem(1024), a_mem(1024), a_mem(1024), a_mem(512)
    gqk = gqk_f.rearrange("p (t n) -> p t n", t=TT)
    gv = gv_f.rearrange("p (t n) -> p t n", t=TT)
    gr = gr_f.rearrange("p (t n) -> p t n", t=TT)
    gqT = gqT_f.rearrange("p (c t) -> p c t", c=2)
    sbqT = gqk_f.rearrange("p (c t) -> p c t", c=4)
    sbkT = gv_f.rearrange("p (c t) -> p c t", c=4)
    sbv = gr
    uT = a_mem(4 * (T + CPAD)).rearrange("p (c t) -> p c t", c=4)
    conv_y_f = a_mem(1024)
    conv_y = conv_y_f.rearrange("p (c t) -> p c t", c=4)
    sb_sp = a_mem(768)
    sg = a_mem(2048).rearrange("p (h t n) -> p h t n", h=2, t=TT)
    merged_f = a_mem(2048)
    merged = merged_f.rearrange("p (t n) -> p t n", t=TT)
    lrT = a_mem(256)
    lam = a_mem(8).rearrange("p (c n) -> p c n", c=2)
    nla, gdec = pairbuf[:, 0:512], pairbuf[:, 512:1024]
    gstate = sg[:, 0, :, :].rearrange("p t n -> p (t n)").rearrange("p (c n v) -> p c n v", c=2, n=4)
    go_f, gsq_f = merged_f[:, 0:1024], merged_f[:, 1024:2048]
    conv_u = wide[:, 0:1024].rearrange("p (t n) -> p t n", t=TT)
    conv_s = wide[:, 1024:2048].rearrange("p (t n) -> p t n", t=TT)
    sb_q, sb_k = conv_u, conv_s
    sb_z, sb_e = wide[:, 0:768], wide[:, 768:1536]
    conv_n = pairbuf.rearrange("p (t n) -> p t n", t=TT)
    ssg, stdg, rstdg = column(8), column(8), column(8)
    cmu, css, cstd, crstd = column(TT), column(TT), column(TT), column(TT)

    b_mem = Carve(shared.at)
    fqk_f = b_mem(2048)
    fq = fqk_f[:, 0:1024].rearrange("p (t n) -> p t n", t=TT)
    fk = fqk_f[:, 1024:2048].rearrange("p (t n) -> p t n", t=TT)
    rqk = fq
    rope = fk
    ret_s = fqk_f.rearrange("p (h n) -> p h n", h=4)
    fqkT_f = b_mem(2048)
    fqT = fqkT_f[:, 0:1024].rearrange("p (c t) -> p c t", c=4)
    fkT = fqkT_f[:, 1024:2048].rearrange("p (c t) -> p c t", c=4)
    kmT = fqkT_f.rearrange("p (c m) -> p c m", c=KD)
    fvrT_f = b_mem(2048)
    fv_f, rT_f = fvrT_f[:, 0:1024], fvrT_f[:, 1024:2048]
    fv = fv_f.rearrange("p (t n) -> p t n", t=TT)
    rT = rT_f.rearrange("p (c t) -> p c t", c=4)
    rv_f, rg_f = b_mem(512), b_mem(512)
    rv = rv_f.rearrange("p (t n) -> p t n", t=TT)
    rg = rg_f.rearrange("p (t n) -> p t n", t=TT)
    fl_f = b_mem(1024)
    fl = fl_f.rearrange("p (h s) -> p h s", h=4)
    fpT_f = b_mem(1024)
    fpT = fpT_f.rearrange("p (b t) -> p b t", b=8)
    vm = b_mem(2048).rearrange("p (m n) -> p m n", m=TT)
    lxT = b_mem(2 * (T + PAD2)).rearrange("p (c t) -> p c t", c=2)
    lyT = b_mem(512)
    flog, fcum = b_mem(16).rearrange("p (t h) -> p t h", t=TT), b_mem(16).rearrange("p (t h) -> p t h", t=TT)
    ftmp = b_mem(16)
    fcT = b_mem(256)
    sin, cos = rope_tables[:, 0:64], rope_tables[:, 64:128]
    lru_c, lru_t, lsp = column(2), column(2), column(2)
    fmax, fden, frd = column(4), column(4), column(4)
    rstat, rstat2, rstat3 = column(8), column(8), column(8)
    lxy = pairbuf.rearrange("p (t n) -> p t n", t=TT)
    ry_f, rsq_f = pairbuf[:, 0:512], pairbuf[:, 512:1024]
    lru = [wide[:, 512 * n:512 * n + 512] for n in range(4)]
    km = xn
    cq = xn
    cqT = fqk_f.rearrange("p (c t) -> p c t", c=KD)
    cp = [fl_f.rearrange("p (h m) -> p h m", h=4), fpT_f.rearrange("p (h m) -> p h m", h=4)]
    cpT = [fvrT_f[:, 512 * g:512 * g + 512] for g in range(4)]
    cmax, cden, crd = column(8), column(8), column(8)

    both_a, both_b = gr_f, fl_f
    x_pre = fqk_f.rearrange("p (t n) -> p t n", t=TT)
    out_a = sg.rearrange("p h t n -> p (h t n)").rearrange("p (t n) -> p t n", t=TT)
    out_b = fvrT_f.rearrange("p (t n) -> p t n", t=TT)
    mem_rows, mem_g, mem_sq = merged, conv_y_f, pairbuf
    positions = ctx.enter_context(nc.sbuf_tensor("positions", [P, TT], I32))[:, :]

    raw_landed = [sem(f"raw_landed{i}") for i in range(RING)]
    high_ready, low_ready, unit_done = sem("high_ready"), sem("low_ready"), sem("unit_done")
    pre_loaded, post_loaded, pack_loaded = sem("pre_gain_loaded"), sem("post_gain_loaded"), sem("pack_loaded")
    ident_loaded, x_loaded = sem("ident_loaded"), [sem(f"x_loaded{t}") for t in range(TT)]
    x_ready, sq_in, std_ready, rstd_ready = sem("x_ready"), sem("sq_in"), sem("std_ready"), sem("rstd_ready")
    h_ready, h_turned, hT_hi_ready, hT_ready = sem("h_ready"), sem("h_turned"), sem("hT_hi_ready"), sem("hT_ready")
    sq_out, sq_bias, std_out_ready, rstd_out_ready = sem("sq_out"), sem("sq_bias"), sem("std_out"), sem("rstd_out")
    out_copied, prepared, weighted, scaled = sem("out_copied"), sem("prepared"), sem("out_weighted"), sem("out_scaled")
    ffn_out, root_loaded, const_loaded = sem("ffn_out"), sem("root_loaded"), sem("const_loaded")
    silu_ready, hid_ready, hid_turned = sem("silu_ready"), sem("hid_ready"), sem("hid_turned")
    gT_hi_ready, gT_ready = sem("gT_hi_ready"), sem("gT_ready")
    stored, memory_loaded = sem("stored"), sem("memory_loaded")
    raw_free, pe_free = sem("raw_free"), sem("pe_free")

    CREDIT = RING

    class Layer:

        def __init__(self, block, l):
            self.l = l
            self.b = block == "B"
            self.unit0 = l * U_LAYER_B + DEPTH * U_LAYER_A if self.b else l * U_LAYER_A
            self.turn0 = l * (U_LAYER_B // RING) + DEPTH * U_LAYER_A // RING if self.b else l * (U_LAYER_A // RING)
            self.sub0 = l * 3 + 3 * DEPTH if self.b else l * 3

        def done_units(self, k):
            return self.unit0 + (k + 1 + CREDIT)

        def turn(self, k):
            return self.turn0 + (k // RING + 1)

        def ffn(self, n):
            return self.l + 2 * DEPTH if self.b else self.l * 2 + n

        def sub(self, j, per, n):
            return self.sub0 * per + (per * j + n)

    class Chunk(Layer):

        def __init__(self, L, c):
            self.l, self.b, self.sub0 = L.l, L.b, L.sub0
            self.unit0 = L.unit0 + (c - 2) * RING
            self.turn0 = L.turn0 + (c - 2)

    def cross_bank(g):
        return 2 * g if g < 2 else 2 + g

    block = ctx.enter_context(nc.Block())

    @block.sync
    def _(sp):
        def unit(L, k, halves):
            sp.wait_ge(low_ready, L.unit0 + (k + 1))
            sp.sem_inc(raw_free, 1)
            for dst, src in halves:
                sp.dma_start(dst, src).then_inc(raw_landed[k % RING], 16)

        def rows(w, l, k0, n, c0, width):
            return w[bass.ds(l, 1), k0:k0 + n * P, c0:c0 + width].rearrange("o (k p) n -> p (o k) n", p=P)

        def square(L, k, w, k0, c0):
            dst = raw[:, k % RING, :].rearrange("p (k n) -> p k n", k=4)
            unit(L, k, [(dst[:, 2 * i:2 * i + 2, :], rows(w, L.l, k0 + 2 * P * i, 2, c0, 512)) for i in range(2)])

        def narrow(L, k, w, c0, width):
            dst = raw[:, k % RING, 0:KD * width].rearrange("p (k n) -> p k n", k=KD)
            unit(L, k, [(dst[:, 4 * i:4 * i + 4, :], rows(w, L.l, 512 * i, 4, c0, width)) for i in range(2)])

        def gate_up(L, k, kh, wg, wu, c):
            dst = raw[:, k % RING, :].rearrange("p (k g n) -> p k g n", k=4, g=2)
            halves = []
            for g, w in enumerate((wg, wu)):
                src = w[bass.ds(L.l, 1), 512 * kh:512 * kh + 512, bass.ds(c * FC, FC)]
                halves.append((dst[:, :, g, :], src.rearrange("o (k p) n -> p (o k) n", p=P)))
            unit(L, k, halves)

        def down(L, k, wd, c):
            dst = raw[:, k % RING, :].rearrange("p (k n) -> p k n", k=2)
            src = wd[bass.ds(L.l, 1), bass.ds(c * FC, FC), :].rearrange("o (k p) n -> p (o k) n", p=P)
            unit(L, k, [(dst[:, i:i + 1, :], src[:, i:i + 1, :]) for i in range(2)])

        def ffn(L, k0, wg, wu, wd):
            for kh in range(2):
                gate_up(L, k0 + kh, kh, wg, wu, 0)

            def chunk(c, k, L=L):
                gate_up(L, k, 0, wg, wu, c)
                gate_up(L, k + 1, 1, wg, wu, c)
                down(L, k + 2, wd, c - 1)

            chunk(1, k0 + 2)
            with sp.Fori(2, NCHUNK - 1) as c:
                chunk(c, k0 + 5, Chunk(L, c))
            chunk(NCHUNK - 1, k0 + U_FFN - 4)
            down(L, k0 + U_FFN - 1, wd, NCHUNK - 1)

        with sp.Fori(0, DEPTH) as l:
            L = Layer("A", l)
            ffn(L, 0, d["ffn1_w_gate"], d["ffn1_w_up"], d["ffn1_w_down"])
            k = U_FFN
            for n, c0 in enumerate(A_CHUNKS.values()):
                for kh in range(2):
                    square(L, k, d["w_in"], 512 * kh, c0)
                    k += 1
                    if (n, kh) == (0, 0):
                        narrow(L, k, d["w_in"], A_LR, RANK)
                        k += 1
            for b in A_SECTIONS:
                for half in range(2):
                    for kh in range(2):
                        square(L, k, d["w_in"], 512 * kh, A_GATES + b * D + 512 * half)
                        k += 1
                for half in range(2):
                    square(L, k, d["w_branch"], b * BW, 512 * half)
                    k += 1
            for kh in range(2):
                for half in range(2):
                    square(L, k, d["w_out"], 512 * kh, 512 * half)
                    k += 1
            assert k == U_FFN + U_MIX_A
            ffn(L, k, d["ffn2_w_gate"], d["ffn2_w_up"], d["ffn2_w_down"])
        with sp.Fori(0, DEPTH) as l:
            L = Layer("B", l)
            k = 0
            for n, c0 in enumerate(B_CHUNKS.values()):
                for kh in range(2):
                    square(L, k, d["w_in_2"], 512 * kh, c0)
                    k += 1
                    if (n, kh) == (0, 0):
                        narrow(L, k, d["w_in_2"], B_FF, 8)
                        k += 1
            for name in ("w_cv_2", "w_ck_2"):
                for half in range(2):
                    for kh in range(2):
                        square(L, k, d[name], 512 * kh, 512 * half)
                        k += 1
            for name in ("w_out_2", "w_cq_2", "w_co_2"):
                for kh in range(2):
                    for half in range(2):
                        square(L, k, d[name], 512 * kh, 512 * half)
                        k += 1
            assert k == U_MIX_B
            ffn(L, k, d["w_gate_2"], d["w_up_2"], d["w_down_2"])
        last = Layer("B", DEPTH)
        for k in range(PAST):
            dst = raw[:, k, :].rearrange("p (k n) -> p k n", k=4)
            src = d["w_co_2"][DEPTH - 1, 0:512, 0:512].rearrange("(k p) n -> p k n", p=P)
            unit(last, k, [(dst[:, 2 * i:2 * i + 2, :], src[:, 2 * i:2 * i + 2, :]) for i in range(2)])
        for t in range(TT):
            sp.wait_ge(x_ready, 2 * 6 * DEPTH + t + 1)
            sp.dma_start(out[0, t * P:(t + 1) * P, :], x[:, t, :]).then_inc(stored, 16)
        sp.wait_ge(stored, 16 * TT)

    @block.gpsimd
    def _(pool):
        nc.gpsimd.sem_inc(low_ready, 1)
        pool.wait_ge(x_loaded[0], 16)
        nc.gpsimd.sem_inc(low_ready, CREDIT - 1)
        total = UNITS + PAST

        def low(slot, u):
            pool.wait_ge(high_ready, u + 1)
            nc.gpsimd.tensor_tensor(w_lo[:, slot, :], raw[:, slot, :], w_hi[:, slot, :].bitcast(F32),
                                    ALU.subtract).then_inc(low_ready, 1)

        with pool.Fori(0, total // RING) as r:
            for slot in range(RING):
                low(slot, r * RING + slot)
        for slot in range(total % RING):
            low(slot, total - total % RING + slot)

    @block.tensor
    def _(pe):
        def products(left, tiles, slot, view, bank, start, stop, before=None, halves=1, mark=None):
            hi, lo = left
            parts = [view(w[:, slot, :]) for w in (w_hi, w_lo)]
            passes = ((hi, 0), (hi, 1), (lo, 0))
            for t in range(TT):
                for half in range(halves):
                    for i, k in enumerate(tiles):
                        if before:
                            before(t, half * len(tiles) + i)
                        for n, (act, part) in enumerate(passes):
                            w = parts[part][:, i, :]
                            if halves > 1:
                                w = w[:, 512 * half:512 * half + 512]
                            mm = nc.tensor.matmul(bank(t, half), act[:, k, t * P:(t + 1) * P], w,
                                                  start=start and i == 0 and n == 0,
                                                  stop=stop and i == len(tiles) - 1 and n == 2)
                    if mark and (t, half) != (TT - 1, halves - 1):
                        mm.then_inc(*mark(t))
            return mm

        def weights(L, k):
            pe.wait_ge(low_ready, L.done_units(k))

        by4 = lambda w: w.rearrange("p (k n) -> p k n", k=4)
        by2 = lambda w: w.rearrange("p (k n) -> p k n", k=2)
        hT, bT = (hT_hi, hT_lo), (bT_hi, bT_lo)

        def first(wait):
            return lambda t, i: wait(t) if i == 0 else None

        def left_ready(L, j, kh):
            return first(lambda t: pe.wait_ge(hT_ready, L.sub(j, 4, 2 * t + kh + 1)))

        def rows_follow(L, j):
            def before(t, i):
                if (t, i) in ((0, 2), (1, 0)):
                    norm_turn(L, j, 1, t)
                left_ready(L, j, 0)(t, i)
            return before

        def square(L, k, left, first, bank, start, stop, before=None, mark=None):
            weights(L, k)
            products(left, range(first, first + 4), k % RING, by4, bank, start, stop, before, 1,
                     mark).then_inc(unit_done, 1)

        def norm_turn(L, j, t, kh):
            pe.wait_ge(h_ready, L.sub(j, 4, 2 * t + kh + 1))
            for c in range(4):
                mm = nc.tensor.transpose(ps[:, 6 - 2 * t + kh, c * P:(c + 1) * P],
                                         xn[:, t, (4 * kh + c) * P:(4 * kh + c + 1) * P], ident)
            mm.then_inc(h_turned, 1)

        def rows_lead(L, j, before=lambda t, i: None):
            def step(t, i):
                before(t, i)
                if (t, i) == (TT - 1, 3):
                    norm_turn(L, j, 0, 0)
            return step

        def rows_led(L, j):
            norm_turn(L, j, 0, 1)

        def banks_free(L, j, t):
            pe.wait_ge(out_copied, L.sub(j, 2, t + 1))

        def turn(src, banks, blocks=4):
            for c in range(blocks):
                for t in range(TT):
                    at = (c % 2) * T + t * P
                    mm = nc.tensor.transpose(ps[:, banks + c // 2, at:at + P], src[:, t, c * P:(c + 1) * P], ident)
            return mm

        def ffn(L, n, j, k0):
            f = L.ffn(n)
            early, mid = lambda t, half: ps[:, t, :], lambda t, half: ps[:, 6 + t, :]
            acc = lambda t, half: ps[:, 2 * t + half, :]

            def gate_up(M, k):
                for kh in range(2):
                    square(M, k + kh, hT, 4 * kh, mid, kh == 0, kh == 1)

            def hidden(c):
                pe.wait_ge(hid_ready, f * NCHUNK + (c + 1))
                for i in range(2):
                    for t in range(TT):
                        mm = nc.tensor.transpose(ps[:, 4, i * T + t * P:i * T + (t + 1) * P],
                                                 hid[:, t, i * P:(i + 1) * P], ident)
                mm.then_inc(hid_turned, 1)

            def down(M, k, c, start, before=None, left=bT, tiles=(KD, KD + 1), mark=None):
                weights(M, k)
                pe.wait_ge(gT_ready, f * NCHUNK + (c + 1))
                products(left, tiles, k % RING, by2, acc, start, mark is not None, before, 2, mark).then_inc(unit_done, 1)

            banks_free(L, j, 0)
            square(L, k0, hT, 0, early, True, False, rows_follow(L, j))
            square(L, k0 + 1, hT, 4, early, False, True, left_ready(L, j, 1))
            square(L, k0 + 2, hT, 0, mid, True, False)
            hidden(0)
            banks_free(L, j, 1)
            if n:
                memory_turn(L.l)
            square(L, k0 + 3, hT, 4, mid, False, True)
            if n:
                pe.wait_ge(*after("memory_low", "t1k1", L.l))
            down(L, k0 + 4, 0, True)
            with pe.Fori(2, NCHUNK - 1) as c:
                M = Chunk(L, c)
                hidden(c - 1)
                gate_up(M, k0 + 5)
                down(M, k0 + 7, c - 1, False)
            end, c = k0 + U_FFN - 1, NCHUNK - 1
            hidden(c - 1)
            gate_up(L, end - 3)
            down(L, end - 1, c - 1, False, first(lambda t: hidden(c) if t else None))
            down(L, end, c, False, rows_lead(L, j + 1), hT, (0, 1), lambda t: (ffn_out, 1))
            rows_led(L, j + 1)

        def pair(n):
            return lambda t, half: ps[:, 2 * (n % 2) + t, :]

        def narrow(L, k, width, j):
            weights(L, k)
            pe.wait_ge(hT_ready, L.sub(j, 4, 4))
            view = lambda w: w[:, k % RING, 0:KD * width].rearrange("p (k n) -> p k n", k=KD)
            passes = ((hT_hi, view(w_hi)), (hT_hi, view(w_lo)), (hT_lo, view(w_hi)))
            for i in range(KD):
                for n, (act, w) in enumerate(passes):
                    mm = nc.tensor.matmul(ps[0:width, 6, 0:T], w[:, i, :], act[:, i, :], start=i == 0 and n == 0,
                                          stop=i == KD - 1 and n == 2)
            mm.then_inc(unit_done, 1)

        def gla_alpha(l):
            pe.wait_ge(const_loaded, 16 * 4)
            pe.wait_ge(*after("gla_rank", "turned", l))
            pe.wait_ge(pack_loaded, l * 16 + 16)
            for t in range(TT):
                mm = nc.tensor.matmul(ps[:, 7, t * T:(t + 1) * T], lrT[0:RANK, t * P:(t + 1) * P],
                                      packed(PACK_A, "w_alpha")[0:RANK, :], start=True, stop=True)
            mm.then_inc(*done("gla_alpha", "logits"))

        def gla_decays(l):
            pe.wait_ge(*after("gla_in", "qk", l))
            for c in range(2):
                for t in range(TT):
                    mm = nc.tensor.transpose(ps[:, 6, c * T + t * P:c * T + (t + 1) * P], gqk[:, t, c * P:(c + 1) * P],
                                             ident)
            mm.then_inc(*done("gla_turned", "q"))
            pe.wait_ge(*after("gla_keep", "softplus", l))
            for t in range(TT):
                nc.tensor.matmul(ps[:, 4, t * T:(t + 1) * T], konst("gla_suffix"), nla[:, t * T:(t + 1) * T],
                                 start=True, stop=True)
            for c in range(2):
                for t in range(TT):
                    mm = nc.tensor.matmul(ps[:, 5, 4 * c + 2 * t:4 * c + 2 * t + 2],
                                          nla[:, t * T + c * P:t * T + (c + 1) * P], konst("gla_chunk"),
                                          start=True, stop=True)
            mm.then_inc(*done("gla_sums", "sums"))

        def gla_updates(l):
            pe.wait_ge(*after("gla_decay", "keys", l))
            pe.wait_ge(*after("gla_in", "v", l))
            pe.wait_ge(*after("gla_decay", "q", l))
            pe.sem_inc(pe_free, 1)
            for half in range(2):
                rows = slice(64 * half, 64 * half + 64)
                for t in range(TT):
                    for c in range(2):
                        for e in range(2):
                            h = 2 * c + e
                            mm = nc.tensor.matmul(
                                ps[64 * e:64 * e + 64, 6 + half, (2 * c + t) * P:(2 * c + t + 1) * P],
                                gdec[rows, t * T + h * 64:t * T + h * 64 + 64], gv[rows, t, h * P:(h + 1) * P],
                                start=True, stop=True)
            mm.then_inc(*done("gla_updates", "updates"))

        def gla_reads(l):
            pe.wait_ge(*after("gla_state", "last", l))
            pe.sem_inc(pe_free, 1)
            for e in range(2):
                rows = slice(64 * e, 64 * e + 64)
                for n in range(4):
                    t, half = n // 2, n % 2
                    for c in range(2):
                        mm = nc.tensor.matmul(
                            ps[64 * half:64 * half + 64, 4 + e, (2 * t + c) * P:(2 * t + c + 1) * P],
                            gqT[rows, c, n * 64:n * 64 + 64], gstate[rows, c, n, :], start=True, stop=True)
            mm.then_inc(*done("gla_reads", "reads"))

        def conv_turn(l):
            pe.wait_ge(*after("conv_glu", "glu", l))
            turn(conv_u, 6).then_inc(*done("conv_turned", "u"))

        def sb_turn_q(l):
            pe.wait_ge(*after("sb_in", "q", l))
            pe.wait_ge(*after("gla_out", "rows", l))
            turn(sb_q, 4).then_inc(*done("sb_turned", "q"))

        def gla_turn(l):
            pe.wait_ge(*after("gla_out", "gated", l))
            pe.wait_ge(*after("conv_glu", "u", l))
            turn(go_f.rearrange("p (t n) -> p t n", t=TT), 6).then_inc(*done("gla_out_turned", "turned"))

        def sb_turn_k(l):
            pe.wait_ge(*after("sb_in", "k", l))
            pe.wait_ge(*after("sb_in", "qT", l))
            turn(sb_k, 4).then_inc(*done("sb_turned", "k"))

        def sb_logits(l, c):
            pe.wait_ge(*after("sb_in", "kT", l))
            if c:
                pe.wait_ge(*after("sb_keep", f"copied{c - 1}", l))
            for e in range(2):
                r = slice(64 * e, 64 * e + 64)
                nc.tensor.matmul(ps[:, 4 + e, 0:256], sbkT[r, c, 0:P], sbqT[r, c, :], start=True, stop=True)
                mm = nc.tensor.matmul(ps[:, 4 + e, 256:384], sbkT[r, c, P:T], sbqT[r, c, P:T], start=True, stop=True)
            mm.then_inc(*done("sb_logits", f"logits{c}"))

        def sb_sums(l, c):
            pe.wait_ge(*after("sb_keep", f"masked{c}", l))
            if c:
                pe.wait_ge(*after("sb_keep", f"exponent{c - 1}", l))
                pe.wait_ge(*after("sb_out_low", f"out{c - 1}", l))
            else:
                pe.wait_ge(*after("gla_out_low", "out", l))
            for e in range(2):
                s = sb_sp[:, e * 384:(e + 1) * 384]
                nc.tensor.matmul(ps[:, 6 + e, 256:384], konst("tri_ge"), s[:, 256:384], start=True, stop=True)
                nc.tensor.matmul(ps[:, 6 + e, 0:256], konst("tri_ge"), s[:, 0:256], start=True, stop=False)
                mm = nc.tensor.matmul(ps[:, 6 + e, P:256], konst("ones"), s[:, 256:384], start=False, stop=True)
            mm.then_inc(*done("sb_sums", f"sums{c}"))

        def sb_out(l, c):
            pe.wait_ge(*after("sb_weights", f"weights{c}", l))
            for e in range(2):
                w = sb_e[:, e * 384:(e + 1) * 384]
                r, h = slice(64 * e, 64 * e + 64), 2 * c + e
                v = sbv[:, :, h * 64:h * 64 + 64]
                nc.tensor.matmul(ps[r, 6, 384:512], v[:, 0, :], w[:, 0:P], start=True, stop=True)
                nc.tensor.matmul(ps[r, 7, 384:512], v[:, 0, :], w[:, P:256], start=True, stop=False)
                mm = nc.tensor.matmul(ps[r, 7, 384:512], v[:, 1, :], w[:, 256:384], start=False, stop=True)
            mm.then_inc(*done("sb_out", f"out{c}"))

        def conv_rows(l):
            pe.wait_ge(*after("conv_taps", f"tap{CW - 1}_3", l))
            pe.wait_ge(*after("sb_out_low", "out3", l))
            for t in range(TT):
                for c in range(4):
                    mm = nc.tensor.transpose(ps[:, 6 + t, c * P:(c + 1) * P], conv_y[:, c, t * P:(t + 1) * P], ident)
            mm.then_inc(*done("conv_rows", "rows"))

        def conv_normed(l):
            pe.wait_ge(*after("conv_norm", "normed1", l))
            pe.wait_ge(*after("sb_keep", "copied3", l))
            turn(conv_n, 4).then_inc(*done("conv_normed", "turned"))

        def merged_turn(l, kh):
            if kh == 0:
                pe.wait_ge(*after("conv_out", "act3", l))
            pe.wait_ge(*after("merge", f"branch2_{kh}", l))
            for t in range(TT):
                for c in range(4):
                    mm = nc.tensor.transpose(ps[:, 4 + 2 * kh + t, c * P:(c + 1) * P],
                                             merged[:, t, (4 * kh + c) * P:(4 * kh + c + 1) * P], ident)
                mm.then_inc(*done("merged_turned", f"k{kh}t{t}"))

        def mixer_a(L):
            l, k = L.l, U_FFN
            evicted = list(A_CHUNKS)
            steps = {("gla_v", 1): [gla_alpha], ("gla_r", 1): [gla_decays],
                     ("conv_a", 1): [gla_updates], ("conv_g", 1): [gla_reads], ("sb_q", 0): [conv_turn],
                     ("sb_k", 0): [sb_turn_q], ("sb_k", 1): [gla_turn], ("sb_v", 0): [sb_turn_k]}
            for n, name in enumerate(evicted):
                if n < 2:
                    banks_free(L, 1, n)
                else:
                    prev = evicted[n - 2]
                    pe.wait_ge(*after(f"{prev.split('_')[0]}_in", prev.split("_")[1], l))
                for kh in range(2):
                    square(L, k, hT, 4 * kh, pair(n), kh == 0, kh == 1, rows_follow(L, 1) if (n, kh) == (0, 0) else None)
                    k += 1
                    if (n, kh) == (0, 0):
                        narrow(L, k, RANK, 1)
                        k += 1
                    for step in steps.get((name, kh), ()):
                        step(l)
            first_of_branch = {2: 0, 0: 4, 1: 0}
            for i, b in enumerate(A_SECTIONS):
                for half in range(2):
                    if i:
                        pe.wait_ge(*after("merge", f"branch{i - 1}_{half}", l))
                    else:
                        pe.wait_ge(*after("sb_in", "v" if half else "k", l))
                    for kh in range(2):
                        square(L, k, hT, 4 * kh, pair(half), kh == 0, kh == 1)
                        k += 1
                        n = 6 * i + 2 * half + kh
                        if n % 2 == 0 and 2 <= n <= 8:
                            sb_out(l, n // 2 - 1)
                        if n % 2 == 0 and n < 8:
                            sb_logits(l, n // 2)
                        if n % 2 == 1 and n < 8:
                            sb_sums(l, n // 2)
                        if n == 13:
                            conv_normed(l)
                pe.wait_ge(*after(("gla_out_low", "sb_out_low", "conv_out_low")[i], ("out", "out3", "out")[i], l))
                for half in range(2):
                    pe.wait_ge(*after("gates", f"gate{i}_{half}", l))
                    square(L, k, bT, first_of_branch[b], pair(half), True, True,
                           first(lambda t: merged_turn(l, 0) if t else None) if i == 2 and half else None)
                    k += 1
                    n = 6 * i + 4 + half
                    if n in (4,):
                        sb_out(l, 1)
                        sb_logits(l, 2)
                    if n == 5:
                        sb_sums(l, 2)
                    if n == 11:
                        conv_rows(l)
            def before(kh, half):
                def wait(t):
                    pe.wait_ge(*after("merged_low", f"k{kh}t{t}", l))
                    if t:
                        pe.wait_ge(*after("merge", "branch2_1", l))
                return first(wait)

            for kh in range(2):
                for half in range(2):
                    square(L, k, hT, 4 * kh, lambda t, _, half=half: ps[:, 2 * t + half, :], kh == 0, kh == 1,
                           rows_lead(L, 2, before(kh, half)) if kh and half else before(kh, half),
                           (lambda t: done("mix_a_out", "t0")) if kh and half else None)
                    k += 1
                    if (kh, half) == (0, 0):
                        merged_turn(l, 1)
            rows_led(L, 2)

        def memory_turn(l):
            for t in range(TT):
                pe.wait_ge(*after("memory_rows", f"normed{t}", l))
                for kh in range(2):
                    for c in range(4):
                        mm = nc.tensor.transpose(ps[:, 2 * t + kh, c * P:(c + 1) * P],
                                                 mem_rows[:, t, (4 * kh + c) * P:(4 * kh + c + 1) * P], ident)
                    mm.then_inc(*done("memory_turned", f"t{t}k{kh}"))

        def fox_forget(l):
            pe.wait_ge(*after("fox_gate", "copied", l))
            pe.sem_inc(pe_free, 1)
            for t in range(TT):
                mm = nc.tensor.transpose(ps[:, 6, T + 8 * t:T + 8 * t + 8], fcT[0:8, t * P:(t + 1) * P], ident[0:8, 0:8])
            mm.then_inc(*done("fox_forget", "turned"))

        def fox_decay(l):
            pe.wait_ge(*after("fox_gate", "log", l))
            nc.tensor.matmul(ps[:, 7, 0:8], konst("tri_le"), flog[:, 0, :], start=True, stop=True)
            nc.tensor.matmul(ps[:, 7, 8:16], konst("ones"), flog[:, 0, :], start=True, stop=False)
            nc.tensor.matmul(ps[:, 7, 8:16], konst("tri_le"), flog[:, 1, :], start=False, stop=True)
            for r in (0, 64):
                nc.tensor.matmul(ps[r:r + 8, 7, 128:256], flog[:, 0, :], konst("tri_le"), start=True, stop=True)
                nc.tensor.matmul(ps[r:r + 8, 7, 256:384], flog[:, 0, :], konst("ones"), start=True, stop=False)
                mm = nc.tensor.matmul(ps[r:r + 8, 7, 256:384], flog[:, 1, :], konst("tri_le"), start=False, stop=True)
            mm.then_inc(*done("fox_decay", "sums"))

        def fox_turn(l, which):
            pe.wait_ge(*after("fox_in", which, l))
            if which == "k":
                pe.wait_ge(*after("fox_gate", "rows", l))
            turn(fq if which == "q" else fk, 4 if which == "q" else 6).then_inc(*done("fox_turned", which))

        def lru_turn(l):
            pe.wait_ge(*after("lru_in", "xy", l))
            pe.wait_ge(*after("fox_in", "qT", l))
            turn(lxy, 4).then_inc(*done("lru_turned", "xy"))

        def fox_logits(l, g):
            t, n = g // 2, P * (g // 2 + 1)
            if g == 0:
                pe.wait_ge(*after("fox_in", "kT", l))
                pe.wait_ge(*after("fox_gate", "rows", l))
            elif g == 1:
                pe.wait_ge(*after("fox_rows", "rows0", l))
            elif g == 2:
                pe.wait_ge(*after("ret_scores", "scores1", l))
            else:
                pe.wait_ge(*after("fox_rows", "rows2", l))
            for i in range(2):
                c = 2 * (g % 2) + i
                for e in range(2):
                    r, h = 64 * e, 2 * c + e
                    bank = ps[:, 6 + e, i * T:i * T + n]
                    pick = konst("fox_pick").rearrange("p (h q) -> p h q", h=8)
                    nc.tensor.matmul(bank, pick[r:r + 8, h, :], fcT[r:r + 8, 0:n], start=True, stop=False)
                    mm = nc.tensor.matmul(bank, fqT[r:r + 64, c, t * P:(t + 1) * P], fkT[r:r + 64, c, 0:n],
                                          start=False, stop=True)
            mm.then_inc(*done("fox_logits", f"logits{g}"))

        def lru_gates(l):
            pe.wait_ge(*after("lru_conv", f"tap{CW2 - 1}_1", l))
            for g, name in enumerate(("w_r", "w_i")):
                w = packed(PACK_B, name).rearrange("p (c n) -> p c n", c=2)
                for c in range(2):
                    mm = nc.tensor.matmul(ps[:, 4 + g, c * T:(c + 1) * T], w[:, c, :], lru[0][:, c * T:(c + 1) * T],
                                          start=True, stop=True)
            mm.then_inc(*done("lru_gates", "logits"))

        def fox_turn_p(l, g):
            pe.wait_ge(*after("fox_rows", f"weights{g}", l))
            if g == 0:
                pe.wait_ge(*after("lru_act", "i1", l))
            else:
                pe.wait_ge(*after("fox_out_low", f"out{g - 1}", l))
            for s in range(g // 2 + 1):
                for b in range(4):
                    mm = nc.tensor.transpose(ps[:, 4 + s, b * P:(b + 1) * P], fl[:, b, s * P:(s + 1) * P], ident)
            mm.then_inc(*done("fox_p_turned", f"turned{g}"))

        def fox_out(l, g):
            pe.wait_ge(*after("fox_p", f"copied{g}", l))
            pe.wait_ge(*after("fox_in", "v", l))
            for i in range(2):
                for e in range(2):
                    h = 2 * (2 * (g % 2) + i) + e
                    for s in range(g // 2 + 1):
                        mm = nc.tensor.matmul(ps[64 * e:64 * e + 64, 4, i * P:(i + 1) * P], fv[:, s, h * 64:h * 64 + 64],
                                              fpT[:, 4 * s + 2 * i + e, :], start=s == 0, stop=s == g // 2)
            mm.then_inc(*done("fox_out", f"out{g}"))

        def ret_turn(l):
            pe.wait_ge(*after("ret_rope", "rotated", l))
            pe.wait_ge(*after("fox_rows", "rows1", l))
            turn(rope, 6).then_inc(*done("ret_turned", "qk"))

        def ret_scores(l, c):
            if c == 0:
                pe.wait_ge(*after("ret_rope", "qkT", l))
            else:
                pe.wait_ge(*after("ret_scores", "scores0", l))
            for e in range(2):
                r = slice(64 * e, 64 * e + 64)
                q, kk = rT[r, c, :], rT[r, 2 + c, :]
                nc.tensor.matmul(ps[:, 6 + e, 0:256], kk[:, 0:P], q, start=True, stop=True)
                mm = nc.tensor.matmul(ps[:, 6 + e, 256:384], kk[:, P:T], q[:, P:T], start=True, stop=True)
            mm.then_inc(*done("ret_dots", f"dots{c}"))

        def ret_rows(l):
            pe.wait_ge(*after("ret_scores", "scores1", l))
            pe.wait_ge(*after("ret_in", "v", l))
            pe.wait_ge(*after("fox_rows", "rows3", l))
            for t in range(TT):
                for h in range(4):
                    o = ps[:, 6, t * 256 + h * 64:t * 256 + h * 64 + 64]
                    if t == 0:
                        mm = nc.tensor.matmul(o, ret_s[:, h, 0:P], rv[:, 0, h * 64:h * 64 + 64], start=True, stop=True)
                    else:
                        nc.tensor.matmul(o, ret_s[:, h, P:T], rv[:, 0, h * 64:h * 64 + 64], start=True, stop=False)
                        mm = nc.tensor.matmul(o, ret_s[:, h, T:384], rv[:, 1, h * 64:h * 64 + 64], start=False, stop=True)
            mm.then_inc(*done("ret_rows", "rows"))

        def ret_back(l):
            pe.wait_ge(*after("ret_norm", "gated", l))
            turn(ry_f.rearrange("p (t n) -> p t n", t=TT), 6, 2).then_inc(*done("ret_back", "turned"))

        def keys_turn(l, half):
            pe.wait_ge(*after("memory_in", f"k{half}", l))
            if half == 0:
                pe.wait_ge(*after("fox_out_low", "out3", l))
            else:
                pe.wait_ge(*after("ret_out_low", "out", l))
            turn(km[:, :, half * 512:half * 512 + 512], 4 + 2 * half).then_inc(*done("keys_turned", f"k{half}"))

        def mixer_b(L):
            l = L.l
            k = 0
            chunks = [("fox_q", 512), ("fox_k", 0), ("lru_xy", 0), ("fox_v", 0), ("ret_qk", 0), ("ret_vg", 0)]
            read = [("fox_in", "q"), ("fox_in", "k"), ("lru_in", "xy"), ("fox_in", "v"), ("ret_in", "qk"),
                    ("ret_in", "g"), ("memory_in", "v0"), ("memory_in", "v1"), ("memory_in", "k0"), ("memory_in", "k1")]
            steps = {0: [fox_forget], 1: [fox_decay, lambda l: fox_turn(l, "q")], 2: [lambda l: fox_turn(l, "k")],
                     3: [lru_turn, lambda l: fox_logits(l, 0)], 4: [lru_gates, lambda l: fox_logits(l, 1)],
                     5: [lambda l: fox_turn_p(l, 0), ret_turn]}
            for n in range(len(chunks)):
                if n < 2:
                    banks_free(L, 0, n)
                else:
                    pe.wait_ge(*after(*read[n - 2], l))
                for kh in range(2):
                    square(L, k, hT, 4 * kh, pair(n), kh == 0, kh == 1, rows_follow(L, 0) if (n, kh) == (0, 0) else None)
                    k += 1
                    if (n, kh) == (0, 0):
                        narrow(L, k, 8, 0)
                        k += 1
                for step in steps[n]:
                    step(l)
            memory_steps = [[lambda: fox_out(l, 0), lambda: ret_scores(l, 0)], [lambda: fox_turn_p(l, 1), lambda: ret_scores(l, 1)],
                            [lambda: fox_out(l, 1), lambda: fox_logits(l, 2)], [lambda: fox_logits(l, 3)],
                            [lambda: fox_turn_p(l, 2)], [lambda: fox_out(l, 2), lambda: ret_rows(l)],
                            [lambda: fox_turn_p(l, 3)], [lambda: fox_out(l, 3), lambda: ret_back(l)]]
            for n in range(4):
                pe.wait_ge(*after(*read[4 + n], l))
                for kh in range(2):
                    square(L, k, bT, 4 * kh, pair(n), kh == 0, kh == 1)
                    k += 1
                    for step in memory_steps[2 * n + kh]:
                        step()
            acc = lambda half: (lambda t, _: ps[:, 2 * t + half, :])
            pe.wait_ge(*after("lru_low", "out", l))
            pe.wait_ge(*after("memory_in", "k1", l))
            for kh in range(2):
                if kh:
                    pe.wait_ge(*after("fox_out_low", "out3", l))
                    pe.wait_ge(*after("ret_out_low", "out", l))
                else:
                    pe.wait_ge(*after("fox_out_low", "out2", l))
                for half in range(2):
                    square(L, k, hT, 4 * kh, acc(half), kh == 0, kh == 1, rows_lead(L, 1) if kh and half else None,
                           (lambda t: done("mix_b_out", "t0")) if kh and half else None)
                    k += 1
                    if kh == 0:
                        keys_turn(l, half)
            rows_led(L, 1)
            assert k == 25

        def cross(L):
            l, k = L.l, 25
            acc = lambda half: (lambda t, _: ps[:, 2 * t + half, :])
            def begin(t, i):
                if i == 0:
                    banks_free(L, 1, t)
                rows_follow(L, 1)(t, i)

            for kh in range(2):
                for half in range(2):
                    square(L, k, hT, 4 * kh, acc(half), kh == 0, kh == 1, begin if k == 25 else left_ready(L, 1, kh),
                           (lambda t: done("cross_q", "t0")) if kh and half else None)
                    k += 1
            for half in range(2):
                if half == 0:
                    pe.wait_ge(*after("cross_in", "q0", l))
                    pe.wait_ge(*after("memory_keys", "k1", l))
                else:
                    pe.wait_ge(*after("cross_in", "q1_1", l))
                turn(cq[:, :, half * 512:half * 512 + 512], 4 + 2 * half).then_inc(*done("cross_turned", f"q{half}"))

            def logits(g):
                t, half = g % 2, g // 2
                pe.wait_ge(*after("cross_in", f"qT{half}", l))
                for i in range(2):
                    for c in range(2):
                        n = 4 * half + 2 * i + c
                        mm = nc.tensor.matmul(ps[:, 2 * t + half, i * T:(i + 1) * T], cqT[:, n, t * P:(t + 1) * P],
                                              kmT[:, n, :], start=c == 0, stop=c == 1)
                mm.then_inc(*done("cross_logits", f"logits{g}"))

            def turn_weights(g):
                t, half = g % 2, g // 2
                pe.wait_ge(*after("cross_rows", f"weights{g}", l))
                for m in range(2):
                    for i in range(2):
                        mm = nc.tensor.transpose(ps[:, 4 + g, (2 * m + i) * P:(2 * m + i + 1) * P],
                                                 cp[t][:, 2 * half + i, m * P:(m + 1) * P], ident)
                mm.then_inc(*done("cross_p_turned", f"turned{g}"))

            def read(g):
                pe.wait_ge(*after("cross_p", f"copied{g}", l))
                for c in range(4):
                    for m in range(2):
                        at = (2 * m + c // 2) * P
                        mm = nc.tensor.matmul(ps[:, cross_bank(g), c * P:(c + 1) * P],
                                              vm[:, m, (4 * (g // 2) + c) * P:(4 * (g // 2) + c + 1) * P],
                                              cpT[g][:, at:at + P], start=m == 0, stop=m == 1)
                mm.then_inc(*done("cross_out", f"out{g}"))

            def split(kh):
                return first(lambda t: pe.wait_ge(*after("cross_out_low", f"out{2 * kh + t}", l)))

            for g in range(4):
                logits(g)
            for pair_of_groups in ((0, 1), (2, 3)):
                for g in pair_of_groups:
                    turn_weights(g)
                if 0 in pair_of_groups:
                    for g in pair_of_groups:
                        read(g)
            for kh in range(2):
                for half in range(2):
                    square(L, k, hT, 4 * kh, acc(half), kh == 0, kh == 1,
                           rows_lead(L, 2, split(kh)) if kh and half else split(kh),
                           (lambda t: done("cross_half", "t0")) if kh and half else None)
                    k += 1
                    if (kh, half) == (0, 0):
                        for g in (2, 3):
                            read(g)
            rows_led(L, 2)
            assert k == U_MIX_B

        nc.tensor.sem_inc(unit_done, CREDIT)
        pe.wait_ge(ident_loaded, 16)
        for kh in range(2):
            norm_turn(Layer("A", 0), 0, 0, kh)
        with pe.Fori(0, DEPTH) as l:
            L = Layer("A", l)
            ffn(L, 0, 0, 0)
            mixer_a(L)
            ffn(L, 1, 2, U_FFN + U_MIX_A)
        with pe.Fori(0, DEPTH) as l:
            L = Layer("B", l)
            mixer_b(L)
            cross(L)
            ffn(L, 0, 2, U_MIX_B)
        for kh in range(2):
            norm_turn(Layer("B", DEPTH), 0, 1, kh)

    @block.scalar
    def _(act):
        def high(L, k):
            slot = k % RING
            act.wait_ge(raw_landed[slot], L.turn(k) * 32)
            act.wait_ge(unit_done, L.unit0 + (k + 1))
            nc.scalar.activation(w_hi[:, slot, :], raw[:, slot, :], ACT.Copy).then_inc(high_ready, 1)

        def multiplied(L, k):
            act.wait_ge(unit_done, L.done_units(k))

        def rows_of(L):
            return out_b if L.b else out_a

        def norm_in(L, j):
            for t in range(TT):
                act.wait_ge(x_ready, L.sub(j, 2, t + 1))
                nc.scalar.activation(rows_of(L)[:, t, :], x[:, t, :], ACT.Square,
                                     accum_out=ss_in[:, t:t + 1]).then_inc(sq_in, 1)
            gain(post_g, L.sub0 + j, 1, post_loaded)
            gain(pre_g, L.sub0 + (j + 1), 0, pre_loaded)
            for t in range(TT):
                act.wait_ge(sq_in, L.sub(j, 2, t + 1))
                nc.scalar.activation(std_in[:, t:t + 1], ss_in[:, t:t + 1], ACT.Sqrt, bias=EPS,
                                     scale=1.0 / D).then_inc(std_ready, 1)

        def rms_ready(L, j):
            act.wait_ge(rstd_ready, L.sub(j, 2, TT))

        def gain(dst, s, side, loaded):
            act.dma_start(dst[:, :], d["gains"][bass.ds(s, 1), side, :].partition_broadcast(P)).then_inc(loaded, 16)

        def turned(L, j, t, kh):
            act.wait_ge(h_turned, L.sub(j, 4, 2 * t + kh + 1))
            nc.scalar.activation(hT_hi[:, 4 * kh:4 * kh + 4, t * P:(t + 1) * P],
                                 ps[:, 6 - 2 * t + kh, :].rearrange("p (c n) -> p c n", c=4),
                                 ACT.Copy).then_inc(hT_hi_ready, 1)

        def root(L, j):
            act.wait_ge(ident_loaded, 16)
            nc.scalar.activation(root_warm, ident[:, 0:1], ACT.Sqrt).then_inc(root_loaded, 1)
            act.wait_ge(root_loaded, L.sub(j, 1, 1))

        def norm_out(L, j, last, complete, half):
            m = 4.0 if half else 1.0
            def over(t):
                act.wait_ge(rstd_out_ready, L.sub(j, 2, t + 1))
                nc.scalar.activation(rows_of(L)[:, t, :].rearrange("p (h n) -> p h n", h=2), ps[:, 2 * t:2 * t + 2, :],
                                     ACT.Copy, scale=rstd_out[:, t:t + 1]).then_inc(out_copied, 1)

            def squares(t, h):
                act.wait_ge(*complete(t, h))
                if t:
                    act.wait_ge(sq_out, L.sub(j, 4, h + 1))
                nc.scalar.activation(pairbuf[:, 512 * h:512 * h + 512], ps[:, 2 * t + h, :], ACT.Square,
                                     accum_out=ss_out[:, 2 * t + h:2 * t + h + 1]).then_inc(sq_out, 1)

            def root_mean(t):
                act.wait_ge(sq_out, L.sub(j, 4, 2 * t + 2))
                act.wait_ge(sq_bias, L.sub(j, 2, t + 1))
                nc.scalar.activation(std_out[:, t:t + 1], ss_out[:, 2 * t + 1:2 * t + 2], ACT.Sqrt,
                                     bias=bias_out[:, t:t + 1], scale=m / D).then_inc(std_out_ready, 1)

            squares(0, 0)
            squares(0, 1)
            root_mean(0)
            squares(1, 0)
            over(0)
            turned(L, j + 1, 0, 0)
            squares(1, 1)
            root_mean(1)
            turned(L, j + 1, 0, 1)
            over(1)
            turned(L, j + 1, 1, 0)
            high(L, last + PAST)
            turned(L, j + 1, 1, 1)

        def ffn(L, n, j, k0):
            f = L.ffn(n)

            def silu(M, k, c, bank=6):
                multiplied(M, k)
                for t in range(TT):
                    silu_t = nc.scalar.activation(sil[:, t, :], ps[:, bank + t, 0:FC], ACT.Silu, scale=rstd_in[:, t:t + 1])
                silu_t.then_inc(silu_ready, 1)

            def hidden(c, dst=bT_hi[:, KD:KD + 2, :]):
                act.wait_ge(hid_turned, f * NCHUNK + (c + 1))
                nc.scalar.activation(dst, ps[:, 4, :].rearrange("p (i t) -> p i t", i=2),
                                     ACT.Copy).then_inc(gT_hi_ready, 1)

            def chunk(M, k, c):
                hidden(c - 1)
                high(M, k + AHEAD)
                high(M, k + 1 + AHEAD)
                silu(M, k + 1, c)
                high(M, k + 2 + AHEAD)

            if n:
                memory_std(L.l)
            high(L, k0 + 1 + AHEAD)
            norm_in(L, j)
            rms_ready(L, j)
            silu(L, k0 + 1, 0, 0)
            high(L, k0 + 2 + AHEAD)
            hidden(0)
            if n:
                memory_high(L.l)
            high(L, k0 + 3 + AHEAD)
            silu(L, k0 + 3, 1)
            high(L, k0 + 4 + AHEAD)
            with act.Fori(2, NCHUNK - 1) as c:
                chunk(Chunk(L, c), k0 + 5, c)
            end, c = k0 + U_FFN - 1, NCHUNK - 1
            hidden(c - 1)
            high(L, end - 3 + AHEAD)
            high(L, end - 2 + AHEAD)
            silu(L, end - 2, c)
            high(L, end - 1 + AHEAD)
            hidden(c, hT_hi[:, 0:2, :])
            root(L, j)
            high(L, end + AHEAD)
            norm_out(L, j, end, lambda t, h: (unit_done, L.done_units(end)) if t and h else (ffn_out, f * 3 + (2 * t + h + 1)),
                     not L.b)

        def copy(dst, src, stage, step, scale=1.0, func=ACT.Copy):
            nc.scalar.activation(dst, src, func, scale=scale).then_inc(*done(stage, step))

        def rows(dst, src, stage, step, func=ACT.Copy):
            for t in range(TT):
                last = nc.scalar.activation(dst[:, t, :], src[:, t, :], func, scale=rstd_in[:, t:t + 1])
            last.then_inc(*done(stage, step))

        def mixed(L, k, stage):
            return lambda t, h: ((unit_done, L.done_units(k - 1)) if not h else
                                 (unit_done, L.done_units(k)) if t else after(stage, "t0", L.l))

        def chunk_rows(n):
            return ps[:, 2 * (n % 2):2 * (n % 2) + 2, :]

        def two(bank):
            return ps[:, bank:bank + 2, :].rearrange("p b (c t) -> p (b c) t", c=2)

        def gla_alpha(l):
            act.wait_ge(*after("gla_keep", "logits", l))
            nc.scalar.activation(gdec, nla, ACT.Abs).then_inc(*done("gla_soft", "abs"))
            act.wait_ge(*after("gla_soft", "abs", l))
            nc.scalar.activation(gdec, gdec, ACT.Exp, scale=-1.0).then_inc(*done("gla_soft", "exp"))
            act.wait_ge(*after("gla_soft", "exp", l))
            nc.scalar.activation(gdec, gdec, ACT.Ln, bias=1.0).then_inc(*done("gla_soft", "ln"))

        def gla_decays(l):
            act.wait_ge(*after("gla_sums", "sums", l))
            nc.scalar.activation(gdec, ps[:, 4, :], ACT.Exp, scale=-1.0 / TAU).then_inc(*done("gla_exp", "to_end"))
            nc.scalar.activation(lam.rearrange("p c n -> p (c n)"), ps[:, 5, 0:8], ACT.Exp,
                                 scale=-1.0 / TAU).then_inc(*done("gla_exp", "chunk"))

        def gla_std(l):
            act.wait_ge(*after("gla_out", "sums", l))
            nc.scalar.activation(stdg, ssg, ACT.Sqrt, bias=EPS, scale=1.0 / P).then_inc(*done("gla_std", "std"))

        def gla_out(l):
            act.wait_ge(*after("gla_out_turned", "turned", l))
            for c in range(4):
                nc.scalar.activation(bT_hi[:, c, :], two(6)[:, c, :], ACT.Copy,
                                     scale=packed(PACK_A, "gla_g")[:, c:c + 1]).then_inc(*done("gla_out_high", f"out{c}"))

        def sb_weights(l, c):
            if c == 0:
                nc.scalar.activation(root_warm, ident[:, 0:1], ACT.Exp).then_inc(*done("sb_weights", "table"))
                act.wait_ge(*after("sb_weights", "table", l))
            act.wait_ge(*after("sb_logits", f"logits{c}", l))
            nc.scalar.activation(sb_e.rearrange("p (e n) -> p e n", e=2), ps[:, 4:6, 0:384],
                                 ACT.Abs).then_inc(*done("sb_weights", f"abs{c}"))
            act.wait_ge(*after("sb_weights", f"abs{c}", l))
            nc.scalar.activation(sb_e, sb_e, ACT.Exp, scale=-1.0).then_inc(*done("sb_weights", f"exp{c}"))
            act.wait_ge(*after("sb_weights", f"exp{c}", l))
            nc.scalar.activation(sb_e, sb_e, ACT.Ln, bias=1.0).then_inc(*done("sb_weights", f"ln{c}"))

        def sb_exp(l, c):
            act.wait_ge(*after("sb_keep", f"exponent{c}", l))
            nc.scalar.activation(sb_e, sb_z, ACT.Exp).then_inc(*done("sb_weights", f"weights{c}"))

        def sb_out(l, c):
            act.wait_ge(*after("sb_out", f"out{c}", l))
            nc.scalar.activation(bT_hi[:, 4 + c, :].rearrange("p (t n) -> p t n", t=TT), ps[:, 6:8, 384:512],
                                 ACT.Copy).then_inc(*done("sb_out_high", f"out{c}"))

        def conv_std(l):
            for t in range(TT):
                act.wait_ge(*after("conv_norm", f"centred{t}", l))
                nc.scalar.activation(conv_y_f[:, t * 512:(t + 1) * 512], conv_n[:, t, :], ACT.Square,
                                     accum_out=css[:, t:t + 1]).then_inc(*done("conv_std", f"sum{t}"))
            for t in range(TT):
                act.wait_ge(*after("conv_std", f"sum{t}", l))
                nc.scalar.activation(cstd[:, t:t + 1], css[:, t:t + 1], ACT.Sqrt, bias=EPS,
                                     scale=1.0 / BW).then_inc(*done("conv_std", f"std{t}"))

        def conv_out(l):
            act.wait_ge(*after("conv_normed", "turned", l))
            for c in range(4):
                nc.scalar.activation(conv_y[:, c, :], two(4)[:, c, :], ACT.Silu, bias=packed(PACK_A, "ln_b")[:, c:c + 1],
                                     scale=packed(PACK_A, "ln_g")[:, c:c + 1]).then_inc(*done("conv_out", f"act{c}"))
            act.wait_ge(*after("conv_out", "act3", l))
            multiplied_gla = U_FFN + 17 + 5
            act.wait_ge(unit_done, Layer("A", l).done_units(multiplied_gla))
            nc.scalar.activation(bT_hi[:, 0:4, :], conv_y, ACT.Copy).then_inc(*done("conv_out", "high"))

        def merged_high(l, kh):
            for t in range(TT):
                act.wait_ge(*after("merged_turned", f"k{kh}t{t}", l))
                nc.scalar.activation(hT_hi[:, 4 * kh:4 * kh + 4, t * P:(t + 1) * P],
                                     ps[:, 4 + 2 * kh + t, :].rearrange("p (c n) -> p c n", c=4),
                                     ACT.Copy).then_inc(*done("merged_high", f"k{kh}t{t}"))

        def mixer_a(L):
            l, k = L.l, U_FFN + 1
            plan = {"gla_qk": (gqk, "gla_in", "qk", ACT.Copy), "gla_v": (gv, "gla_in", "v", ACT.Copy),
                    "gla_r": (gr, "gla_in", "r", ACT.Silu), "conv_a": (conv_u, "conv_in", "a", ACT.Copy),
                    "conv_g": (conv_s, "conv_in", "g", ACT.Sigmoid), "sb_q": (sb_q, "sb_in", "q", ACT.Copy),
                    "sb_k": (sb_k, "sb_in", "k", ACT.Copy), "sb_v": (sbv, "sb_in", "v", ACT.Copy)}
            for n, name in enumerate(A_CHUNKS):
                high(L, k + AHEAD)
                if n == 0:
                    norm_in(L, 1)
                    act.dma_start(pack[:, 0:PACK_A_W], d["pack_a"][bass.ds(l, 1), :, :].rearrange(
                        "o p n -> p (o n)")).then_inc(pack_loaded, 16)
                    rms_ready(L, 1)
                if name == "gla_r":
                    gla_alpha(l)
                if name == "conv_a":
                    gla_decays(l)
                if name == "sb_k":
                    act.wait_ge(*after("sb_turned", "q", l))
                    copy(sbqT, two(4), "sb_in", "qT", 64 ** -0.5)
                if name == "sb_v":
                    gla_out(l)
                    act.wait_ge(*after("sb_turned", "k", l))
                    copy(sbkT, two(4), "sb_in", "kT")
                if name == "sb_q":
                    gla_std(l)
                high(L, k + 1 + AHEAD)
                multiplied(L, k + 1)
                dst, stage, step, func = plan[name]
                if name == "sb_q":
                    act.wait_ge(*after("conv_turned", "u", l))
                if name == "sb_v":
                    act.wait_ge(*after("gla_out", "gated", l))
                rows(dst, chunk_rows(n), stage, step, func)
                k += 2
            for i, b in enumerate(A_SECTIONS):
                for half in range(2):
                    for kh in range(2):
                        high(L, k + AHEAD)
                        n = 6 * i + 2 * half + kh
                        if n == 14:
                            conv_out(l)
                        if kh:
                            multiplied(L, k)
                            if i:
                                act.wait_ge(*after("merge", f"branch{i - 1}_{half}", l))
                            rows(sg[:, half, :, :], chunk_rows(half), "gates", f"gate{i}_{half}", ACT.Sigmoid)
                        if n < 12:
                            section_step(l, n)
                        if n == 12:
                            conv_std(l)
                        k += 1
                for half in range(2):
                    high(L, k + AHEAD)
                    section_step(l, 6 * i + 4 + half)
                    k += 1
            merged_high(l, 0)
            for n in range(4):
                high(L, k + AHEAD)
                if n == 0:
                    merged_high(l, 1)
                    memory_load(l)
                if n == 2:
                    root(L, 1)
                k += 1
            norm_out(L, 1, k - 1, mixed(L, k - 1, "mix_a_out"), False)

        def section_step(l, n):
            if n % 2 == 0 and 2 <= n <= 8:
                sb_out(l, n // 2 - 1)
            if n % 2 == 0 and n < 8:
                sb_weights(l, n // 2)
            if n % 2 == 1 and n < 8:
                sb_exp(l, n // 2)

        def memory_load(l):
            act.dma_start(mem_rows[:, :, :], d["mem"][0, :, :].rearrange("(t p) n -> p t n", p=P)).then_inc(memory_loaded, 16)
            act.dma_start(mem_g, d["mem_g"][0:1, :].partition_broadcast(P)).then_inc(memory_loaded, 16)

        def memory_std(l):
            act.wait_ge(memory_loaded, l * 32 + 32)
            for t in range(TT):
                if t:
                    act.wait_ge(*after("memory_std", f"sum{t - 1}", l))
                nc.scalar.activation(mem_sq, mem_rows[:, t, :], ACT.Square,
                                     accum_out=ss_mem[:, t:t + 1]).then_inc(*done("memory_std", f"sum{t}"))
            for t in range(TT):
                act.wait_ge(*after("memory_std", f"sum{t}", l))
                nc.scalar.activation(std_mem[:, t:t + 1], ss_mem[:, t:t + 1], ACT.Sqrt, bias=EPS,
                                     scale=1.0 / D).then_inc(*done("memory_std", f"std{t}"))

        def memory_high(l):
            for t in range(TT):
                for kh in range(2):
                    act.wait_ge(*after("memory_turned", f"t{t}k{kh}", l))
                    nc.scalar.activation(bT_hi[:, 4 * kh:4 * kh + 4, t * P:(t + 1) * P],
                                         ps[:, 2 * t + kh, :].rearrange("p (c n) -> p c n", c=4),
                                         ACT.Copy).then_inc(*done("memory_high", f"t{t}k{kh}"))

        def rope():
            for name, table in (("sin", sin), ("cos", cos)):
                act.wait_ge(*after("rope_angles", name, 0))
                nc.scalar.activation(table, table, ACT.Sin).then_inc(*done("rope_tables", name))

        def fox_soft(l):
            act.wait_ge(*after("fox_gate", "logits", l))
            z = flog.rearrange("p t h -> p (t h)")
            nc.scalar.activation(ftmp, z, ACT.Abs).then_inc(*done("fox_soft", "abs"))
            act.wait_ge(*after("fox_soft", "abs", l))
            nc.scalar.activation(ftmp, ftmp, ACT.Exp, scale=-1.0).then_inc(*done("fox_soft", "exp"))
            act.wait_ge(*after("fox_soft", "exp", l))
            nc.scalar.activation(ftmp, ftmp, ACT.Ln, bias=1.0).then_inc(*done("fox_soft", "ln"))

        def lru_lambda(l):
            act.wait_ge(pack_loaded, l * 16 + (16 * DEPTH + 16))
            nc.scalar.activation(lru_t, packed(PACK_B, "lam"), ACT.Abs).then_inc(*done("lru_act", "abs"))
            act.wait_ge(*after("lru_act", "abs", l))
            nc.scalar.activation(lru_t, lru_t, ACT.Exp, scale=-1.0).then_inc(*done("lru_act", "lambda"))

        def lru_gates(l):
            act.wait_ge(*after("lru_gates", "logits", l))
            for g, (dst, bias) in enumerate(((lru[1], "b_r"), (lru[2], "b_i"))):
                for c in range(2):
                    nc.scalar.activation(dst[:, c * T:(c + 1) * T], ps[:, 4 + g, c * T:(c + 1) * T], ACT.Sigmoid,
                                         bias=packed(PACK_B, bias)[:, c:c + 1]).then_inc(*done("lru_act", f"{'ri'[g]}{c}"))

        def lru_decay(l):
            act.wait_ge(*after("lru_math", "log1", l))
            nc.scalar.activation(lru[3], lru[1], ACT.Tanh).then_inc(*done("lru_act", "tanh"))
            act.wait_ge(*after("lru_act", "tanh", l))
            nc.scalar.activation(lru[1], lru[1], ACT.Exp).then_inc(*done("lru_act", "decay"))
            act.wait_ge(*after("lru_turn", "y", l))
            nc.scalar.activation(lyT, lyT, ACT.Gelu_apprx_tanh).then_inc(*done("lru_act", "gelu"))

        def lru_root(l):
            act.wait_ge(*after("lru_math", "square", l))
            nc.scalar.activation(lru[3], lru[3], ACT.Sqrt).then_inc(*done("lru_act", "root"))

        def lru_high(l):
            act.wait_ge(*after("lru_math", "out", l))
            nc.scalar.activation(hT_hi[:, 0:2, :], lru[0].rearrange("p (c t) -> p c t", c=2),
                                 ACT.Copy).then_inc(*done("lru_act", "high"))

        def fox_exp(l, g):
            n = P * (g // 2 + 1)
            act.wait_ge(*after("fox_rows", f"max{g}", l))
            for b in range(4):
                nc.scalar.activation(fl[:, b, 0:n], fl[:, b, 0:n], ACT.Exp, bias=fmax[:, b:b + 1],
                                     accum_out=fden[:, b:b + 1]).then_inc(*done("fox_exp", f"g{g}h{b}"))

        def fox_p(l, g):
            act.wait_ge(*after("fox_p_turned", f"turned{g}", l))
            n = g // 2 + 1
            nc.scalar.activation(fpT[:, 0:4 * n, :], ps[:, 4:4 + n, :].rearrange("p s (b t) -> p (s b) t", b=4),
                                 ACT.Copy).then_inc(*done("fox_p", f"copied{g}"))

        def fox_tiles(w, g):
            c, t = 2 + 2 * (g % 2), g // 2
            return w[:, c:c + 2, t * P:(t + 1) * P]

        def fox_out(l, g):
            act.wait_ge(*after("fox_out", f"out{g}", l))
            nc.scalar.activation(fox_tiles(hT_hi, g), ps[:, 4, 0:256].rearrange("p (c t) -> p c t", c=2),
                                 ACT.Copy).then_inc(*done("fox_out_high", f"out{g}"))

        def ret_std(l):
            act.wait_ge(*after("ret_norm", "sums", l))
            nc.scalar.activation(rstat2, rstat, ACT.Sqrt, bias=EPS, scale=1.0 / 64).then_inc(*done("ret_std", "std"))

        def ret_out(l):
            act.wait_ge(*after("ret_back", "turned", l))
            nc.scalar.activation(hT_hi[:, 6:8, :], ps[:, 6, :].rearrange("p (c t) -> p c t", c=2),
                                 ACT.Copy).then_inc(*done("ret_out_high", "out"))

        def keys(l, half):
            act.wait_ge(*after("keys_turned", f"k{half}", l))
            copy(kmT[:, 4 * half:4 * half + 4, :], two(4 + 2 * half), "memory_keys", f"k{half}")

        def mixer_b(L):
            l = L.l
            k = 1
            between = {0: lambda: (fox_soft(l), lru_lambda(l)),
                       2: lambda: (act.wait_ge(*after("fox_turned", "q", l)), copy(fqT, two(4), "fox_in", "qT", 64 ** -0.5)),
                       3: lambda: (act.wait_ge(*after("fox_turned", "k", l)), copy(fkT, two(6), "fox_in", "kT")),
                       4: lambda: fox_exp(l, 0),
                       5: lambda: lru_gates(l)}
            evicted = [(fq, "fox_in", "q"), (fk, "fox_in", "k"), (lxy, "lru_in", "xy"), (fv, "fox_in", "v"),
                       (rqk, "ret_in", "qk"), (rv, "ret_in", "v")]
            for n in range(6):
                if n != 1:
                    high(L, k + AHEAD)
                if n == 0:
                    norm_in(L, 0)
                    act.dma_start(pack[:, 0:PACK_B_W], d["pack_b"][bass.ds(l, 1), :, :].rearrange(
                        "o p n -> p (o n)")).then_inc(pack_loaded, 16)
                    rms_ready(L, 0)
                elif n in between:
                    between[n]()
                high(L, k + 1 + AHEAD)
                if n == 0:
                    high(L, k + 2 + AHEAD)
                    between[n]()
                multiplied(L, k + 1)
                dst, stage, step = evicted[n]
                rows(dst, chunk_rows(n) if n < 5 else chunk_rows(n)[:, :, 0:256], stage, step)
                if n == 5:
                    rows(rg, chunk_rows(n)[:, :, 256:512], "ret_in", "g", ACT.Silu)
                k += 2
            steps = [lambda: (fox_p(l, 0), fox_exp(l, 1)),
                     lambda: (lru_decay(l), fox_out(l, 0)),
                     lambda: (fox_p(l, 1), lru_root(l)),
                     lambda: (fox_out(l, 1), fox_exp(l, 2)),
                     lambda: lru_high(l),
                     lambda: (fox_p(l, 2), fox_exp(l, 3)),
                     lambda: (fox_out(l, 2), ret_std(l)),
                     lambda: fox_p(l, 3)]
            for n in range(4):
                name = ("v0", "v1", "k0", "k1")[n]
                dst = (vm, km)[n // 2][:, :, (n % 2) * 512:(n % 2) * 512 + 512]
                for kh in range(2):
                    high(L, k + kh + AHEAD)
                    steps[2 * n + kh]()
                multiplied(L, k + 1)
                if name == "k0":
                    act.wait_ge(*after("lru_low", "out", l))
                copy(dst, chunk_rows(n), "memory_in", name)
                k += 2
            for n in range(4):
                high(L, k + AHEAD)
                if n == 0:
                    fox_out(l, 3)
                    ret_out(l)
                else:
                    if n < 3:
                        keys(l, n - 1)
                    if n == 2:
                        root(L, 0)
                k += 1
            norm_out(L, 0, k - 1, mixed(L, k - 1, "mix_b_out"), False)

        def cross(L):
            l, k = L.l, 25
            for n in range(4):
                if n == 2:
                    nc.scalar.activation(root_warm, ident[:, 0:1], ACT.Exp).then_inc(*done("cross_exp", "table"))
                    act.wait_ge(*after("cross_exp", "table", l))
                if n:
                    high(L, k + AHEAD)
                if n == 1:
                    norm_in(L, 1)
                    rms_ready(L, 1)
                k += 1

            def q(t, first, last, step):
                cols = slice(512 * first, 512 * last)
                copy(cq[:, t, cols].rearrange("p (h n) -> p h n", n=512), ps[:, 2 * t + first:2 * t + last, :], "cross_in",
                     step, rstd_in[:, t:t + 1])

            def exp(g):
                t, half = g % 2, g // 2
                act.wait_ge(*after("cross_max", f"max{g}", l))
                for i in range(2):
                    nc.scalar.activation(cp[t][:, 2 * half + i, :], ps[:, 2 * t + half, i * T:(i + 1) * T], ACT.Exp,
                                         bias=cmax[:, 2 * g + i:2 * g + i + 1],
                                         accum_out=cden[:, 2 * g + i:2 * g + i + 1]).then_inc(*done("cross_exp", f"g{g}h{i}"))

            def weights(g):
                act.wait_ge(*after("cross_p_turned", f"turned{g}", l))
                copy(cpT[g], ps[:, 4 + g, :], "cross_p", f"copied{g}")

            def out_high(g):
                t, half = g % 2, g // 2
                act.wait_ge(*after("cross_out", f"out{g}", l))
                copy(hT_hi[:, 4 * half:4 * half + 4, t * P:(t + 1) * P],
                     ps[:, cross_bank(g), :].rearrange("p (c n) -> p c n", c=4), "cross_out_high", f"out{g}")

            multiplied(L, k - 2)
            q(1, 0, 1, "q1_0")
            act.wait_ge(*after("cross_q", "t0", l))
            q(0, 0, 2, "q0")
            multiplied(L, k - 1)
            q(1, 1, 2, "q1_1")
            for half in range(2):
                act.wait_ge(*after("cross_turned", f"q{half}", l))
                copy(cqT[:, 4 * half:4 * half + 4, :], two(4 + 2 * half), "cross_in", f"qT{half}", 256 ** -0.5)
            high(L, k + AHEAD)
            for step in (lambda: exp(0), lambda: exp(1), lambda: exp(2), lambda: weights(0), lambda: exp(3),
                         lambda: weights(1), lambda: out_high(0), lambda: out_high(1), lambda: weights(2),
                         lambda: weights(3)):
                step()
            k += 1
            for n in range(1, 4):
                high(L, k + AHEAD)
                if n == 1:
                    for g in (2, 3):
                        out_high(g)
                if n == 2:
                    root(L, 1)
                k += 1
            norm_out(L, 1, k - 1, mixed(L, k - 1, "cross_half"), False)

        act.dma_start(const[:, 0:P], d["const"][:, 0:P]).then_inc(ident_loaded, 16)
        for t in range(TT):
            act.dma_start(x[:, t, :], d["x"][0, t * P:(t + 1) * P, :]).then_inc(x_loaded[t], 16)
            if t == 0:
                gain(pre_g, 0, 0, pre_loaded)
        nc.scalar.sem_inc(out_copied, TT)
        act.dma_start(positions, d["positions"][:, :]).then_inc(const_loaded, 16)
        at, width = CONST["inv_freq"]
        act.dma_start(const[:, at:at + width], d["const"][:, at:at + width]).then_inc(const_loaded, 16)
        for t in range(TT):
            act.wait_ge(raw_landed[t], 32)
            nc.scalar.activation(w_hi[:, t, :], raw[:, t, :], ACT.Copy).then_inc(high_ready, 1)
            if t:
                rope()
            for kh in range(2):
                turned(Layer("A", 0), 0, t, kh)
        high(Layer("A", 0), AHEAD)
        for at, end in ((P, at), (at + width, CONST_ARRAY.shape[1])):
            act.dma_start(const[:, at:end], d["const"][:, at:end]).then_inc(const_loaded, 16)
        with act.Fori(0, DEPTH) as l:
            L = Layer("A", l)
            ffn(L, 0, 0, 0)
            mixer_a(L)
            ffn(L, 1, 2, U_FFN + U_MIX_A)
        with act.Fori(0, DEPTH) as l:
            L = Layer("B", l)
            mixer_b(L)
            cross(L)
            ffn(L, 0, 2, U_MIX_B)
        act.wait_ge(pre_loaded, 16 * (6 * DEPTH + 1))

    @block.vector
    def _(dve):
        V = nc.vector

        def flat(w):
            return w.bitcast(F32)

        def multiplied(L, k):
            dve.wait_ge(unit_done, L.done_units(k))

        def norm_in(L, j):
            for t in range(TT):
                dve.wait_ge(std_ready, L.sub(j, 2, t + 1))
                V.reciprocal(rstd_in[:, t:t + 1], std_in[:, t:t + 1]).then_inc(rstd_ready, 1)
            dve.wait_ge(rstd_ready, L.sub(j, 2, TT))

        def prepare(L, j):
            dve.wait_ge(post_loaded, L.sub(j, 16, 16))
            dve.wait_ge(pre_loaded, L.sub(j, 16, 32))
            V.tensor_tensor(both_b if L.b else both_a, post_g[:, :], pre_g[:, :], ALU.mult).then_inc(prepared, 1)
            for t in range(TT):
                dve.wait_ge(x_ready, L.sub(j, 2, t + 1))
                V.tensor_tensor(x_pre[:, t, :], x[:, t, :], pre_g[:, :], ALU.mult).then_inc(prepared, 1)

        def low(L, j, t, kh):
            dve.wait_ge(hT_hi_ready, L.sub(j, 4, 2 * t + kh + 1))
            tiles = (slice(None), slice(4 * kh, 4 * kh + 4), slice(t * P, (t + 1) * P))
            V.tensor_tensor(hT_lo[tiles], ps[:, 6 - 2 * t + kh, :].rearrange("p (c n) -> p c n", c=4),
                            flat(hT_hi[tiles]), ALU.subtract).then_inc(hT_ready, 1)

        def norm_out(L, j, half):
            m = 4.0 if half else 1.0
            rows, both_g = (out_b, both_b) if L.b else (out_a, both_a)
            dve.wait_ge(prepared, L.sub(j, 3, 3))
            for t in range(TT):
                for h in range(2):
                    dve.wait_ge(sq_out, L.sub(j, 4, 2 * t + h + 1))
                    if h == 0:
                        V.tensor_scalar(bias_out[:, t:t + 1], ss_out[:, 2 * t:2 * t + 1], m / D, m * EPS, ALU.mult,
                                        ALU.add).then_inc(sq_bias, 1)
                    cols = slice(512 * h, 512 * h + 512)
                    V.tensor_tensor(xn[:, t, cols], ps[:, 2 * t + h, :], both_g[:, cols], ALU.mult).then_inc(weighted, 1)
                    if (t, h) == (1, 0):
                        low(L, j + 1, 0, 0)
                dve.wait_ge(std_out_ready, L.sub(j, 2, t + 1))
                V.reciprocal(rstd_out[:, t:t + 1], std_out[:, t:t + 1]).then_inc(rstd_out_ready, 1)
                dve.wait_ge(rstd_out_ready, L.sub(j, 2, t + 1))
                for kh in range(2):
                    cols = slice(512 * kh, 512 * kh + 512)
                    dve.wait_ge(weighted, L.sub(j, 4, 2 * t + kh + 1))
                    V.scalar_tensor_tensor(xn[:, t, cols], xn[:, t, cols], rstd_out[:, t:t + 1], x_pre[:, t, cols], ALU.mult,
                                           ALU.add).then_inc(h_ready, 1)
            for t, kh in ((0, 1), (1, 0), (1, 1)):
                low(L, j + 1, t, kh)
            for t in range(TT):
                dve.wait_ge(out_copied, L.sub(j, 2, 2 + t + 1))
                V.tensor_tensor(rows[:, t, :], rows[:, t, :], post_g[:, :], ALU.mult).then_inc(scaled, 1)
                dve.wait_ge(scaled, L.sub(j, 2, t + 1))
                V.tensor_tensor(x[:, t, :], x[:, t, :], rows[:, t, :], ALU.add).then_inc(x_ready, 1)

        def ffn(L, n, j, k0):
            f = L.ffn(n)

            def hidden(c, bank=6):
                dve.wait_ge(silu_ready, f * NCHUNK + (c + 1))
                for t in range(TT):
                    up = V.scalar_tensor_tensor(hid[:, t, :], ps[:, bank + t, FC:2 * FC], rstd_in[:, t:t + 1], sil[:, t, :],
                                                ALU.mult, ALU.mult)
                up.then_inc(hid_ready, 1)

            def hidden_low(c, hi=bT_hi[:, KD:KD + 2, :], lo=bT_lo[:, KD:KD + 2, :]):
                dve.wait_ge(gT_hi_ready, f * NCHUNK + (c + 1))
                V.tensor_tensor(lo, ps[:, 4, :].rearrange("p (i t) -> p i t", i=2), flat(hi),
                                ALU.subtract).then_inc(gT_ready, 1)

            norm_in(L, j)
            if n:
                memory_rows(L.l)
            hidden(0, 0)
            hidden_low(0)
            if n:
                memory_low(L.l)
            hidden(1)
            prepare(L, j)
            with dve.Fori(2, NCHUNK - 1) as c:
                hidden_low(c - 1)
                hidden(c)
            hidden_low(NCHUNK - 2)
            hidden(NCHUNK - 1)
            hidden_low(NCHUNK - 1, hT_hi[:, 0:2, :], hT_lo[:, 0:2, :])
            norm_out(L, j, not L.b)

        def two(bank):
            return ps[:, bank:bank + 2, :].rearrange("p b (c t) -> p (b c) t", c=2)

        def gla_rank_rows(L, k):
            l = L.l
            multiplied(L, k)
            V.tensor_copy(lrT[0:RANK, :], ps[0:RANK, 6, 0:T]).then_inc(*done("gla_rank", "turned"))

        def gla_logits(l):
            dve.wait_ge(*after("gla_alpha", "logits", l))
            for t in range(TT):
                s = slice(t * T, (t + 1) * T)
                V.scalar_tensor_tensor(nla[:, s], ps[:, 7, s], rstd_in[:, t:t + 1], packed(PACK_A, "b_alpha"), ALU.mult,
                                       ALU.add).then_inc(*done("gla_keep", "logits" if t else "logits0"))

        def gla_keep(l):
            dve.wait_ge(*after("gla_soft", "abs", l))
            V.tensor_scalar(nla, nla, -1.0, 0.0, ALU.mult, ALU.max).then_inc(*done("gla_keep", "max"))
            dve.wait_ge(*after("gla_keep", "max", l))
            dve.wait_ge(*after("gla_soft", "ln", l))
            V.tensor_tensor(nla, nla, gdec, ALU.add).then_inc(*done("gla_keep", "softplus"))

        def gla_keys(l):
            dve.wait_ge(*after("gla_turned", "q", l))
            V.tensor_copy(gqT, ps[:, 6, :].rearrange("p (c t) -> p c t", c=2)).then_inc(*done("gla_decay", "q"))
            dve.wait_ge(*after("gla_exp", "to_end", l))
            dve.wait_ge(*after("gla_in", "qk", l))
            g = gdec.rearrange("p (t n) -> p t n", t=TT)
            V.tensor_tensor(g, g, gqk[:, :, 256:512], ALU.mult).then_inc(*done("gla_decay", "keys"))

        def gla_states(l):
            dve.wait_ge(*after("gla_updates", "updates", l))
            dve.wait_ge(*after("gla_exp", "chunk", l))
            for n in range(4):
                for c in range(2):
                    t, half = n // 2, n % 2
                    update = ps[:, 6 + half, (2 * c + t) * P:(2 * c + t + 1) * P]
                    step = "last" if (n, c) == (3, 1) else f"n{n}c{c}"
                    if n == 0:
                        V.tensor_copy(gstate[:, c, n, :], update).then_inc(*done("gla_state", step))
                    else:
                        dve.wait_ge(*after("gla_state", f"n{n - 1}c{c}", l))
                        V.scalar_tensor_tensor(gstate[:, c, n, :], gstate[:, c, n - 1, :], lam[:, c, n:n + 1], update,
                                               ALU.mult, ALU.add).then_inc(*done("gla_state", step))

        def gla_rows(l):
            dve.wait_ge(*after("gla_reads", "reads", l))
            o = go_f.rearrange("p (t c e v) -> p t c e v", t=TT, c=2, e=2)
            for e in range(2):
                V.tensor_scalar(o[:, :, :, e, :], ps[:, 4 + e, :].rearrange("p (t c v) -> p t c v", t=TT, c=2), 0.125, None,
                                ALU.mult).then_inc(*done("gla_out", "rows" if e else "rows_even"))
            dve.wait_ge(*after("gla_out", "rows", l))
            V.tensor_tensor(gsq_f, go_f, go_f, ALU.mult).then_inc(*done("gla_out", "squares"))
            dve.wait_ge(*after("gla_out", "squares", l))
            V.tensor_reduce(ssg, gsq_f.rearrange("p (h v) -> p h v", h=8), AX.X, ALU.add).then_inc(*done("gla_out", "sums"))

        def gla_gated(l):
            dve.wait_ge(*after("gla_std", "std", l))
            V.reciprocal(rstdg, stdg).then_inc(*done("gla_out", "rstd"))
            dve.wait_ge(*after("gla_in", "r", l))
            V.tensor_tensor(go_f, go_f, gr_f, ALU.mult).then_inc(*done("gla_out", "with_r"))
            dve.wait_ge(*after("gla_out", "with_r", l))
            o = go_f.rearrange("p (h v) -> p h v", h=8)
            V.tensor_tensor(o, o, rstdg.unsqueeze(2).broadcast_to([P, 8, P]), ALU.mult).then_inc(*done("gla_out", "gated"))

        def gla_low(l):
            for c in range(4):
                dve.wait_ge(*after("gla_out_high", f"out{c | 1}", l))
                V.scalar_tensor_tensor(bT_lo[:, c, :], two(6)[:, c, :], packed(PACK_A, "gla_g")[:, c:c + 1],
                                       flat(bT_hi[:, c, :]), ALU.mult, ALU.subtract).then_inc(
                    *done("gla_out_low", "out" if c == 3 else f"out{c}"))

        def conv_glu(l):
            dve.wait_ge(*after("conv_in", "g", l))
            V.tensor_tensor(conv_u, conv_u, conv_s, ALU.mult).then_inc(*done("conv_glu", "glu"))

        def conv_in(l):
            dve.wait_ge(*after("conv_turned", "u", l))
            V.tensor_copy(uT[:, :, CPAD:CPAD + T], two(6)).then_inc(*done("conv_glu", "u"))
            dve.wait_ge(*after("conv_glu", "u", l))

        def conv_taps(l, first, last):
            w = packed(PACK_A, "conv_w").rearrange("p (c w) -> p c w", c=4)
            for i in range(first, min(last, CW - 1) + 1):
                for c in range(4):
                    src = uT[:, c, i:i + T]
                    if i == 0:
                        V.tensor_scalar(conv_y[:, c, :], src, w[:, c, 0:1], packed(PACK_A, "conv_b")[:, c:c + 1], ALU.mult,
                                        ALU.add).then_inc(*done("conv_taps", f"tap0_{c}"))
                    else:
                        dve.wait_ge(*after("conv_taps", f"tap{i - 1}_{c}", l))
                        V.scalar_tensor_tensor(conv_y[:, c, :], src, w[:, c, i:i + 1], conv_y[:, c, :], ALU.mult,
                                               ALU.add).then_inc(*done("conv_taps", f"tap{i}_{c}"))

        def conv_centre(l):
            dve.wait_ge(*after("conv_rows", "rows", l))
            V.tensor_reduce(cmu, ps[:, 6:8, :], AX.X, ALU.add).then_inc(*done("conv_norm", "sums"))
            dve.wait_ge(*after("conv_norm", "sums", l))
            V.tensor_scalar(cmu, cmu, 1.0 / BW, None, ALU.mult).then_inc(*done("conv_norm", "means"))
            dve.wait_ge(*after("conv_norm", "means", l))
            for t in range(TT):
                V.tensor_scalar(conv_n[:, t, :], ps[:, 6 + t, :], cmu[:, t:t + 1], None,
                                ALU.subtract).then_inc(*done("conv_norm", f"centred{t}"))

        def conv_normed(l):
            for t in range(TT):
                dve.wait_ge(*after("conv_std", f"std{t}", l))
                V.reciprocal(crstd[:, t:t + 1], cstd[:, t:t + 1]).then_inc(*done("conv_norm", f"rstd{t}"))
                dve.wait_ge(*after("conv_norm", f"rstd{t}", l))
                V.tensor_scalar(conv_n[:, t, :], conv_n[:, t, :], crstd[:, t:t + 1], None,
                                ALU.mult).then_inc(*done("conv_norm", f"normed{t}"))

        def conv_low(l):
            dve.wait_ge(*after("conv_out", "high", l))
            V.tensor_tensor(bT_lo[:, 0:4, :], conv_y, flat(bT_hi[:, 0:4, :]), ALU.subtract).then_inc(*done("conv_out_low", "out"))

        def diagonal(w):
            return w.rearrange("p (e b n) -> p e b n", e=2, b=3)[:, :, 0::2, :]

        def mask(name):
            return konst(name).unsqueeze(1).unsqueeze(1).broadcast_to([P, 2, 2, P])

        def sb_keep(l, c):
            dve.wait_ge(*after("sb_weights", f"ln{c}", l))
            pair_of_heads = lambda w: w.rearrange("p (e n) -> p e n", e=2)
            V.scalar_tensor_tensor(pair_of_heads(sb_sp), ps[:, 4:6, 0:384], 0.0, pair_of_heads(sb_e), ALU.max,
                                   ALU.add).then_inc(*done("sb_keep", f"softplus{c}"))
            dve.wait_ge(*after("sb_keep", f"softplus{c}", l))
            V.tensor_tensor(diagonal(sb_sp), diagonal(sb_sp), mask("sb_keep"), ALU.mult).then_inc(*done("sb_keep", f"masked{c}"))
            V.tensor_copy(pair_of_heads(sb_z), ps[:, 4:6, 0:384]).then_inc(*done("sb_keep", f"copied{c}"))
            dve.wait_ge(*after("sb_keep", f"copied{c}", l))
            V.tensor_tensor(diagonal(sb_z), diagonal(sb_z), mask("sb_neg"), ALU.add).then_inc(*done("sb_keep", f"barred{c}"))

        def sb_exponent(l, c):
            dve.wait_ge(*after("sb_sums", f"sums{c}", l))
            dve.wait_ge(*after("sb_keep", f"barred{c}", l))
            z = sb_z.rearrange("p (e n) -> p e n", e=2)
            V.tensor_tensor(z, z, ps[:, 6:8, 0:384], ALU.subtract).then_inc(*done("sb_keep", f"exponent{c}"))

        def sb_low(l, c):
            dve.wait_ge(*after("sb_out_high", f"out{c}", l))
            tiles = lambda w: w[:, 4 + c, :].rearrange("p (t n) -> p t n", t=TT)
            V.tensor_tensor(tiles(bT_lo), ps[:, 6:8, 384:512], flat(tiles(bT_hi)),
                            ALU.subtract).then_inc(*done("sb_out_low", f"out{c}"))

        def merge(L, k, i, half):
            l = L.l
            multiplied(L, k)
            dve.wait_ge(*after("gates", f"gate{i}_{half}", l))
            out_, rows = merged[:, :, half * 512:half * 512 + 512], sg[:, half, :, :]
            if i == 0:
                V.tensor_tensor(out_, rows, ps[:, 2 * half:2 * half + 2, :], ALU.mult).then_inc(*done("merge", f"branch{i}_{half}"))
                return
            V.tensor_tensor(rows, rows, ps[:, 2 * half:2 * half + 2, :], ALU.mult).then_inc(*done("merge", f"gated{i}_{half}"))
            dve.wait_ge(*after("merge", f"gated{i}_{half}", l))
            V.tensor_tensor(out_, out_, rows, ALU.add).then_inc(*done("merge", f"branch{i}_{half}"))

        def merged_low(l, kh):
            for t in range(TT):
                dve.wait_ge(*after("merged_high", f"k{kh}t{t}", l))
                tiles = (slice(None), slice(4 * kh, 4 * kh + 4), slice(t * P, (t + 1) * P))
                V.tensor_tensor(hT_lo[tiles], ps[:, 4 + 2 * kh + t, :].rearrange("p (c n) -> p c n", c=4),
                                flat(hT_hi[tiles]), ALU.subtract).then_inc(*done("merged_low", f"k{kh}t{t}"))

        def mixer_a(L):
            l, k = L.l, U_FFN
            norm_in(L, 1)
            gla_rank_rows(L, k + 1)
            gla_logits(l)
            gla_keep(l)
            gla_keys(l)
            gla_states(l)
            conv_glu(l)
            gla_rows(l)
            gla_gated(l)
            conv_in(l)
            taps = [0]

            def some_taps():
                conv_taps(l, taps[0], taps[0] + 1)
                taps[0] += 2

            for _ in range(2):
                some_taps()
            gla_low(l)
            for _ in range(3):
                some_taps()
            k += 17
            for n in range(18):
                i, m = n // 6, n % 6
                if n == 15:
                    conv_low(l)
                if n == 17:
                    merged_low(l, 0)
                if m >= 4:
                    merge(L, k + n, i, m - 4)
                if n % 2 == 0 and 2 <= n <= 8:
                    sb_low(l, n // 2 - 1)
                if n % 2 == 0 and n < 8:
                    sb_keep(l, n // 2)
                if n % 2 == 1 and n < 8:
                    sb_exponent(l, n // 2)
                if n < 11:
                    some_taps()
                if n == 12:
                    conv_centre(l)
                    conv_normed(l)
                if n == 13:
                    prepare(L, 1)
            assert taps[0] >= CW
            merged_low(l, 1)
            norm_out(L, 1, False)

        def memory_rows(l):
            for t in range(TT):
                dve.wait_ge(*after("memory_std", f"std{t}", l))
                V.reciprocal(rstd_mem[:, t:t + 1], std_mem[:, t:t + 1]).then_inc(*done("memory_rows", f"rstd{t}"))
                dve.wait_ge(*after("memory_rows", f"rstd{t}", l))
                V.scalar_tensor_tensor(mem_rows[:, t, :], mem_rows[:, t, :], rstd_mem[:, t:t + 1], mem_g, ALU.mult,
                                       ALU.mult).then_inc(*done("memory_rows", f"normed{t}"))

        def memory_low(l):
            for t in range(TT):
                for kh in range(2):
                    dve.wait_ge(*after("memory_high", f"t{t}k{kh}", l))
                    tiles = (slice(None), slice(4 * kh, 4 * kh + 4), slice(t * P, (t + 1) * P))
                    V.tensor_tensor(bT_lo[tiles], ps[:, 2 * t + kh, :].rearrange("p (c n) -> p c n", c=4),
                                    flat(bT_hi[tiles]), ALU.subtract).then_inc(*done("memory_low", f"t{t}k{kh}"))

        def rope_angles():
            ANGLE, WHOLE, POS = sb_sp[:, 0:64], sb_sp[:, 64:128], sb_sp[:, 128:128 + TT]
            dve.wait_ge(const_loaded, 16 * 2)
            V.tensor_copy(POS, positions).then_inc(*done("rope_angles", "positions"))
            dve.wait_ge(*after("rope_angles", "positions", 0))
            for t in range(TT):
                V.tensor_scalar(ANGLE[:, 32 * t:32 * t + 32], konst("inv_freq"), POS[:, t:t + 1], None,
                                ALU.mult).then_inc(*done("rope_angles", f"angles{t}"))
            dve.wait_ge(*after("rope_angles", f"angles{TT - 1}", 0))
            for name, table, quarter in (("sin", sin, 0.0), ("cos", cos, 0.25)):
                ROUND = 1.5 * 2 ** 23
                steps = [
                    lambda: V.tensor_scalar(WHOLE, ANGLE, 1.0 / (2 * np.pi), quarter, ALU.mult, ALU.add),
                    lambda: V.tensor_scalar(WHOLE, WHOLE, ROUND, None, ALU.add),
                    lambda: V.tensor_scalar(WHOLE, WHOLE, ROUND, None, ALU.subtract),
                    lambda: V.scalar_tensor_tensor(table, WHOLE, -TURN[0], ANGLE, ALU.mult, ALU.add),
                    lambda: V.scalar_tensor_tensor(table, WHOLE, -TURN[1], table, ALU.mult, ALU.add),
                    lambda: V.scalar_tensor_tensor(table, WHOLE, -TURN[2], table, ALU.mult, ALU.add),
                    lambda: V.tensor_scalar(table, table, quarter * 2 * np.pi, PI_BELOW, ALU.add, ALU.min),
                    lambda: V.tensor_scalar(table, table, -PI_BELOW, None, ALU.max)]
                for n, step in enumerate(steps):
                    label = name if n == len(steps) - 1 else f"{name}{n}"
                    step().then_inc(*done("rope_angles", label))
                    dve.wait_ge(*after("rope_angles", label, 0))

        def fox_gate(L):
            l = L.l
            multiplied(L, 1)
            V.tensor_copy(fcT[0:8, :], ps[0:8, 6, 0:T]).then_inc(*done("fox_gate", "copied"))
            dve.wait_ge(*after("fox_forget", "turned", l))
            dve.wait_ge(pack_loaded, l * 16 + (16 * DEPTH + 16))
            for t in range(TT):
                V.scalar_tensor_tensor(flog[:, t, :], ps[:, 6, T + t * 8:T + t * 8 + 8], rstd_in[:, t:t + 1], packed(PACK_B, "fox_b"),
                                       ALU.mult, ALU.add).then_inc(*done("fox_gate", "logits" if t else "logits0"))
            dve.wait_ge(*after("fox_soft", "ln", l))
            z = flog.rearrange("p t h -> p (t h)")
            V.scalar_tensor_tensor(z, z, 0.0, ftmp, ALU.min, ALU.subtract).then_inc(*done("fox_gate", "log"))

        def fox_sums(l):
            dve.wait_ge(*after("fox_decay", "sums", l))
            V.tensor_copy(fcum.rearrange("p t h -> p (t h)"), ps[:, 7, 0:16]).then_inc(*done("fox_gate", "sums"))
            V.tensor_copy(fcT[0:8, :], ps[0:8, 7, 128:384]).then_inc(*done("fox_gate", "rows0"))
            V.tensor_copy(fcT[64:72, :], ps[64:72, 7, 128:384]).then_inc(*done("fox_gate", "rows"))

        def lru_lambda(l):
            e, s, s2, acc = lru_t, lru_c, stat[:, 100:102], stat[:, 102:104]

            def then(ins, step):
                ins.then_inc(*done("lru_lambda", step))
                dve.wait_ge(*after("lru_lambda", step, l))

            then(V.tensor_scalar(lsp, packed(PACK_B, "lam"), -1.0, 0.0, ALU.mult, ALU.max), "max")
            dve.wait_ge(*after("lru_act", "lambda", l))
            then(V.tensor_scalar(s, e, 2.0, None, ALU.add), "two")
            then(V.reciprocal(s, s), "over")
            then(V.tensor_tensor(s, s, e, ALU.mult), "s")
            then(V.tensor_tensor(s2, s, s, ALU.mult), "s2")
            then(V.tensor_scalar(acc, s2, 1.0 / 17, 1.0 / 15, ALU.mult, ALU.add), "term15")
            for n in range(13, 0, -2):
                then(V.tensor_tensor(acc, acc, s2, ALU.mult), f"times{n}")
                then(V.tensor_scalar(acc, acc, 1.0 / n, None, ALU.add), f"term{n}")
            then(V.tensor_tensor(acc, acc, s, ALU.mult), "half")
            then(V.scalar_tensor_tensor(lsp, acc, 2.0, lsp, ALU.mult, ALU.add), "softplus")
            then(V.tensor_scalar(lsp, lsp, -LRU_C, None, ALU.mult), "scaled")

        def lru_conv(l):
            dve.wait_ge(*after("lru_turned", "xy", l))
            V.tensor_copy(lxT[:, :, PAD2:PAD2 + T], two(4)[:, 0:2, :]).then_inc(*done("lru_turn", "x"))
            V.tensor_copy(lyT.rearrange("p (c t) -> p c t", c=2), two(4)[:, 2:4, :]).then_inc(*done("lru_turn", "y"))
            dve.wait_ge(*after("lru_turn", "x", l))
            w = packed(PACK_B, "conv_w").rearrange("p (c w) -> p c w", c=2)
            for i in range(CW2):
                for c in range(2):
                    src, dst = lxT[:, c, i:i + T], lru[0][:, c * T:(c + 1) * T]
                    if i == 0:
                        V.tensor_scalar(dst, src, w[:, c, 0:1], packed(PACK_B, "conv_b")[:, c:c + 1], ALU.mult,
                                        ALU.add).then_inc(*done("lru_conv", f"tap0_{c}"))
                    else:
                        dve.wait_ge(*after("lru_conv", f"tap{i - 1}_{c}", l))
                        V.scalar_tensor_tensor(dst, src, w[:, c, i:i + 1], dst, ALU.mult,
                                               ALU.add).then_inc(*done("lru_conv", f"tap{i}_{c}"))

        def lru_log(l):
            dve.wait_ge(*after("lru_act", "i1", l))
            for c in range(2):
                r = lru[1][:, c * T:(c + 1) * T]
                V.tensor_scalar(r, r, lsp[:, c:c + 1], None, ALU.mult).then_inc(*done("lru_math", f"log{c}"))
            V.tensor_tensor(lru[2], lru[2], lru[0], ALU.mult).then_inc(*done("lru_math", "ix"))

        def lru_square(l):
            dve.wait_ge(*after("lru_act", "tanh", l))
            dve.wait_ge(*after("lru_math", "ix", l))
            V.tensor_scalar(lru[0], lru[3], -1.0, 1.0, ALU.mult, ALU.add).then_inc(*done("lru_math", "less"))
            dve.wait_ge(*after("lru_math", "less", l))
            V.reciprocal(lru[0], lru[0]).then_inc(*done("lru_math", "over"))
            dve.wait_ge(*after("lru_math", "over", l))
            V.scalar_tensor_tensor(lru[3], lru[3], -2.0, lru[0], ALU.mult, ALU.mult).then_inc(*done("lru_math", "square"))

        def lru_scan(l):
            dve.wait_ge(*after("lru_act", "root", l))
            V.tensor_tensor(lru[2], lru[2], lru[3], ALU.mult).then_inc(*done("lru_math", "u"))
            dve.wait_ge(*after("lru_math", "u", l))
            for c in range(2):
                s = slice(c * T, (c + 1) * T)
                V.tensor_tensor_scan(lru[3][:, s], lru[1][:, s], lru[2][:, s], 0.0, ALU.mult,
                                     ALU.add).then_inc(*done("lru_math", f"scan{c}"))
            dve.wait_ge(*after("lru_math", "scan1", l))
            dve.wait_ge(*after("lru_act", "gelu", l))
            V.tensor_tensor(lru[0], lru[3], lyT, ALU.mult).then_inc(*done("lru_math", "out"))

        def lru_low(l):
            dve.wait_ge(*after("lru_act", "high", l))
            V.tensor_tensor(hT_lo[:, 0:2, :], lru[0].rearrange("p (c t) -> p c t", c=2), flat(hT_hi[:, 0:2, :]),
                            ALU.subtract).then_inc(*done("lru_low", "out"))

        def fox_rows(l, g):
            t, n = g // 2, P * (g // 2 + 1)
            dve.wait_ge(*after("fox_logits", f"logits{g}", l))
            if g:
                dve.wait_ge(*after("fox_p_turned", f"turned{g - 1}", l))
            for i in range(2):
                for e in range(2):
                    b, h = 2 * i + e, 2 * (2 * (g % 2) + i) + e
                    src, decay = ps[:, 6 + e, i * T:i * T + n], fcum[:, t, h:h + 1]
                    label = f"rows{g}" if b == 3 else f"rows{g}_{b}"
                    if t:
                        V.tensor_scalar(fl[:, b, 0:P], src[:, 0:P], decay, None, ALU.add).then_inc(
                            *done("fox_rows", f"early{g}_{b}"))
                    V.scalar_tensor_tensor(fl[:, b, t * P:n], src[:, t * P:n], decay, konst("fox_neg"), ALU.add,
                                           ALU.add).then_inc(*done("fox_rows", label))
            dve.wait_ge(*after("fox_rows", f"rows{g}", l))
            V.tensor_reduce(fmax, fl[:, :, 0:n], AX.X, ALU.max).then_inc(*done("fox_rows", f"top{g}"))
            dve.wait_ge(*after("fox_rows", f"top{g}", l))
            V.tensor_scalar(fmax, fmax, -1.0, None, ALU.mult).then_inc(*done("fox_rows", f"max{g}"))

        def fox_weights(l, g):
            n = P * (g // 2 + 1)
            dve.wait_ge(*after("fox_exp", f"g{g}h3", l))
            V.reciprocal(frd, fden).then_inc(*done("fox_rows", f"over{g}"))
            dve.wait_ge(*after("fox_rows", f"over{g}", l))
            for b in range(4):
                V.tensor_scalar(fl[:, b, 0:n], fl[:, b, 0:n], frd[:, b:b + 1], None, ALU.mult).then_inc(
                    *done("fox_rows", f"weights{g}" if b == 3 else f"weights{g}_{b}"))

        def fox_low(l, g):
            dve.wait_ge(*after("fox_out_high", f"out{g}", l))
            c, t = 2 + 2 * (g % 2), g // 2
            tiles = (slice(None), slice(c, c + 2), slice(t * P, (t + 1) * P))
            V.tensor_tensor(hT_lo[tiles], ps[:, 4, 0:256].rearrange("p (c t) -> p c t", c=2), flat(hT_hi[tiles]),
                            ALU.subtract).then_inc(*done("fox_out_low", f"out{g}"))

        def ret_rope(l):
            dve.wait_ge(*after("ret_in", "qk", l))
            src = rqk.rearrange("p t (h u f) -> p t h u f", h=8, u=2)
            dst = rope.rearrange("p t (h u f) -> p t h u f", h=8, u=2)
            tmp = rsq_f.rearrange("p (t h f) -> p t h f", t=TT, h=8)
            for t in range(TT):
                wave = {"c": cos[:, 32 * t:32 * t + 32].unsqueeze(1).broadcast_to([P, 8, 32]),
                        "s": sin[:, 32 * t:32 * t + 32].unsqueeze(1).broadcast_to([P, 8, 32])}
                for u, (same, other, op) in enumerate((("c", "s", ALU.subtract), ("c", "s", ALU.add))):
                    V.tensor_tensor(dst[:, t, :, u, :], src[:, t, :, u, :], wave[same], ALU.mult).then_inc(
                        *done("ret_rope", f"same{t}{u}"))
                    if u:
                        dve.wait_ge(*after("ret_rope", f"sum{t}0", l))
                    V.tensor_tensor(tmp[:, t, :, :], src[:, t, :, 1 - u, :], wave[other], ALU.mult).then_inc(
                        *done("ret_rope", f"other{t}{u}"))
                    dve.wait_ge(*after("ret_rope", f"other{t}{u}", l))
                    V.tensor_tensor(dst[:, t, :, u, :], dst[:, t, :, u, :], tmp[:, t, :, :], op).then_inc(
                        *done("ret_rope", "rotated" if t and u else f"sum{t}{u}"))

        def ret_turned(l):
            dve.wait_ge(*after("ret_turned", "qk", l))
            V.tensor_copy(rT, two(6)).then_inc(*done("ret_rope", "qkT"))

        def ret_scores(l, c):
            dve.wait_ge(*after("ret_dots", f"dots{c}", l))
            decay = konst("ret_decay").rearrange("p (h n) -> p h n", h=4)[:, 2 * c:2 * c + 2, :]
            s = ret_s[:, 2 * c:2 * c + 2, :]
            V.tensor_tensor(s[:, :, 0:256], ps[:, 6:8, 0:256], decay, ALU.mult).then_inc(*done("ret_scores", f"first{c}"))
            V.tensor_tensor(s[:, :, 256:384], ps[:, 6:8, 256:384], decay[:, :, 0:P], ALU.mult).then_inc(
                *done("ret_scores", f"scores{c}"))

        def ret_norm(l):
            dve.wait_ge(*after("ret_rows", "rows", l))
            y = ry_f.rearrange("p (h v) -> p h v", h=8)
            V.tensor_reduce(rstat3, ps[:, 6, :].rearrange("p (h v) -> p h v", h=8), AX.X, ALU.add).then_inc(
                *done("ret_norm", "totals"))
            dve.wait_ge(*after("ret_norm", "totals", l))
            V.tensor_scalar(rstat3, rstat3, 1.0 / 64, None, ALU.mult).then_inc(*done("ret_norm", "means"))
            dve.wait_ge(*after("ret_norm", "means", l))
            V.tensor_tensor(y, ps[:, 6, :].rearrange("p (h v) -> p h v", h=8),
                            rstat3.unsqueeze(2).broadcast_to([P, 8, 64]), ALU.subtract).then_inc(*done("ret_norm", "centred"))
            dve.wait_ge(*after("ret_norm", "centred", l))
            V.tensor_tensor(rsq_f, ry_f, ry_f, ALU.mult).then_inc(*done("ret_norm", "squares"))
            dve.wait_ge(*after("ret_norm", "squares", l))
            V.tensor_reduce(rstat, rsq_f.rearrange("p (h v) -> p h v", h=8), AX.X, ALU.add).then_inc(*done("ret_norm", "sums"))

        def ret_gated(l):
            dve.wait_ge(*after("ret_std", "std", l))
            V.reciprocal(rstat3, rstat2).then_inc(*done("ret_norm", "over"))
            dve.wait_ge(*after("ret_in", "g", l))
            V.tensor_tensor(ry_f, ry_f, rg_f, ALU.mult).then_inc(*done("ret_norm", "with_g"))
            dve.wait_ge(*after("ret_norm", "with_g", l))
            y = ry_f.rearrange("p (h v) -> p h v", h=8)
            V.tensor_tensor(y, y, rstat3.unsqueeze(2).broadcast_to([P, 8, 64]), ALU.mult).then_inc(*done("ret_norm", "gated"))

        def ret_low(l):
            dve.wait_ge(*after("ret_out_high", "out", l))
            V.tensor_tensor(hT_lo[:, 6:8, :], ps[:, 6, :].rearrange("p (c t) -> p c t", c=2), flat(hT_hi[:, 6:8, :]),
                            ALU.subtract).then_inc(*done("ret_out_low", "out"))

        def mixer_b(L):
            l = L.l
            V.memset(lxT[:, :, 0:PAD2], 0.0).then_inc(*done("lru_turn", "pad"))
            norm_in(L, 0)
            fox_gate(L)
            fox_sums(l)
            lru_lambda(l)
            lru_conv(l)
            fox_rows(l, 0)
            fox_weights(l, 0)
            ret_rope(l)
            fox_rows(l, 1)
            lru_log(l)
            ret_turned(l)
            fox_weights(l, 1)
            lru_square(l)
            fox_low(l, 0)
            ret_scores(l, 0)
            ret_scores(l, 1)
            lru_scan(l)
            fox_low(l, 1)
            fox_rows(l, 2)
            fox_weights(l, 2)
            lru_low(l)
            fox_rows(l, 3)
            fox_weights(l, 3)
            fox_low(l, 2)
            ret_norm(l)
            ret_gated(l)
            ret_low(l)
            fox_low(l, 3)
            prepare(L, 0)
            dve.wait_ge(*after("memory_keys", "k1", l))
            norm_out(L, 0, False)

        def cross(L):
            l = L.l
            norm_in(L, 1)

            def top(g):
                dve.wait_ge(*after("cross_logits", f"logits{g}", l))
                m = cmax[:, 2 * g:2 * g + 2]
                V.tensor_reduce(m, ps[:, 2 * (g % 2) + g // 2, :].rearrange("p (h n) -> p h n", h=2), AX.X,
                                ALU.max).then_inc(*done("cross_max", f"top{g}"))
                dve.wait_ge(*after("cross_max", f"top{g}", l))
                V.tensor_scalar(m, m, -1.0, None, ALU.mult).then_inc(*done("cross_max", f"max{g}"))

            def weights(g):
                dve.wait_ge(*after("cross_exp", f"g{g}h1", l))
                V.reciprocal(crd[:, 2 * g:2 * g + 2], cden[:, 2 * g:2 * g + 2]).then_inc(*done("cross_rows", f"over{g}"))
                dve.wait_ge(*after("cross_rows", f"over{g}", l))
                for i in range(2):
                    w = cp[g % 2][:, 2 * (g // 2) + i, :]
                    V.tensor_scalar(w, w, crd[:, 2 * g + i:2 * g + i + 1], None,
                                    ALU.mult).then_inc(*done("cross_rows", f"weights{g}" if i else f"weights{g}_0"))

            def out_low(g):
                t, half = g % 2, g // 2
                dve.wait_ge(*after("cross_out_high", f"out{g}", l))
                tiles = (slice(None), slice(4 * half, 4 * half + 4), slice(t * P, (t + 1) * P))
                V.tensor_tensor(hT_lo[tiles], ps[:, cross_bank(g), :].rearrange("p (c n) -> p c n", c=4),
                                flat(hT_hi[tiles]), ALU.subtract).then_inc(*done("cross_out_low", f"out{g}"))

            top(0)
            top(1)
            weights(0)
            top(2)
            weights(1)
            top(3)
            weights(2)
            weights(3)
            for g in range(4):
                out_low(g)
            prepare(L, 1)
            norm_out(L, 1, False)

        V.memset(uT[:, :, 0:CPAD], 0.0).then_inc(*done("start", "pad"))
        dve.wait_ge(*after("start", "pad", 0))
        dve.wait_ge(pre_loaded, 16)
        for t in range(TT):
            dve.wait_ge(x_loaded[t], 16)
            for kh in range(2):
                cols = slice(512 * kh, 512 * kh + 512)
                V.tensor_tensor(xn[:, t, cols], x[:, t, cols], pre_g[:, cols], ALU.mult).then_inc(h_ready, 1)
            if t:
                rope_angles()
            for kh in range(2):
                low(Layer("A", 0), 0, t, kh)
        V.sem_inc(x_ready, TT)
        dve.wait_ge(const_loaded, 16 * 4)
        with dve.Fori(0, DEPTH) as l:
            L = Layer("A", l)
            ffn(L, 0, 0, 0)
            mixer_a(L)
            ffn(L, 1, 2, U_FFN + U_MIX_A)
        with dve.Fori(0, DEPTH) as l:
            L = Layer("B", l)
            mixer_b(L)
            cross(L)
            ffn(L, 0, 2, U_MIX_B)
        dve.wait_ge(hT_ready, 4 * (6 * DEPTH + 1))

    return S.seen


TURN = (6.28125, 0.0019350051879882812, 2 * np.pi - 6.28125 - 0.0019350051879882812)
PI_BELOW = 3.1415925


_WHOLE = ["x", "ffn1_w_gate", "ffn1_w_up", "ffn1_w_down", "ffn2_w_gate", "ffn2_w_up", "ffn2_w_down", "w_in", "w_branch",
          "w_out", "w_in_2", "w_cq_2", "w_ck_2", "w_cv_2", "w_co_2", "w_out_2", "w_gate_2", "w_up_2", "w_down_2"]


def _layout(inputs):
    get = lambda name: np.ascontiguousarray(np.asarray(inputs[name]))
    arrays = {name: get(name) for name in _WHOLE}
    arrays["w_branch"] = arrays["w_branch"].reshape(DEPTH, 3 * BW, D)
    gains = np.zeros((6 * DEPTH + 1, 2, D), np.float32)
    for l in range(DEPTH):
        for j in range(3):
            gains[3 * l + j, 0], gains[3 * l + j, 1] = get("norm_pre")[l, j], get("norm_post")[l, j]
        for j, name in enumerate(("mix", "cross", "ffn")):
            gains[3 * DEPTH + 3 * l + j, 0] = get(f"pre_{name}_g_2")[l]
            gains[3 * DEPTH + 3 * l + j, 1] = get(f"post_{name}_g_2")[l]
    arrays["gains"] = gains
    arrays["mem"], arrays["mem_g"] = get("mem_2"), get("mem_norm_g_2")[None, :]
    arrays["positions"] = np.ascontiguousarray(get("positions_2").reshape(TT, P).T)
    arrays["const"] = CONST_ARRAY

    def tiles(v):
        v = v.reshape(v.shape[:-1] + (-1, P))
        return np.moveaxis(np.moveaxis(v, -1, 0), -1, 1)

    a = np.zeros((DEPTH, P, PACK_A_W), np.float32)
    b = np.zeros((DEPTH, P, PACK_B_W), np.float32)

    def put(array, table, l, name, value):
        at, w = table[name]
        array[l, :value.shape[0], at:at + w] = value.reshape(value.shape[0], w)

    for l in range(DEPTH):
        put(a, PACK_A, l, "conv_w", tiles(get("conv_w")[l]))
        for name, source in (("conv_b", "conv_b"), ("ln_g", "conv_ln_g"), ("ln_b", "conv_ln_b"), ("gla_g", "gla_norm_g")):
            put(a, PACK_A, l, name, tiles(get(source)[l]))
        put(a, PACK_A, l, "w_alpha", get("gla_w_alpha")[l])
        put(a, PACK_A, l, "b_alpha", np.repeat(get("gla_b_alpha")[l][None, :], P, axis=0))
        put(b, PACK_B, l, "conv_w", tiles(get("conv_w_2")[l]))
        for name, source in (("conv_b", "conv_b_2"), ("b_r", "b_rg_2"), ("b_i", "b_ig_2"), ("lam", "lru_lambda_2")):
            put(b, PACK_B, l, name, tiles(get(source)[l]))
        put(b, PACK_B, l, "fox_b", np.repeat(get("fox_b_f_2")[l][None, :], P, axis=0))
        for name, source in (("w_r", "w_rg_2"), ("w_i", "w_ig_2")):
            at, _ = PACK_B[name]
            for n in range(4):
                c, e = n // 2, n % 2
                b[l, 64 * e:64 * e + 64, at + c * P + 64 * e:at + c * P + 64 * e + 64] = get(source)[l, n]
    arrays["pack_a"], arrays["pack_b"] = a, b
    return arrays


def kernel(**inputs):
    import concourse.bacc as _bacc
    from concourse.bass_utils import run_bass_kernel_spmd

    arrays = _layout(inputs)
    counted = None
    for _ in range(2):
        nc = _bacc.Bacc("TRN2", target_bir_lowering=False, num_devices=1)
        d = {name: nc.dram_tensor(f"in_{name}", v.shape, I32 if name == "positions" else F32, kind="ExternalInput").ap()
             for name, v in arrays.items()}
        out = nc.dram_tensor("out", (1, T, D), F32, kind="ExternalOutput").ap()
        counted = build(nc, d, out, counted)
    result = run_bass_kernel_spmd(nc, [{f"in_{name}": v for name, v in arrays.items()}], core_ids=[0])
    return np.asarray(result.results[0]["out"])
```
